# Optimizing a Trainium2 kernel written in Bass

```python
import jax, jax.numpy as jnp
from jax import lax
import numpy as np
import math

D_MODEL = 1024
BATCH = 1
SEQ = 512
DEPTH = 2

HG_HEADS = 4
HG_DIM = 128
HG_WIDTH = HG_HEADS * HG_DIM
HG_CHUNK = 64
NSA_HEADS = 8
NSA_KV_HEADS = 2
NSA_GROUP = NSA_HEADS // NSA_KV_HEADS
NSA_DIM = 64
NSA_WIDTH = NSA_HEADS * NSA_DIM
NSA_KV_WIDTH = NSA_KV_HEADS * NSA_DIM
CMP_LEN = 32
CMP_STRIDE = 16
CMP_HIDDEN = 256
SLC_LEN = 64
SLC_TOP = 16
SLC_QBLOCK = 32
WINDOW = 512
SWA_QBLOCK = 128
N_BRANCH = 3
MIX_WIDTH = HG_WIDTH + NSA_WIDTH
D_FF = ((8 * D_MODEL + 3 * 256 - 1) // (3 * 256)) * 256
ROPE_THETA = 10000.0
RMS_EPS = 1e-6
NEG = -1e30
FORCED_SCORE = 1e9
IN_SPLITS = (HG_WIDTH, HG_WIDTH, HG_WIDTH, HG_WIDTH, NSA_WIDTH,
             NSA_KV_WIDTH, NSA_KV_WIDTH, NSA_KV_WIDTH, NSA_KV_WIDTH, NSA_KV_WIDTH, NSA_KV_WIDTH,
             NSA_HEADS * N_BRANCH)
IN_WIDTH = sum(IN_SPLITS)
IN_SPLIT_POINTS = tuple(int(v) for v in np.cumsum(IN_SPLITS)[:-1])


def rms_norm(x, gain):
    xf = x.astype(jnp.float32)
    y = xf * lax.rsqrt(jnp.mean(xf * xf, axis=-1, keepdims=True) + RMS_EPS)
    return (y * gain.astype(jnp.float32)).astype(x.dtype)

def rope(x, pos):
    half = x.shape[-1] // 2
    freqs = ROPE_THETA ** (-jnp.arange(half, dtype=jnp.float32) / half)
    ang = pos.astype(jnp.float32)[:, None] * freqs[None, :]
    cos = jnp.cos(ang)[:, None, :]
    sin = jnp.sin(ang)[:, None, :]
    xf = x.astype(jnp.float32)
    x1, x2 = xf[..., :half], xf[..., half:]
    return jnp.concatenate([x1 * cos - x2 * sin, x1 * sin + x2 * cos], axis=-1).astype(x.dtype)

def hgrn2_mixer(q, f_logit, i, g, lower_bound, g_norm):
    B, T, _ = q.shape
    dt = q.dtype
    n_chunk = T // HG_CHUNK
    lb = lower_bound.astype(jnp.float32)
    f = lb + (1.0 - lb) * jax.nn.sigmoid(f_logit.astype(jnp.float32))
    log_f = jnp.log(f)
    k = 1.0 - f
    qf = jax.nn.silu(q.astype(jnp.float32))
    v = i.astype(jnp.float32)

    def to_chunks(a):
        return a.reshape(B, n_chunk, HG_CHUNK, HG_HEADS, HG_DIM).transpose(1, 0, 3, 2, 4)

    causal = jnp.tril(jnp.ones((HG_CHUNK, HG_CHUNK), dtype=bool))[:, :, None]

    def step(S, xs):
        qc, kc, vc, lfc = xs
        b = jnp.cumsum(lfc, axis=2)
        diff = b[:, :, :, None, :] - b[:, :, None, :, :]
        decay = jnp.exp(jnp.where(causal, diff, -jnp.inf))
        A = jnp.einsum('bhtd,bhsd,bhtsd->bhts', qc, kc, decay)
        o = (jnp.einsum('bhts,bhsv->bhtv', A, vc)
             + jnp.einsum('bhtd,bhdv->bhtv', qc * jnp.exp(b), S))
        b_last = b[:, :, -1:, :]
        S = (jnp.exp(b_last[:, :, 0, :])[..., None] * S
             + jnp.einsum('bhsd,bhsv->bhdv', kc * jnp.exp(b_last - b), vc))
        return S, o

    S0 = jnp.zeros((B, HG_HEADS, HG_DIM, HG_DIM), jnp.float32)
    _, o = lax.scan(step, S0, (to_chunks(qf), to_chunks(k), to_chunks(v), to_chunks(log_f)))
    o = o.transpose(1, 0, 3, 2, 4).reshape(B, T, HG_HEADS, HG_DIM)
    o = rms_norm(o, g_norm) * jax.nn.silu(g.astype(jnp.float32).reshape(B, T, HG_HEADS, HG_DIM))
    return o.reshape(B, T, HG_WIDTH).astype(dt)

def compress(a, pe, w1, w2):
    B, T, G, d = a.shape
    R = CMP_LEN // CMP_STRIDE
    n_cmp = (T - CMP_LEN) // CMP_STRIDE + 1
    seg = a.reshape(B, T // CMP_STRIDE, CMP_STRIDE, G, d)
    blocks = jnp.concatenate([seg[:, r:r + n_cmp] for r in range(R)], axis=2)
    blocks = blocks + pe[None, None, :, None, :]
    flat = blocks.transpose(0, 1, 3, 2, 4).reshape(B, n_cmp, G, CMP_LEN * d)
    return jax.nn.silu(flat @ w1) @ w2

def cmp_to_slc_matrix(T):
    n_cmp = (T - CMP_LEN) // CMP_STRIDE + 1
    n_slc = T // SLC_LEN
    c_start = np.arange(n_cmp) * CMP_STRIDE
    c_end = c_start + CMP_LEN - 1
    s_start = np.arange(n_slc) * SLC_LEN
    s_end = s_start + SLC_LEN - 1
    M = (c_start[:, None] <= s_end[None, :]) & (c_end[:, None] >= s_start[None, :])
    return jnp.asarray(M.astype(np.float32))

def nsa_mixer(q, k_cmp, v_cmp, k_slc, v_slc, k_swa, v_swa, gate_logit, q_gain, k_gain,
              pe_k, w1_k, w2_k, pe_v, w1_v, w2_v):
    B, T, _ = q.shape
    dt = q.dtype
    H, G, Hg, d = NSA_HEADS, NSA_KV_HEADS, NSA_GROUP, NSA_DIM
    pos = jnp.arange(T)
    scale = d ** -0.5
    qr = rope(rms_norm(q.reshape(B, T, H, d), q_gain), pos)
    qg = qr.reshape(B, T, G, Hg, d)

    def kv_heads(a):
        return a.reshape(B, T, G, d)

    kc = compress(kv_heads(k_cmp), pe_k, w1_k, w2_k)
    vc = compress(kv_heads(v_cmp), pe_v, w1_v, w2_v)
    n_cmp = kc.shape[1]
    cmp_end = jnp.arange(n_cmp) * CMP_STRIDE + CMP_LEN - 1
    kc = rope(rms_norm(kc, k_gain[0]), cmp_end)
    s = jnp.einsum('btghd,bngd->bghtn', qg, kc).astype(jnp.float32) * scale
    m_cmp = cmp_end[None, :] <= pos[:, None]
    p_cmp = jax.nn.softmax(jnp.where(m_cmp, s, NEG), axis=-1) * m_cmp
    o_cmp = jnp.einsum('bghtn,bngd->btghd', p_cmp.astype(dt), vc)

    n_slc = T // SLC_LEN
    imp = jnp.einsum('bghtn,nj->bgtj', p_cmp, cmp_to_slc_matrix(T))
    blk = jnp.arange(n_slc)
    cur = pos // SLC_LEN
    forced = (blk[None, :] == 0) | (blk[None, :] == cur[:, None]) | (blk[None, :] == cur[:, None] - 1)
    causal_blk = blk[None, :] <= cur[:, None]
    score = jnp.where(forced, FORCED_SCORE, jnp.where(causal_blk, imp, NEG))
    top = min(SLC_TOP, n_slc)
    _, idx = lax.top_k(score, top)

    ks = rope(rms_norm(kv_heads(k_slc), k_gain[1]), pos)
    kb = ks.reshape(B, n_slc, SLC_LEN, G, d).transpose(0, 3, 1, 2, 4)
    vb = kv_heads(v_slc).reshape(B, n_slc, SLC_LEN, G, d).transpose(0, 3, 1, 2, 4)
    nq = T // SLC_QBLOCK
    q_blocks = qg.reshape(B, nq, SLC_QBLOCK, G, Hg, d).transpose(1, 0, 3, 4, 2, 5)
    idx_blocks = idx.reshape(B, G, nq, SLC_QBLOCK, top).transpose(2, 0, 1, 3, 4)
    t_blocks = pos.reshape(nq, SLC_QBLOCK)
    bi = jnp.arange(B)[:, None, None, None]
    gi = jnp.arange(G)[None, :, None, None]
    tok = jnp.arange(SLC_LEN)

    def slc_block(xs):
        qb, ib, tb = xs
        kg = kb[bi, gi, ib]
        vg = vb[bi, gi, ib]
        sb = jnp.einsum('bghqd,bgqnsd->bghqns', qb, kg).astype(jnp.float32) * scale
        kpos = ib[..., None] * SLC_LEN + tok
        mb = (kpos <= tb[None, None, :, None, None])[:, :, None]
        sb = jnp.where(mb, sb, NEG)
        pb = jax.nn.softmax(sb.reshape(B, G, Hg, SLC_QBLOCK, -1), axis=-1).reshape(sb.shape)
        return jnp.einsum('bghqns,bgqnsd->bghqd', pb.astype(dt), vg)

    o_slc = lax.map(slc_block, (q_blocks, idx_blocks, t_blocks))
    o_slc = o_slc.transpose(1, 0, 4, 2, 3, 5).reshape(B, T, G, Hg, d)

    kw = rope(rms_norm(kv_heads(k_swa), k_gain[2]), pos)
    vw = kv_heads(v_swa)
    kpad = jnp.pad(kw, ((0, 0), (WINDOW, 0), (0, 0), (0, 0)))
    vpad = jnp.pad(vw, ((0, 0), (WINDOW, 0), (0, 0), (0, 0)))
    nw = T // SWA_QBLOCK
    span = WINDOW + SWA_QBLOCK
    qw_blocks = qg.reshape(B, nw, SWA_QBLOCK, G, Hg, d).transpose(1, 0, 3, 4, 2, 5)

    def swa_block(xs):
        qb, n = xs
        start = n * SWA_QBLOCK
        kblk = lax.dynamic_slice_in_dim(kpad, start, span, axis=1)
        vblk = lax.dynamic_slice_in_dim(vpad, start, span, axis=1)
        tq = start + jnp.arange(SWA_QBLOCK)
        tk = start - WINDOW + jnp.arange(span)
        mw = (tk[None, :] <= tq[:, None]) & (tk[None, :] > tq[:, None] - WINDOW) & (tk[None, :] >= 0)
        sw = jnp.einsum('bghqd,bkgd->bghqk', qb, kblk).astype(jnp.float32) * scale
        pw = jax.nn.softmax(jnp.where(mw, sw, NEG), axis=-1)
        return jnp.einsum('bghqk,bkgd->bghqd', pw.astype(dt), vblk)

    o_swa = lax.map(swa_block, (qw_blocks, jnp.arange(nw)))
    o_swa = o_swa.transpose(1, 0, 4, 2, 3, 5).reshape(B, T, G, Hg, d)

    gate = jax.nn.sigmoid(gate_logit.astype(jnp.float32)).reshape(B, T, G, Hg, N_BRANCH)
    o = (gate[..., 0:1] * o_cmp.astype(jnp.float32)
         + gate[..., 1:2] * o_slc.astype(jnp.float32)
         + gate[..., 2:3] * o_swa.astype(jnp.float32))
    return o.reshape(B, T, NSA_WIDTH).astype(dt)

def first_inputs(seed: int = 0) -> dict:
    key = jax.random.key(seed)
    ks = jax.random.split(key, 20)

    def dense(k, shape, fan_in):
        return jax.random.normal(k, shape, jnp.float32) * fan_in ** -0.5

    def gain(k, shape):
        return 1.0 + 0.05 * jax.random.normal(k, shape, jnp.float32)

    return {
        'x': jax.random.normal(ks[0], (BATCH, SEQ, D_MODEL), jnp.float32),
        'w_in': dense(ks[1], (DEPTH, D_MODEL, IN_WIDTH), D_MODEL),
        'w_out': dense(ks[2], (DEPTH, MIX_WIDTH, D_MODEL), MIX_WIDTH),
        'hg_lb_logits': 0.1 * jax.random.normal(ks[3], (DEPTH, HG_WIDTH), jnp.float32),
        'hg_gnorm': gain(ks[4], (DEPTH, HG_DIM)),
        'q_gain': gain(ks[5], (DEPTH, NSA_DIM)),
        'k_gain': gain(ks[6], (DEPTH, N_BRANCH, NSA_DIM)),
        'cmp_pe_k': 0.1 * jax.random.normal(ks[7], (DEPTH, CMP_LEN, NSA_DIM), jnp.float32),
        'cmp_w1_k': dense(ks[8], (DEPTH, CMP_LEN * NSA_DIM, CMP_HIDDEN), CMP_LEN * NSA_DIM),
        'cmp_w2_k': dense(ks[9], (DEPTH, CMP_HIDDEN, NSA_DIM), CMP_HIDDEN),
        'cmp_pe_v': 0.1 * jax.random.normal(ks[10], (DEPTH, CMP_LEN, NSA_DIM), jnp.float32),
        'cmp_w1_v': dense(ks[11], (DEPTH, CMP_LEN * NSA_DIM, CMP_HIDDEN), CMP_LEN * NSA_DIM),
        'cmp_w2_v': dense(ks[12], (DEPTH, CMP_HIDDEN, NSA_DIM), CMP_HIDDEN),
        'w_ffn_in': dense(ks[13], (DEPTH, D_MODEL, 2 * D_FF), D_MODEL),
        'w_ffn_out': dense(ks[14], (DEPTH, D_FF, D_MODEL), D_FF),
        'norm_mix': gain(ks[15], (DEPTH, D_MODEL)),
        'norm_ffn': gain(ks[16], (DEPTH, D_MODEL)),
    }

def first_block(x, w_in, w_out, hg_lb_logits, hg_gnorm, q_gain, k_gain,
              cmp_pe_k, cmp_w1_k, cmp_w2_k, cmp_pe_v, cmp_w1_v, cmp_w2_v,
              w_ffn_in, w_ffn_out, norm_mix, norm_ffn):
    lb = jnp.cumsum(jax.nn.softmax(hg_lb_logits.astype(jnp.float32), axis=0), axis=0)
    lb = lb - lb[0:1]
    h = x
    for l in range(DEPTH):
        xn = rms_norm(h, norm_mix[l])
        proj = xn @ w_in[l]
        (hq, hf, hi, hg, nq, kc, vc, ksl, vsl, ksw, vsw, ngate) = jnp.split(proj, IN_SPLIT_POINTS, axis=-1)
        o_hg = hgrn2_mixer(hq, hf, hi, hg, lb[l], hg_gnorm[l])
        o_nsa = nsa_mixer(nq, kc, vc, ksl, vsl, ksw, vsw, ngate, q_gain[l], k_gain[l],
                          cmp_pe_k[l], cmp_w1_k[l], cmp_w2_k[l], cmp_pe_v[l], cmp_w1_v[l], cmp_w2_v[l])
        mix = jnp.concatenate([o_hg, o_nsa], axis=-1)
        h = h + mix @ w_out[l]
        xn = rms_norm(h, norm_ffn[l])
        gu = xn @ w_ffn_in[l]
        g_ff, u_ff = gu[..., :D_FF], gu[..., D_FF:]
        h = h + (jax.nn.silu(g_ff) * u_ff) @ w_ffn_out[l]
    return h


DEPTH_2 = 1

HEAD_DIM = 64
FOX_HEADS = 8
FOX_WIDTH = FOX_HEADS * HEAD_DIM
DIFF_HEADS = 4
DIFF_QK_WIDTH = DIFF_HEADS * 2 * HEAD_DIM
DIFF_V_DIM = 2 * HEAD_DIM
DIFF_V_WIDTH = DIFF_HEADS * DIFF_V_DIM
IN_WIDTH_2 = 3 * FOX_WIDTH + FOX_HEADS + 2 * DIFF_QK_WIDTH + DIFF_V_WIDTH + 2 * D_MODEL
MEM_LEN = 256
CROSS_HEADS = 4
CROSS_WIDTH = CROSS_HEADS * HEAD_DIM
N_GROUPS = 4
EXPERTS_PER_GROUP = 8
N_EXPERTS = N_GROUPS * EXPERTS_PER_GROUP
TOP_K = 2
D_FF_EXPERT = 512
MOE_BLOCK = 256
Q_BLOCK = 128
NORM_EPS = 1e-6
SUBLN_EPS = 1e-5
FGATE_BIAS_INIT = 3.0


def _rms_norm(t, g, eps=NORM_EPS):
    tf = t.astype(jnp.float32)
    tf = tf * lax.rsqrt(jnp.mean(tf * tf, axis=-1, keepdims=True) + eps)
    return (tf * g.astype(jnp.float32)).astype(t.dtype)

def _split_heads(t, n):
    b, s, w = t.shape
    return t.reshape(b, s, n, w // n).transpose(0, 2, 1, 3)

def _merge_heads(t):
    b, h, s, d = t.shape
    return t.transpose(0, 2, 1, 3).reshape(b, s, h * d)

def _in_offsets():
    sizes = (FOX_WIDTH, FOX_WIDTH, FOX_WIDTH, FOX_HEADS, DIFF_QK_WIDTH, DIFF_QK_WIDTH,
             DIFF_V_WIDTH, D_MODEL, D_MODEL)
    return [int(o) for o in np.cumsum(sizes)[:-1]]

def _rope_tables(positions, dtype):
    half = HEAD_DIM // 2
    inv_freq = ROPE_THETA ** (-jnp.arange(half, dtype=jnp.float32) * 2.0 / HEAD_DIM)
    ang = positions.astype(jnp.float32)[..., None] * inv_freq
    cos = jnp.cos(ang)[:, :, None, None, :].astype(dtype)
    sin = jnp.sin(ang)[:, :, None, None, :].astype(dtype)
    return cos, sin

def _rope(t, cos, sin):
    half = t.shape[-1] // 2
    t1, t2 = t[..., :half], t[..., half:]
    return jnp.concatenate([t1 * cos - t2 * sin, t2 * cos + t1 * sin], axis=-1)

def _causal_mask(q0, q1):
    qpos = q0 + jnp.arange(q1 - q0)
    kpos = jnp.arange(q1)
    return qpos[:, None] >= kpos[None, :]

def _fox_attention(q, k, v, log_f):
    c = jnp.cumsum(log_f, axis=-1)
    scale = HEAD_DIM ** -0.5
    n_q = q.shape[2]
    outs = []
    for blk in range(n_q // Q_BLOCK):
        q0, q1 = blk * Q_BLOCK, (blk + 1) * Q_BLOCK
        s = jnp.einsum('bhqd,bhkd->bhqk', q[:, :, q0:q1], k[:, :, :q1]).astype(jnp.float32) * scale
        s = s + c[:, :, q0:q1, None] - c[:, :, None, :q1]
        s = jnp.where(_causal_mask(q0, q1), s, -jnp.inf)
        p = jax.nn.softmax(s, axis=-1).astype(v.dtype)
        outs.append(jnp.einsum('bhqk,bhkd->bhqd', p, v[:, :, :q1]))
    return jnp.concatenate(outs, axis=2)

def _diff_attention(q1, q2, k1, k2, v, lam):
    scale = HEAD_DIM ** -0.5
    n_q = q1.shape[2]
    outs = []
    for blk in range(n_q // Q_BLOCK):
        q0, qe = blk * Q_BLOCK, (blk + 1) * Q_BLOCK
        mask = _causal_mask(q0, qe)
        s1 = jnp.einsum('bhqd,bhkd->bhqk', q1[:, :, q0:qe], k1[:, :, :qe]).astype(jnp.float32) * scale
        s2 = jnp.einsum('bhqd,bhkd->bhqk', q2[:, :, q0:qe], k2[:, :, :qe]).astype(jnp.float32) * scale
        p1 = jax.nn.softmax(jnp.where(mask, s1, -jnp.inf), axis=-1)
        p2 = jax.nn.softmax(jnp.where(mask, s2, -jnp.inf), axis=-1)
        a = (p1 - lam * p2).astype(v.dtype)
        outs.append(jnp.einsum('bhqk,bhkd->bhqd', a, v[:, :, :qe]))
    return jnp.concatenate(outs, axis=2)

def _cross_attention(hx, hm, w_q, w_kv, w_o):
    b, m = hm.shape[0], hm.shape[1]
    q = _split_heads(hx @ w_q, CROSS_HEADS)
    kv = (hm @ w_kv).reshape(b, m, 2, CROSS_HEADS, HEAD_DIM)
    k = kv[:, :, 0].transpose(0, 2, 1, 3)
    v = kv[:, :, 1].transpose(0, 2, 1, 3)
    s = jnp.einsum('bhsd,bhmd->bhsm', q, k).astype(jnp.float32) * HEAD_DIM ** -0.5
    p = jax.nn.softmax(s, axis=-1).astype(v.dtype)
    return _merge_heads(jnp.einsum('bhsm,bhmd->bhsd', p, v)) @ w_o

def _routed_experts(t, expert_ids, gate_w, w_gate, w_up, w_down):
    n_tok, d = t.shape
    n_assign = n_tok * TOP_K
    flat_e = expert_ids.reshape(n_assign).astype(jnp.int32)
    flat_tok = jnp.arange(n_assign, dtype=jnp.int32) // TOP_K
    flat_w = gate_w.reshape(n_assign)
    order = jnp.argsort(flat_e)
    e_sorted = flat_e[order]
    counts = jnp.zeros((N_EXPERTS,), jnp.int32).at[flat_e].add(1)
    padded = (counts + MOE_BLOCK - 1) // MOE_BLOCK * MOE_BLOCK
    pad_end = jnp.cumsum(padded)
    pad_start = pad_end - padded
    seg_start = jnp.cumsum(counts) - counts
    dest = pad_start[e_sorted] + jnp.arange(n_assign, dtype=jnp.int32) - seg_start[e_sorted]
    n_blocks = -(-n_assign // MOE_BLOCK) + N_EXPERTS
    n_rows = n_blocks * MOE_BLOCK
    row_tok = jnp.full((n_rows,), n_tok, jnp.int32).at[dest].set(flat_tok[order])
    row_w = jnp.zeros((n_rows,), t.dtype).at[dest].set(flat_w[order])
    block_start = jnp.arange(n_blocks, dtype=jnp.int32) * MOE_BLOCK
    block_expert = jnp.minimum(jnp.searchsorted(pad_end, block_start, side='right'), N_EXPERTS - 1)
    t_pad = jnp.concatenate([t, jnp.zeros((1, d), t.dtype)], axis=0)
    xs = t_pad[row_tok].reshape(n_blocks, MOE_BLOCK, d)

    def expert_block(args):
        xb, e = args
        hb = jax.nn.silu(xb @ w_gate[e]) * (xb @ w_up[e])
        return hb @ w_down[e]

    ys = lax.map(expert_block, (xs, block_expert)).reshape(n_rows, d)
    out = jnp.zeros((n_tok + 1, d), t.dtype).at[row_tok].add(ys * row_w[:, None])
    return out[:n_tok]

def _hier_moe(t, w_group, b_group, w_expert, b_expert, w_gate, w_up, w_down):
    n_tok = t.shape[0]
    group_logits = (t @ w_group + b_group).astype(jnp.float32)
    group_prob = jax.nn.softmax(group_logits, axis=-1)
    g_sel = jnp.argmax(group_logits, axis=-1)
    g_w = jnp.take_along_axis(group_prob, g_sel[:, None], axis=-1)
    exp_logits = (t @ w_expert + b_expert).astype(jnp.float32).reshape(n_tok, N_GROUPS, EXPERTS_PER_GROUP)
    sel_logits = jnp.take_along_axis(exp_logits, g_sel[:, None, None], axis=1)[:, 0]
    top_vals, top_idx = lax.top_k(sel_logits, TOP_K)
    weights = jax.nn.softmax(top_vals, axis=-1) * g_w
    expert_ids = g_sel[:, None].astype(jnp.int32) * EXPERTS_PER_GROUP + top_idx.astype(jnp.int32)
    return _routed_experts(t, expert_ids, weights.astype(t.dtype), w_gate, w_up, w_down)

def second_inputs(seed: int = 0) -> dict:
    key = jax.random.key(seed)
    ks = jax.random.split(key, 32)
    f32 = jnp.float32
    L = DEPTH_2

    def nrm(k, shape, fan_in):
        return jax.random.normal(k, shape, f32) * fan_in ** -0.5

    def gain(k, shape):
        return 1.0 + 0.02 * jax.random.normal(k, shape, f32)

    return {
        'x': jax.random.normal(ks[0], (BATCH, SEQ, D_MODEL), f32),
        'mem': jax.random.normal(ks[1], (BATCH, MEM_LEN, D_MODEL), f32),
        'positions': jnp.broadcast_to(jnp.arange(SEQ, dtype=jnp.int32), (BATCH, SEQ)),
        'g_mix': gain(ks[2], (L, D_MODEL)),
        'w_in': nrm(ks[3], (L, D_MODEL, IN_WIDTH_2), D_MODEL),
        'b_fgate': FGATE_BIAS_INIT + 0.1 * jax.random.normal(ks[4], (L, FOX_HEADS), f32),
        'w_branch_a': nrm(ks[5], (L, FOX_WIDTH, D_MODEL), FOX_WIDTH),
        'w_branch_b': nrm(ks[6], (L, DIFF_V_WIDTH, D_MODEL), DIFF_V_WIDTH),
        'w_out': nrm(ks[7], (L, D_MODEL, D_MODEL), D_MODEL),
        'lambda_q1': 0.1 * jax.random.normal(ks[8], (L, HEAD_DIM), f32),
        'lambda_k1': 0.1 * jax.random.normal(ks[9], (L, HEAD_DIM), f32),
        'lambda_q2': 0.1 * jax.random.normal(ks[10], (L, HEAD_DIM), f32),
        'lambda_k2': 0.1 * jax.random.normal(ks[11], (L, HEAD_DIM), f32),
        'g_diff_sub': gain(ks[12], (L, DIFF_V_DIM)),
        'g_cross': gain(ks[13], (L, D_MODEL)),
        'g_mem': gain(ks[14], (L, D_MODEL)),
        'w_cq': nrm(ks[15], (L, D_MODEL, CROSS_WIDTH), D_MODEL),
        'w_ckv': nrm(ks[16], (L, D_MODEL, 2 * CROSS_WIDTH), D_MODEL),
        'w_co': nrm(ks[17], (L, CROSS_WIDTH, D_MODEL), CROSS_WIDTH),
        'g_ffn': gain(ks[18], (L, D_MODEL)),
        'w_group': nrm(ks[19], (L, D_MODEL, N_GROUPS), D_MODEL),
        'b_group': 0.01 * jax.random.normal(ks[20], (L, N_GROUPS), f32),
        'w_expert': nrm(ks[21], (L, D_MODEL, N_EXPERTS), D_MODEL),
        'b_expert': 0.01 * jax.random.normal(ks[22], (L, N_EXPERTS), f32),
        'w_exp_gate': nrm(ks[23], (L, N_EXPERTS, D_MODEL, D_FF_EXPERT), D_MODEL),
        'w_exp_up': nrm(ks[24], (L, N_EXPERTS, D_MODEL, D_FF_EXPERT), D_MODEL),
        'w_exp_down': nrm(ks[25], (L, N_EXPERTS, D_FF_EXPERT, D_MODEL), D_FF_EXPERT),
        'g_final': gain(ks[26], (D_MODEL,)),
    }

def second_block(x, mem, positions, g_mix, w_in, b_fgate, w_branch_a, w_branch_b, w_out,
              lambda_q1, lambda_k1, lambda_q2, lambda_k2, g_diff_sub, g_cross, g_mem,
              w_cq, w_ckv, w_co, g_ffn, w_group, b_group, w_expert, b_expert,
              w_exp_gate, w_exp_up, w_exp_down, g_final):
    b, s, d = x.shape
    cos, sin = _rope_tables(positions, x.dtype)
    offsets = _in_offsets()
    for l in range(DEPTH_2):
        lambda_init = 0.8 - 0.6 * math.exp(-0.3 * l)
        h = _rms_norm(x, g_mix[l])
        fq, fk, fv, f_logit, dq, dk, dv, gate_a, gate_b = jnp.split(h @ w_in[l], offsets, axis=-1)
        log_f = jax.nn.log_sigmoid((f_logit + b_fgate[l]).astype(jnp.float32)).transpose(0, 2, 1)
        y_a = _fox_attention(_split_heads(fq, FOX_HEADS), _split_heads(fk, FOX_HEADS),
                             _split_heads(fv, FOX_HEADS), log_f)
        y_a = _merge_heads(y_a)
        dq = _rope(dq.reshape(b, s, DIFF_HEADS, 2, HEAD_DIM), cos, sin)
        dk = _rope(dk.reshape(b, s, DIFF_HEADS, 2, HEAD_DIM), cos, sin)
        lam = (jnp.exp(jnp.sum(lambda_q1[l].astype(jnp.float32) * lambda_k1[l].astype(jnp.float32)))
               - jnp.exp(jnp.sum(lambda_q2[l].astype(jnp.float32) * lambda_k2[l].astype(jnp.float32)))
               + lambda_init)
        y_b = _diff_attention(dq[:, :, :, 0].transpose(0, 2, 1, 3), dq[:, :, :, 1].transpose(0, 2, 1, 3),
                              dk[:, :, :, 0].transpose(0, 2, 1, 3), dk[:, :, :, 1].transpose(0, 2, 1, 3),
                              _split_heads(dv, DIFF_HEADS), lam)
        y_b = _merge_heads(_rms_norm(y_b, g_diff_sub[l], SUBLN_EPS) * (1.0 - lambda_init))
        merged = (jax.nn.sigmoid(gate_a) * (y_a @ w_branch_a[l])
                  + jax.nn.sigmoid(gate_b) * (y_b @ w_branch_b[l]))
        x = x + merged @ w_out[l]
        x = x + _cross_attention(_rms_norm(x, g_cross[l]), _rms_norm(mem, g_mem[l]),
                                 w_cq[l], w_ckv[l], w_co[l])
        hm = _rms_norm(x, g_ffn[l]).reshape(b * s, d)
        x = x + _hier_moe(hm, w_group[l], b_group[l], w_expert[l], b_expert[l],
                          w_exp_gate[l], w_exp_up[l], w_exp_down[l]).reshape(b, s, d)
    return _rms_norm(x, g_final)


def setup_inputs(seed=0):
    out = dict(first_inputs(seed))
    for name, value in second_inputs(seed + 1).items():
        if name != "x":
            out[name + "_2"] = value
    return out


def reference(
    x, w_in, w_out, hg_lb_logits, hg_gnorm, q_gain, k_gain, cmp_pe_k, cmp_w1_k, cmp_w2_k,
    cmp_pe_v, cmp_w1_v, cmp_w2_v, w_ffn_in, w_ffn_out, norm_mix, norm_ffn, mem_2, positions_2,
    g_mix_2, w_in_2, b_fgate_2, w_branch_a_2, w_branch_b_2, w_out_2, lambda_q1_2, lambda_k1_2,
    lambda_q2_2, lambda_k2_2, g_diff_sub_2, g_cross_2, g_mem_2, w_cq_2, w_ckv_2, w_co_2,
    g_ffn_2, w_group_2, b_group_2, w_expert_2, b_expert_2, w_exp_gate_2, w_exp_up_2,
    w_exp_down_2, g_final_2,
):
    x = first_block(
        x, w_in, w_out, hg_lb_logits, hg_gnorm, q_gain, k_gain, cmp_pe_k, cmp_w1_k, cmp_w2_k,
        cmp_pe_v, cmp_w1_v, cmp_w2_v, w_ffn_in, w_ffn_out, norm_mix, norm_ffn,
    )
    return second_block(
        x, mem_2, positions_2, g_mix_2, w_in_2, b_fgate_2, w_branch_a_2, w_branch_b_2, w_out_2,
        lambda_q1_2, lambda_k1_2, lambda_q2_2, lambda_k2_2, g_diff_sub_2, g_cross_2, g_mem_2,
        w_cq_2, w_ckv_2, w_co_2, g_ffn_2, w_group_2, b_group_2, w_expert_2, b_expert_2,
        w_exp_gate_2, w_exp_up_2, w_exp_down_2, g_final_2,
    )


_drawn_inputs = setup_inputs


def setup_inputs(seed=0):
    import zlib

    import numpy as np

    out = dict(_drawn_inputs(seed))
    spreads = {}
    factors = {'hg_lb_logits': 5.621,
     'q_gain': 4.261,
     'k_gain': 4.115,
     'cmp_pe_k': 3.168,
     'g_mix_2': 3.455,
     'b_fgate_2': 4.58,
     'lambda_q2_2': 3.255,
     'lambda_k2_2': 8.0,
     'g_diff_sub_2': 7.875,
     'g_cross_2': 8.0,
     'g_mem_2': 8.0,
     'g_ffn_2': 2.915,
     'b_group_2': 8.0,
     'b_expert_2': 8.0,
     'g_final_2': 2.757}
    for name, (base, spread) in spreads.items():
        noise = np.random.default_rng([zlib.crc32(name.encode()), seed]).standard_normal(out[name].shape)
        drawn = base * np.exp(spread * noise) if base else spread * noise
        out[name] = __import__('jax').numpy.asarray(drawn.astype(out[name].dtype))
    for name, factor in factors.items():
        out[name] = (out[name] * factor).astype(out[name].dtype)
    return out
```

```python
from contextlib import ExitStack

import numpy as np

import concourse.bass as bass
from concourse import mybir

F32 = mybir.dt.float32
BF16 = mybir.dt.bfloat16
I32 = mybir.dt.int32
ALU = mybir.AluOpType
ACT = mybir.ActivationFunctionType
AX = mybir.AxisListType

P = 128
T = 512
D = 1024
KO = D // P
QT = T // P
DEPTH = 2
HEADS = 8
CMP_N = (T - 32) // 16 + 1
FF = 2816
FFC = FF // P
RING = 4
MEM = 256
NEXP = 32
OVER = 7
NEG = -1e30

T_FEAT = 0
T_HI = 12
T_NQ = 16
T_V = 22
T_C = 24
T_CMP = 26
T_WO = 34
T_FFI = 42
T_FFO = 86
T_LAYER = 108
B_FQ, B_FK, B_FV, B_DQ, B_DK, B_DV, B_GA = 0, 4, 8, 12, 16, 20, 24
B_CK, B_CV, B_AB, B_WO, B_CQ, B_CO, B_TILES = 40, 42, 44, 52, 60, 62, 64
NTILES = DEPTH * T_LAYER + B_TILES

C_MIX, C_FFN, C_GN, C_QG, C_KG, C_PE, C_LB, NCOL = 0, 8, 16, 17, 18, 21, 85, 93
ARENA = 25600
LEVELS = 7
MISC = 8 * 24 + 2 * 2 * 64
M_MIX, M_MEM, M_CROSS, M_FFN, M_SUB, M_FREQ, M_BF, M_WF, M_LAM, M_WGE, M_BGE, M_IOTA, M_E, M_END = (
    0, 8, 16, 24, 32, 33, 34, 35, 99, 355, 643, 679, 807, 839)
YROWS = (NEXP + OVER + 1) * P
OVB = OVER + 1
K_ONES, K_BEFORE, K_TID = (2 + QT) * P, (3 + QT) * P, (4 + QT) * P
X_NCK, X_CKT, X_CV = 0, 512, 1024
TWO_PI = 2 * np.pi

ROPES = 7
EV = dict(
    tile=T_LAYER, evac=20, sq=16, sqsum=16, rstd=2, xn=16, h=16, params=2,
    f=4, ln=4, b=4, kd=4, kqexp=4, ediff=4, eexp=4, e=4, gram=16, at=16, qk=4,
    vh=4, vn=4, stat=ROPES, rrstd=ROPES, qn=ROPES, rot=ROPES, rope=ROPES,
    gatem=1, gate=1, dbuild=2, hid=4, kc=1, kce=1, vc=1, vcc=1,
    ket=3, kec=3, osum=4, ds=3, oc=4, s=3, hsq=4, hst=4, hrs=4, hn=4,
    sc=72, mx=72, p=72, tr=76, pt=76, pv=72, ofree=4, mixtok=4,
    res=14, silu=FFC, act=FFC,
    b_in=0, trig=0, trigs=0, fl=0, fls=0, flv=0, nck=0, lam=0, lams=0, lamv=0, fv=0, dv=0, cv=0, mrg=0, ms=0, msr=0)
CREDIT = dict(tile=RING, evac=2, rrstd=1, rope=1, h=8, act=2)


def build(nc, ring_w, xT_in, cols_in, misc_in, tabs_in, masks_in, par_in, sel_in, pos_in, memT_in, gfin_in,
          w_gate, w_up, w_down, hm_dram, y_dram, out):
    ctx = ExitStack()
    with ctx:
        def sb(name, shape, dt=F32):
            return ctx.enter_context(nc.sbuf_tensor(name, shape, dt))

        PS = ctx.enter_context(nc.psum_tensor("PS", [P, 8, 512], F32))

        xT = sb("xT", [P, KO, T])
        xn = sb("xn", [P, KO, T])
        ring = sb("ring", [P, RING, 1024])
        cols = sb("cols", [P, DEPTH, NCOL])
        lcol = sb("lcol", [P, NCOL])
        misc_all = sb("misc_all", [P, DEPTH, MISC])
        misc = sb("misc", [P, MISC])
        tabs = sb("tabs", [P, 2 * T])
        mats = sb("mats", [P, 6, P])
        maskb = sb("maskb", [P, K_TID + 8], BF16)
        eps = sb("eps", [P, 2])
        sq2 = sb("sq2", [P, 2, T])
        lnb = sb("lnb", [P, T])
        cos, sin = tabs[:, 0:T], tabs[:, T:2 * T]
        ones_d, ones_h, ones_64, rotm, ident = (mats[:, i, :] for i in range(5))
        valid0 = mats[:, 5, 0:1]
        ident_b = maskb[:, 0:P]
        causal_b = maskb[:, P:2 * P]

        arena = sb("arena", [P, ARENA])

        def at_(off, *shape):
            n = int(np.prod(shape))
            assert off + n <= ARENA, (off, n)
            v = arena[:, off:off + n]
            if len(shape) == 2:
                v = v.rearrange("p (a b) -> p a b", b=shape[1])
            elif len(shape) == 3:
                v = v.rearrange("p (a b c) -> p a b c", b=shape[1], c=shape[2])
            elif len(shape) == 4:
                v = v.rearrange("p (a b c d) -> p a b c d", b=shape[1], c=shape[2], d=shape[3])
            return v

        mixT = at_(0, 8, T)
        qT = at_(4096, 4, T)
        kT = at_(6144, 4, T)
        bT = at_(8192, 4, T)
        sgT = at_(10240, 4, T)
        Vh = at_(12288, 4, T)
        AT = at_(14336, 16, P)
        qr = at_(16384, 4, T)
        kr = at_(18432, 2, T)
        Vn = at_(19456, 4, 256)
        VC = at_(20480, 2, 4, 64)
        craw = at_(20992, 2, T)
        E = at_(22016, LEVELS, T)
        keT = at_(22016, 3, 4, P)
        Sst = at_(22016 + 1536, 4, P)
        Pr = at_(22016, 3, T)
        PTs = at_(22016 + 1536, 2, T)
        act = at_(4096, FFC, T)
        fq, fk, fv = at_(0, 4, T), at_(2048, 4, T), at_(4096, 4, T)
        dq, dk, dv = at_(6144, 4, T), at_(8192, 4, T), at_(10240, 4, T)
        yaT, ybT = fq, dq
        sga = at_(12288, 16, T)
        memn = at_(20480, KO, MEM)
        merged = xn
        cqT = at_(20480, 2, T)
        wg = (at_(8192, KO, T), at_(0, KO, T))
        wu = (at_(12288, KO, T), at_(4096, KO, T))
        wd = (at_(16384, 4, D), at_(20480, 4, D))
        yg = [at_(1024 * i, D) for i in range(2 * QT)]
        xtok = ring
        xflat = xT[:, :, :].rearrange("p a b -> p (a b)")
        xg = (xflat[:, 0:D], xflat[:, D:2 * D])
        ysb = (xflat[:, 2 * D:3 * D], xflat[:, 3 * D:4 * D])
        nflat = xn[:, :, :].rearrange("p a b -> p (a b)")
        xgT = (nflat[:, 0:D].rearrange("p (a b) -> p a b", b=P), nflat[:, D:2 * D].rearrange("p (a b) -> p a b", b=P))
        hsb = (nflat[:, 2048:2560], nflat[:, 2560:3072])
        hT = (nflat[:, 3072:3584].rearrange("p (a b) -> p a b", b=P),
              nflat[:, 3584:4096].rearrange("p (a b) -> p a b", b=P))

        ftmp = sb("ftmp", [P, 2, T])
        ekb = sb("ekb", [P, 4, T])
        ebuf, kdb = ekb[:, 0:2, :], ekb[:, 2:4, :]
        ebl = sb("ebl", [P, 4, 4])
        gmask = sb("gmask", [P, 8, P])
        cmask = sb("cmask", [P, T])
        gtmp = sb("gtmp", [P, 8 * P])
        qg = sb("qg", [P, 2, T])
        qnb = sb("qnb", [P, 2, T])
        rrs = sb("rrs", [P, 2, T])
        rstd = rrs[:, 0, :]
        DB = ekb[:, :, :].rearrange("p (v a) (g s) -> p v a g s", a=2, g=2)
        hid = sb("hid", [P, 2, 2, 62])
        kcr = sb("kcr", [P, 32])
        nmx = sb("nmx", [P, 4, 4])
        Lt = sb("Lt", [P, 2, 24])
        Rc = sb("Rc", [P, 24])
        gates = sb("gates", [P, QT, 24])
        oa = qg
        mixtok = ftmp[:, 0, :]
        lb = sb("lb", [P, DEPTH, 4])
        oml = sb("oml", [P, DEPTH, 4])
        lbl = sb("lbl", [P, 8])
        lnl = sq2[:, 0, 0:P].rearrange("p (a b) -> p a b", b=64)

        sems = {k: ctx.enter_context(nc.semaphore(k)) for k in EV}
        slot = [ctx.enter_context(nc.semaphore(f"slot{i}")) for i in range(RING)]
        s_in = ctx.enter_context(nc.semaphore("s_in"))
        s_out = ctx.enter_context(nc.semaphore("s_out"))
        s_pre = ctx.enter_context(nc.semaphore("s_pre"))
        a_ch = ctx.enter_context(nc.semaphore("a_ch"))
        v_ch = ctx.enter_context(nc.semaphore("v_ch"))
        g_ch = ctx.enter_context(nc.semaphore("g_ch"))
        NIN = 6
        par = misc_all[:, :, :].rearrange("p a b -> p (a b)")
        sel = gmask
        negc = ekb[:, 0, :]
        ckT = ekb[:, 1, :].rearrange("p (a b) -> p a b", b=MEM)
        cvt = ekb[:, 2, :].rearrange("p (a b) -> p a b", b=MEM)
        small = sb("small", [P, 16])
        coT = gmask[:, :, :].rearrange("p a b -> p (a b)").rearrange("p (a b) -> p a b", b=T)
        gfin = gmask[:, :, :].rearrange("p a b -> p (a b)")
        hmt = (ekb[:, 0:2, :].rearrange("p a b -> p (a b)"), ekb[:, 2:4, :].rearrange("p a b -> p (a b)"),
               qg[:, :, :].rearrange("p a b -> p (a b)"), qnb[:, :, :].rearrange("p a b -> p (a b)"))
        lg = tabs[:, 0:144].rearrange("p (q e) -> p q e", e=36)
        em, oh1, oh2, rnk, tmpe = (tabs[:, 144 + 128 * i:272 + 128 * i].rearrange("p (q e) -> p q e", e=NEXP)
                                   for i in range(5))
        rt = tabs[:, 784:1024]
        pos = sb("pos", [P, 2, QT])
        prel = sb("prel", [P, 2, QT])
        wts = sb("wts", [P, 2, QT])
        posi = sb("posi", [P, 2 * QT], I32)
        idxi = sb("idxi", [P, 2], I32)
        ovi = sb("ovi", [P, 16], I32)
        Ab = sb("Ab", [P, QT, NEXP], BF16)
        Ob = [sq2[:, u, 0:256].bitcast(BF16).rearrange("p (q s) -> p q s", s=P) for u in range(2)]
        hsilu = ftmp[:, 0, :]
        MS = {k: ctx.enter_context(nc.semaphore("m_" + k)) for k in (
            "gather", "tr", "te", "hd", "lg", "rq", "rp", "A", "rk", "ro", "odh", "od", "ix", "ii", "xt", "xea", "xev",
            "gg", "gu", "sl", "hm", "ht", "he", "dn", "yea", "yev", "gf", "fa", "fs", "ff")}
        MS.update({k: [ctx.enter_context(nc.semaphore(f"m_{k}{u}")) for u in range(n)]
                   for k, n in (("xg", 2), ("wg", 2), ("wu", 2), ("wd", 2), ("yd", 2), ("yg", QT))})

        def lin(i, u, mult=1, c=0):
            v = i * (2 * mult) + (u * mult + c)
            return max(v, 0) if isinstance(v, int) else v

        def dma_of(i, u):
            v = (i + u // 2) * 16 + 16
            return max(v, 0) if isinstance(v, int) else v

        def blocks(eng, body, first, end):
            for u in (0, 1):
                body(first // 2, u)
            if end > first + 2:
                with eng.Fori(first // 2 + 1, end // 2) as i:
                    for u in (0, 1):
                        body(i, u)

        def overflow(eng):
            return eng.If(eng.value_load(ovi[0:1, 8:9], min_val=0, max_val=OVER) > 0)

        def nth(name, l, n):
            return l * EV[name] + (n + CREDIT.get(name, 0))

        def nsa_items():
            items = []
            for qt in range(QT):
                q = slice(qt * P, qt * P + P)
                this = []
                for g in range(2):
                    half = slice(64 * g, 64 * g + 64)
                    sc = [(0, P, ident_b, maskb[:, 2 * P + qt * P:3 * P + qt * P])]
                    for j in range(4):
                        sc.append((32 * j, 32 * j + CMP_N, qr[half, j, q], kcr[half, 0:CMP_N]))
                    pv = [(PS[:, 7, 256 * g:256 * g + 256], 0, VC[:, g].rearrange("p j d -> p (j d)"), True, True)]
                    this.append(dict(kind="cmp", n=P, sc=sc, nb=1, pv=pv, L=Lt[:, qt % 2, 4 * g:4 * g + 4]))
                for br in range(2):
                    for h in range(HEADS):
                        g = h // 4
                        half = slice(64 * g, 64 * g + 64)
                        n = P * (qt + 1)
                        sc = [(0, n, qr[half, h % 4, q], kr[half, br, 0:n]), (n - P, n, ident_b, causal_b)]
                        pv = [(PS[:, 5 + br, 64 * h:64 * h + 64], kb,
                               Vn[:, kb, 128 * br + 64 * g:128 * br + 64 * g + 64], kb == 0, kb == qt)
                              for kb in range(qt + 1)]
                        this.append(dict(kind="full", n=n, sc=sc, nb=qt + 1, pv=pv,
                                         L=Lt[:, qt % 2, 8 + 8 * br + h:9 + 8 * br + h]))
                this[0]["first"] = qt
                this[-1]["last"] = qt
                mix = dict(kind="mix", mixn=qt, nb=4, src=mixtok,
                           dst=mixT[:, 4:8, (qt - 1) * P:qt * P])
                items += this[:4] + ([mix] if qt else []) + this[4:]
            items += [None, dict(kind="mix", mixn=QT, nb=4, src=mixtok, dst=mixT[:, 4:8, (QT - 1) * P:QT * P])]
            return number(items)

        def causal_item(kind, qt, q, kk, pv, L, extra=()):
            n = P * (qt + 1)
            sc = [(0, n, q, kk)] + list(extra) + [(n - P, n, ident_b, causal_b)]
            return dict(kind=kind, n=n, sc=sc, nb=qt + 1, pv=pv, L=L)

        def block2_items():
            items = []
            for qt in range(QT):
                qs, n = slice(qt * P, qt * P + P), P * (qt + 1)
                this = []
                for h in range(8):
                    half = slice(64 * (h % 2), 64 * (h % 2) + 64)
                    pv = [(PS[:, 5, 64 * h:64 * h + 64], kb, fv[:, kb, 64 * h:64 * h + 64], kb == 0, kb == qt)
                          for kb in range(qt + 1)]
                    this.append(causal_item("full", qt, fq[half, h // 2, qs], fk[half, h // 2, 0:n], pv,
                                            Lt[:, qt % 2, h:h + 1], [(0, n, sel[:, h, :], negc[:, 0:n])]))
                for i in range(4):
                    for c in range(2):
                        half = slice(64 * c, 64 * c + 64)
                        pv = [(PS[:, 6 + c, P * i:P * i + P], kb, dv[:, kb, P * i:P * i + P], kb == 0, kb == qt)
                              for kb in range(qt + 1)]
                        this.append(causal_item("full", qt, dq[half, i, qs], dk[half, i, 0:n], pv,
                                                Lt[:, qt % 2, 8 + 4 * c + i:9 + 4 * c + i]))
                this[0]["first"] = qt
                this[-1]["last"] = qt

                def mixes(q):
                    s = slice(q * P, q * P + P)
                    return [dict(kind="mix", mixn=2 * q + 1, nb=4, src=ftmp[:, 0, :], dst=yaT[:, :, s]),
                            dict(kind="mix", mixn=2 * q + 2, nb=4, src=ftmp[:, 1, :], dst=ybT[:, :, s], sub=True)]
                items += this[:6] + (mixes(qt - 1) if qt else []) + this[6:]
            items += [None] * 5 + mixes(QT - 1)
            return number(items)

        def cross_items(k0, t0):
            items = []
            for qt in range(QT):
                this = []
                for h in range(4):
                    half = slice(64 * (h % 2), 64 * (h % 2) + 64)
                    pv = [(PS[:, 5, 64 * h:64 * h + 64], kb, cvt[:, kb, 64 * h:64 * h + 64], kb == 0, kb == 1)
                          for kb in range(2)]
                    this.append(dict(kind="full", n=MEM, nb=2, pv=pv, L=Lt[:, qt % 2, h:h + 1],
                                     sc=[(0, MEM, cqT[half, h // 2, qt * P:qt * P + P], ckT[half, h // 2, :])]))
                this[0]["first"] = 4 + qt
                this[-1]["last"] = qt

                def mix(q):
                    return dict(kind="mix", mixn=8 + q + 1, nb=2, src=ftmp[:, 0, 0:256], dst=coT[:, :, q * P:q * P + P])
                items += this[:3] + ([mix(qt - 1)] if qt else []) + this[3:]
            items += [None, mix(QT - 1)]
            return number(items, k0, t0)

        def number(items, k0=0, t0=0):
            k, t = k0, t0
            for it in items:
                if it is None:
                    continue
                it["t"] = t
                t += 1
                if it["kind"] != "mix":
                    it["k"] = k
                    k += 1
            byk = {it["k"]: it for it in items if it and "k" in it}
            for it in items:
                if it and it.get("k", 0) >= k0 + 3:
                    it["t3"] = byk[it["k"] - 3]["t"]
                if it and "t" in it:
                    j = [x for x in items if x and x["t"] == it["t"] - 2 and x["kind"] != "mix"]
                    if j:
                        it["pv2"] = j[0]["k"]
            return items

        NSA = nsa_items()
        BL2 = block2_items()
        CROSS = cross_items(64, 72)
        LAG_T, LAG_V = 2, 3

        block = ctx.enter_context(nc.Block())

        @block.sync
        def _(sp):
            sp.dma_start(xT[:, :, :], xT_in.rearrange("c p t -> p c t")).then_inc(s_in, 16)
            sp.dma_start(cols[:, :, :], cols_in).then_inc(s_in, 16)
            sp.dma_start(tabs[:, :], tabs_in[:, 0:2 * T]).then_inc(s_in, 16)
            sp.dma_start(misc_all[:, :, :], misc_in).then_inc(s_in, 16)
            sp.dma_start(mats[:, :, :], tabs_in[:, 2 * T:2 * T + 6 * P].rearrange("p (a b) -> p a b", b=P)
                           ).then_inc(s_in, 16)
            sp.dma_start(gmask[:, :, :], tabs_in[:, 2 * T + 6 * P:2 * T + 14 * P].rearrange(
                "p (a b) -> p a b", b=P)).then_inc(s_in, 16)
            sp.dma_start(maskb[:, :].bitcast(mybir.dt.uint16), masks_in).then_inc(s_in, 16)
            with sp.Fori(0, NTILES_RUN // RING) as i:
                for s in range(RING):
                    sp.wait_ge(sems["tile"], i * RING + (s + 1))
                    sp.dma_start(ring[:, s, :], ring_w[i * RING + s]).then_inc(slot[s], 16)
            sp.wait_ge(sems["mrg"], 8)

            def load_gu(i, u, e):
                sp.wait_ge(MS["gu"], lin(i, u, 1, -1))
                for name, w, src in (("wg", wg, w_gate), ("wu", wu, w_up)):
                    sp.dma_start(w[u % 2], src[e].rearrange("(k p) n -> p k n", p=P)).then_inc(
                        MS[name][u % 2], 16)

            def load_d(i, u, e):
                sp.wait_ge(MS["dn"], lin(i, u, 2, -2))
                sp.dma_start(wd[u % 2], w_down[e].rearrange("(k p) n -> p k n", p=P)).then_inc(
                    MS["wd"][u % 2], 16)

            def store_y(i, u):
                sp.wait_ge(MS["yea"], lin(i, u, 1, 1))
                sp.wait_ge(MS["yev"], lin(i, u, 1, 1))
                sp.dma_start(y_dram[i + u // 2, u % 2], ysb[u % 2]).then_inc(MS["yd"][u % 2], 16)

            load_gu(0, 0, 0)
            load_d(0, 0, 0)
            load_gu(0, 1, 1)
            sp.wait_ge(sems["h"], nth("h", DEPTH, 16))
            load_gu(0, 2, 2)
            load_d(0, 1, 1)
            load_gu(0, 3, 3)
            store_y(0, 0)
            load_d(0, 2, 2)
            with sp.Fori(1, NEXP // 2 - 1) as i:
                for u in (0, 1):
                    load_gu(i, u + 2, i * 2 + (u + 2))
                    store_y(i, u - 1)
                    load_d(i, u + 1, i * 2 + (u + 1))
            i = NEXP // 2 - 1
            store_y(i, -1)
            load_d(i, 1, NEXP - 1)
            store_y(i, 0)
            store_y(i, 1)
            sp.wait_ge(MS["ro"], 1)
            with overflow(sp):
                ex = [sp.value_load(ovi[0:1, j:j + 1], min_val=0, max_val=NEXP - 1) for j in range(OVB)]
                i = NEXP // 2
                load_gu(i, 0, ex[0])
                load_gu(i, 1, ex[1])
                load_d(i, 0, ex[0])
                for j in range(OVB):
                    if j + 2 < OVB:
                        load_gu(i, j + 2, ex[j + 2])
                    if j:
                        store_y(i, j - 1)
                    if j + 1 < OVB:
                        load_d(i, j + 1, ex[j + 1])
                store_y(i, OVB - 1)
                sp.wait_ge(MS["yd"][(OVB - 2) % 2], dma_of(i, OVB - 2))
                sp.wait_ge(MS["yd"][(OVB - 1) % 2], dma_of(i, OVB - 1))
            sp.wait_ge(MS["yd"][0], dma_of(NEXP // 2 - 1, 0))
            sp.wait_ge(MS["yd"][1], dma_of(NEXP // 2 - 1, 1))
            for qt in range(QT):
                sp.wait_ge(MS["ff"], qt + 1)
                sp.dma_start(out[qt], yg[2 * qt]).then_inc(s_out, 16)
            sp.wait_ge(s_out, 16 * QT)

        @block.gpsimd
        def _(pool):
            def layer(l):
                for h in range(4):
                    pool.wait_ge(sems["eexp"], nth("eexp", l, h + 1))
                    pool.wait_ge(sems["evac"], nth("evac", l, 5 + h))
                    for j in range(LEVELS):
                        w = 64 >> j
                        e = E[:, j, :].rearrange("p (n two w) -> p n two w", two=2, w=w)
                        kv = kT[:, h, :].rearrange("p (n two w) -> p n two w", two=2, w=w)
                        qv = qT[:, h, :].rearrange("p (n two w) -> p n two w", two=2, w=w)
                        nc.gpsimd.tensor_tensor(e[:, :, 0, :], e[:, :, 0, :], kv[:, :, 0, :], ALU.mult)
                        ins = nc.gpsimd.tensor_tensor(e[:, :, 1, :], e[:, :, 1, :], qv[:, :, 1, :], ALU.mult)
                    ins.then_inc(sems["e"], 1)

            with pool.Fori(0, DEPTH_RUN) as l:
                layer(l)

            def gather(i, u):
                pool.wait_ge(MS["ii"], lin(i, u, 1, 1))
                pool.wait_ge(MS["xt"], lin(i, u, 1, -1))
                pool.sem_inc(MS["gather"], 1)
                pool.indirect_dma_start(xg[u % 2], None, hm_dram, bass.IndirectOffsetOnAxis(
                    ap=idxi[:, u % 2:u % 2 + 1], axis=0)).then_inc(MS["xg"][u % 2], 16)

            pool.wait_ge(MS["hd"], 16 * QT)
            gather(0, 0)
            gather(0, 1)
            blocks(pool, lambda i, u: gather(i, u + 2), 0, NEXP)
            def back(rows):
                for qt in range(QT):
                    for k in range(2):
                        pool.indirect_dma_start(yg[2 * qt + k], None, y_dram[0:rows // (2 * P)].rearrange(
                            "a b p d -> (a b p) d"), bass.IndirectOffsetOnAxis(
                                ap=posi[:, QT * k + qt:QT * k + qt + 1], axis=0)).then_inc(MS["yg"][qt], 16)

            pool.wait_ge(MS["yd"][0], dma_of(NEXP // 2 - 1, 0))
            pool.wait_ge(MS["yd"][1], dma_of(NEXP // 2 - 1, 1))
            with overflow(pool):
                blocks(pool, lambda i, u: gather(i, u + 2), NEXP, NEXP + OVB)
                pool.wait_ge(MS["yd"][0], dma_of((NEXP + OVB) // 2 - 1, 0))
                pool.wait_ge(MS["yd"][1], dma_of((NEXP + OVB) // 2 - 1, 1))
                back(YROWS)
            with pool.Else():
                back(NEXP * P)

        @block.scalar
        def _(act_e):
            def norm_rstd(l, n, hn, src=xT, w=T, bank=0):
                for c in range(KO):
                    if hn is not None:
                        act_e.wait_ge(sems["h"], nth("h", l, 8 * hn + c + 1 - 8))
                    i = 8 * n + c
                    if c >= 2:
                        act_e.wait_ge(sems["sqsum"], nth("sqsum", l, i - 1))
                    nc.scalar.activation(sq2[:, c % 2, 0:w], src[:, c, :], ACT.Square).then_inc(sems["sq"], 1)
                act_e.wait_ge(sems["sqsum"], nth("sqsum", l, 8 * n + 8))
                nc.scalar.activation(lnb[:, 0:w], PS[:, bank, 0:w], ACT.Ln, bias=eps[:, 0:1]).then_inc(a_ch, 1)
                act_e.wait_ge(a_ch, a_step())
                nc.scalar.activation(rstd[:, 0:w], lnb[:, 0:w], ACT.Exp, scale=-0.5).then_inc(sems["rstd"], 1)

            ch = {"base": 0, "n": 0}

            def a_step():
                ch["n"] += 1
                return ch["base"] + ch["n"]

            def rope_evac(l, r, src, n):
                if r >= 2:
                    act_e.wait_ge(sems["qn"], nth("qn", l, r - 1))
                gain = lcol[:, C_QG:C_QG + 1] if r < 4 else lcol[:, C_KG + (r - 3) % 3:C_KG + (r - 3) % 3 + 1]
                nc.scalar.activation(qg[:, r % 2, 0:n], src, ACT.Identity, scale=gain)
                return nc.scalar.activation(sq2[:, r % 2, 0:n], src, ACT.Square)

            def evac(l, t):
                act_e.wait_ge(sems["tile"], nth("tile", l, tile_of(t) + 1))
                src = PS[:, t % 2, :]
                if t < 4:
                    ins = nc.scalar.activation(kT[:, t, :], src, ACT.Sigmoid)
                elif t < 8:
                    ins = nc.scalar.activation(qT[:, t - 4, :], src, ACT.Silu)
                elif t < 12:
                    ins = nc.scalar.activation(sgT[:, t - 8, :], src, ACT.Silu)
                elif t < 18:
                    ins = rope_evac(l, t - 12, src, T)
                else:
                    ins = nc.scalar.activation(craw[:, t - 18, :], src, ACT.Identity)
                ins.then_inc(sems["evac"], 1)

            def step(l, kind, i):
                if kind == "norm":
                    norm_rstd(l, i, i)
                elif kind == "feat":
                    evac(l, i)
                elif kind == "gate_h":
                    act_e.wait_ge(sems["f"], nth("f", l, i + 1))
                    nc.scalar.activation(ftmp[:, i % 2, :], ftmp[:, i % 2, :], ACT.Ln).then_inc(sems["ln"], 1)
                elif kind == "scan":
                    act_e.wait_ge(sems["kd"], nth("kd", l, i + 1))
                    if i >= 2:
                        act_e.wait_ge(sems["qk"], nth("qk", l, i - 1))
                    nc.scalar.activation(ebuf[:, i % 2, :], bT[:, i, :], ACT.Exp)
                    nc.scalar.activation(kdb[:, i % 2, :], kdb[:, i % 2, :], ACT.Exp).then_inc(sems["kqexp"], 1)
                elif kind == "decay":
                    act_e.wait_ge(sems["ediff"], nth("ediff", l, i + 1))
                    nc.scalar.activation(E[:, :, :], E[:, :, :], ACT.Exp).then_inc(sems["eexp"], 1)
                elif kind == "hi":
                    act_e.wait_ge(sems["tile"], nth("tile", l, T_HI + 4))
                    for st in range(4):
                        nc.scalar.activation(Vh[:, st, :], PS[:, 2 + st, :], ACT.Identity).then_inc(sems["vh"], 1)
                elif kind == "v":
                    act_e.wait_ge(sems["tile"], nth("tile", l, T_V + 2))
                    for st in range(4):
                        nc.scalar.activation(Vn[:, st, :], PS[:, 2 + st, 0:256], ACT.Identity).then_inc(sems["vn"], 1)
                elif kind == "rs":
                    n = T if i < 6 else CMP_N
                    act_e.wait_ge(sems["stat"], nth("stat", l, i + 1))
                    act_e.wait_ge(sems["rrstd"], nth("rrstd", l, i))
                    nc.scalar.activation(lnb[:, 0:n], PS[:, 6, 0:n], ACT.Ln, bias=eps[:, 0:1]).then_inc(a_ch, 1)
                    act_e.wait_ge(a_ch, a_step())
                    nc.scalar.activation(rrs[:, i % 2, 0:n], lnb[:, 0:n], ACT.Exp, scale=-0.5
                                         ).then_inc(sems["rrstd"], 1)
                elif kind == "gatem":
                    act_e.wait_ge(sems["gatem"], nth("gatem", l, 1))
                    nc.scalar.activation(gates[:, :, :], PS[:, 2, 0:96].rearrange("p (a b) -> p a b", b=24),
                                         ACT.Sigmoid).then_inc(sems["gate"], 1)
                elif kind == "cmph":
                    act_e.wait_ge(sems["tile"], nth("tile", l, T_CMP + 8))
                    for kv in range(2):
                        for hc in range(2):
                            nc.scalar.activation(hid[:, kv, hc, :], PS[:, 2 + 2 * kv + hc, 0:62], ACT.Silu
                                                 ).then_inc(sems["hid"], 1)
                elif kind == "cmpo":
                    act_e.wait_ge(sems["kc"], nth("kc", l, 1))
                    rope_evac(l, 6, PS[:, 2, 0:CMP_N], CMP_N).then_inc(sems["kce"], 1)
                elif kind == "ket":
                    act_e.wait_ge(sems["ket"], nth("ket", l, i + 1))
                    nc.scalar.activation(keT[:, i, :, :], PS[:, 2 + i, :].rearrange("p (a b) -> p a b", b=P),
                                         ACT.Identity).then_inc(sems["kec"], 1)
                elif kind == "state":
                    act_e.wait_ge(sems["osum"], nth("osum", l, i + 1))
                    nc.scalar.activation(mixT[:, 0:4, i * P:(i + 1) * P],
                                         PS[:, 6 + i % 2, :].rearrange("p (a b) -> p a b", b=P),
                                         ACT.Identity).then_inc(sems["oc"], 1)
                elif kind == "hn":
                    if i >= 2:
                        act_e.wait_ge(sems["hst"], nth("hst", l, i - 1))
                    if i == 0:
                        act_e.wait_ge(sems["oc"], nth("oc", l, 4))
                    nc.scalar.activation(sq2[:, i % 2, :], mixT[:, i, :], ACT.Square).then_inc(sems["hsq"], 1)
                    act_e.wait_ge(sems["hst"], nth("hst", l, i + 1))
                    if i >= 1:
                        act_e.wait_ge(sems["hrs"], nth("hrs", l, i))
                    if i >= 2:
                        act_e.wait_ge(sems["hn"], nth("hn", l, i - 1))
                    nc.scalar.activation(lnb[:, :], PS[:, i % 2, :], ACT.Ln, bias=eps[:, 0:1]).then_inc(a_ch, 1)
                    act_e.wait_ge(a_ch, a_step())
                    nc.scalar.activation(rrs[:, i % 2, :], lnb[:, :], ACT.Exp, scale=-0.5).then_inc(sems["hrs"], 1)
                elif kind == "attention":
                    attend(l, NSA)
                elif kind == "ffn":
                    def body(j):
                        for u in range(2):
                            act_e.wait_ge(sems["tile"], l * T_LAYER + j * 4 + (T_FFI + 2 * u + 1 + RING))
                            act_e.wait_ge(sems["act"], l * FFC + j * 2 + (u + 1))
                            nc.scalar.activation(sq2[:, u, :], PS[:, 2 * u, :], ACT.Silu).then_inc(sems["silu"], 1)
                    with act_e.Fori(0, FFC // 2) as j:
                        body(j)

            def step2(kind, i):
                l = DEPTH
                if kind == "norm":
                    norm_rstd(l, *NORMS2[i], **(dict(src=memn, w=MEM, bank=6) if i == 1 else {}))
                elif kind == "trig":
                    act_e.wait_ge(sems["trig"], nth("trig", 0, 1))
                    nc.scalar.activation(tabs[:, :], tabs[:, :], ACT.Sin).then_inc(sems["trigs"], 1)
                elif kind == "lam":
                    act_e.wait_ge(sems["lam"], nth("lam", 0, 1))
                    nc.scalar.activation(small[:, 0:2], small[:, 0:2], ACT.Exp).then_inc(sems["lams"], 1)
                elif kind == "feat":
                    act_e.wait_ge(sems["tile"], nth("tile", l, tile2_of(i) + 1))
                    src = PS[:, i % 2, :]
                    if i < 4:
                        ins = nc.scalar.activation(fq[:, i, :], src, ACT.Identity, scale=0.125)
                    elif i < 8:
                        ins = nc.scalar.activation(fk[:, i - 4, :], src, ACT.Identity)
                    elif i < 16:
                        r = i - 8
                        act_e.wait_ge(sems["rope"], nth("rope", l, max(r - 1, 0)))
                        ins = nc.scalar.activation(qnb[:, r % 2, :], src, ACT.Identity, scale=0.125 if r < 4 else 1.0)
                    elif i < 32:
                        ins = nc.scalar.activation(sga[:, i - 16, :], src, ACT.Sigmoid)
                    elif i < 34:
                        ins = nc.scalar.activation(ckT[:, i - 32, :], src[:, 0:MEM], ACT.Identity)
                    else:
                        ins = nc.scalar.activation(cqT[:, i - 34, :], src, ACT.Identity, scale=0.125)
                    ins.then_inc(sems["evac"], 1)
                elif kind == "flog":
                    act_e.wait_ge(sems["fl"], nth("fl", 0, 1))
                    nc.scalar.activation(lnb[0:8, :], PS[0:8, 6, :], ACT.Identity, bias=par[0:8, M_BF:M_BF + 1]
                                    ).then_inc(a_ch, 1)
                    act_e.wait_ge(a_ch, a_step())
                    nc.scalar.activation(qg[0:8, 0, :], lnb[0:8, :], ACT.Abs).then_inc(a_ch, 1)
                    act_e.wait_ge(a_ch, a_step())
                    nc.scalar.activation(qg[0:8, 0, :], qg[0:8, 0, :], ACT.Exp, scale=-1.0).then_inc(a_ch, 1)
                    act_e.wait_ge(a_ch, a_step())
                    nc.scalar.activation(qg[0:8, 1, :], qg[0:8, 0, :], ACT.Ln, bias=cmask[0:8, 1:2]
                                         ).then_inc(sems["fls"], 1)
                elif kind == "tok":
                    t0, nt, dst, sem = TOK2[i]
                    act_e.wait_ge(sems["tile"], nth("tile", l, t0 + nt))
                    buf = {"fv": fv, "dv": dv, "cv": cvt}[sem]
                    n, w = (4, T) if sem != "cv" else (2, MEM)
                    for st in range(n):
                        nc.scalar.activation(buf[:, st, :], PS[:, 2 + st, 0:w], ACT.Identity).then_inc(sems[sem], 1)
                elif kind == "attention":
                    attend(l, BL2)
                elif kind == "cross":
                    attend(l, CROSS)

            def attend(l, items):
                for s in range(len(items) + 5):
                    last = items[s - LAG_V - 1] if 0 <= s - LAG_V - 1 < len(items) else None
                    if items is BL2 and last and "last" in last:
                        act_e.wait_ge(sems["ms"], nth("ms", 0, last["last"] + 1))
                        nc.scalar.activation(small[:, 4:8], small[:, 4:8], ACT.Ln, scale=1.0 / P,
                                                   bias=eps[:, 1:2]).then_inc(a_ch, 1)
                        act_e.wait_ge(a_ch, a_step())
                        nc.scalar.activation(small[:, 8:12], small[:, 4:8], ACT.Exp, scale=-0.5
                                             ).then_inc(sems["msr"], 1)
                    it = items[s] if s < len(items) else None
                    if it is None or it["kind"] == "mix":
                        continue
                    k = it["k"]
                    act_e.wait_ge(sems["mx"], nth("mx", l, k + 1))
                    if "t3" in it:
                        act_e.wait_ge(sems["tr"], nth("tr", l, it["t3"] + 1))
                    if it["kind"] == "cmp":
                        ins = nc.scalar.activation(Pr[:, k % 3, 0:P], Pr[:, k % 3, 0:P], ACT.Exp)
                    else:
                        n = it["n"]
                        ins = nc.scalar.activation(Pr[:, k % 3, 0:n], PS[:, k % 3, 0:n], ACT.Exp,
                                                   bias=nmx[:, k % 4, 0:1], accum_out=it["L"])
                    ins.then_inc(sems["p"], 1)

            act_e.wait_ge(s_in, 16 * (NIN + 1))
            act_e.wait_ge(s_pre, 2)
            nc.scalar.activation(lb[:, 1, :], lbl[:, 0:4], ACT.Sigmoid).then_inc(s_pre, 1)
            with act_e.Fori(0, DEPTH_RUN) as l:
                ch["n"] = 0
                ch["base"] = l * A_CH
                act_e.wait_ge(sems["params"], nth("params", l, 2))
                for kind, i in STEPS:
                    step(l, kind, i)
                assert ch["n"] == A_CH, ch["n"]
            ch["n"] = 0
            ch["base"] = DEPTH * A_CH
            act_e.wait_ge(sems["h"], nth("h", DEPTH, 0))
            act_e.dma_start(par[:, 0:M_END], par_in).then_inc(sems["b_in"], 16)
            act_e.dma_start(gtmp[:, 0:T].bitcast(I32), pos_in).then_inc(sems["b_in"], 16)
            act_e.dma_start(sel[:, :, :], sel_in).then_inc(sems["b_in"], 16)
            act_e.dma_start(memn[:, :, :], memT_in).then_inc(sems["b_in"], 16)
            act_e.wait_ge(sems["b_in"], 64)
            for kind, i in STEPS2:
                step2(kind, i)

            act_e.wait_ge(sems["h"], nth("h", DEPTH, 16))
            act_e.dma_start(gfin, gfin_in).then_inc(MS["gf"], 16)
            for g in range(16):
                act_e.wait_ge(MS["tr"], g + 1)
                qt, half = g % 8 // 2, g % 2
                dst = (hmt[qt] if g < 8 else xtok[:, qt, :])[:, half * T:half * T + T]
                nc.scalar.activation(dst, PS[:, 4 + g % 4, :], ACT.Identity).then_inc(MS["te"], 1)
                if g < 8 and half:
                    act_e.wait_ge(MS["te"], g + 1)
                    act_e.dma_start(hm_dram[qt * P:qt * P + P, :], hmt[qt]).then_inc(MS["hd"], 16)
            act_e.wait_ge(MS["rq"], 1)
            nc.scalar.activation(rt[:, 0:16], rt[:, 0:16], ACT.Exp).then_inc(MS["rp"], 1)
            act_e.wait_ge(MS["rq"], 2)
            nc.scalar.activation(rt[:, 20:24], rt[:, 20:24], ACT.Exp).then_inc(MS["rp"], 1)

            def xgt_a(i, u):
                act_e.wait_ge(MS["xt"], lin(i, u, 1, 1))
                act_e.wait_ge(MS["gu"], lin(i, u, 1, -1))
                nc.scalar.activation(xgT[u % 2][:, 0:4, :], PS[:, 0, :].rearrange("p (a b) -> p a b", b=P),
                                     ACT.Identity).then_inc(MS["xea"], 1)

            def silu(i, u):
                act_e.wait_ge(MS["gg"], lin(i, u, 1, 1))
                act_e.wait_ge(MS["hm"], lin(i, u, 1, 0))
                nc.scalar.activation(hsilu, PS[:, 2, :], ACT.Silu).then_inc(MS["sl"], 1)

            def ht_copy(i, u):
                act_e.wait_ge(MS["ht"], lin(i, u, 1, 1))
                act_e.wait_ge(MS["dn"], lin(i, u, 2, -2))
                nc.scalar.activation(hT[u % 2], PS[:, 4, :].rearrange("p (a b) -> p a b", b=P), ACT.Identity
                                     ).then_inc(MS["he"], 1)

            def y_a(i, u):
                act_e.wait_ge(MS["dn"], lin(i, u, 2, 1))
                act_e.wait_ge(MS["yd"][(u - 2) % 2], dma_of(i, u - 2))
                nc.scalar.activation(ysb[u % 2][:, 0:T], PS[:, 5, :], ACT.Identity).then_inc(MS["yea"], 1)

            def moe_a(i, u):
                xgt_a(i, u + 1)
                ht_copy(i, u - 1)
                silu(i, u)
                y_a(i, u - 1)

            xgt_a(0, 0)
            xgt_a(0, 1)
            silu(0, 0)
            moe_a(0, 1)
            with act_e.Fori(1, NEXP // 2) as i:
                moe_a(i, 0)
                moe_a(i, 1)
            ht_copy(NEXP // 2 - 1, 1)
            y_a(NEXP // 2 - 1, 1)
            with overflow(act_e):
                i0 = NEXP // 2
                xgt_a(i0, 1)
                silu(i0, 0)
                moe_a(i0, 1)
                with act_e.Fori(i0 + 1, i0 + OVB // 2) as i:
                    moe_a(i, 0)
                    moe_a(i, 1)
                ht_copy(i0 + OVB // 2 - 1, 1)
                y_a(i0 + OVB // 2 - 1, 1)
            for qt in range(QT):
                act_e.wait_ge(MS["fa"], qt + 1)
                nc.scalar.activation(yg[2 * qt + 1], yg[2 * qt], ACT.Square, accum_out=small[:, qt:qt + 1]
                                ).then_inc(a_ch, 1)
                act_e.wait_ge(a_ch, a_step())
                nc.scalar.activation(small[:, 4 + qt:5 + qt], small[:, qt:qt + 1], ACT.Ln, scale=1.0 / D,
                                           bias=eps[:, 0:1]).then_inc(a_ch, 1)
                act_e.wait_ge(a_ch, a_step())
                nc.scalar.activation(small[:, 8 + qt:9 + qt], small[:, 4 + qt:5 + qt], ACT.Exp, scale=-0.5
                                     ).then_inc(MS["fs"], 1)

        @block.vector
        def _(v):
            ch = {"base": 0, "n": 0}

            def v_step():
                ch["n"] += 1
                return ch["base"] + ch["n"]

            def step(l, kind, i):
                if kind == "norm":
                    v.wait_ge(sems["rstd"], nth("rstd", l, i + 1))
                    for c in range(KO):
                        g = (C_MIX if i == 0 else C_FFN) + c
                        nc.vector.scalar_tensor_tensor(out=xn[:, c, :], in0=xT[:, c, :], scalar=lcol[:, g:g + 1],
                                                       in1=rstd[:, :], op0=ALU.mult, op1=ALU.mult
                                                       ).then_inc(sems["xn"], 1)
                elif kind == "gate_h":
                    v.wait_ge(sems["evac"], nth("evac", l, i + 1))
                    nc.vector.tensor_scalar(ftmp[:, i % 2, :], kT[:, i, :], lcol[:, C_LB + 4 + i:C_LB + 5 + i],
                                                  lcol[:, C_LB + i:C_LB + i + 1], ALU.mult, ALU.add).then_inc(v_ch, 1)
                    v.wait_ge(v_ch, v_step())
                    nc.vector.tensor_scalar(kT[:, i, :], ftmp[:, i % 2, :], -1.0, 1.0, ALU.mult, ALU.add
                                            ).then_inc(sems["f"], 1)
                elif kind == "scan":
                    v.wait_ge(sems["ln"], nth("ln", l, i + 1))
                    if i >= 2:
                        v.wait_ge(sems["qk"], nth("qk", l, i - 1))
                    nc.vector.tensor_tensor_scan(bT[:, i, :], cmask[:, :], ftmp[:, i % 2, :], 0.0,
                                                       ALU.mult, ALU.add).then_inc(v_ch, 1)
                    v.wait_ge(v_ch, v_step())
                    bv = bT[:, i, :].rearrange("p (c t) -> p c t", t=P)
                    kv = kdb[:, i % 2, :].rearrange("p (c t) -> p c t", t=P)
                    nc.vector.tensor_tensor(kv, bv[:, :, P - 1:P].broadcast_to([P, 4, P]), bv, ALU.subtract
                                            ).then_inc(sems["kd"], 1)
                elif kind == "decay":
                    if i >= 1:
                        v.wait_ge(sems["gram"], nth("gram", l, 4 * i))
                    for j in range(LEVELS):
                        w = 64 >> j
                        e = E[:, j, :].rearrange("p (n two w) -> p n two w", two=2, w=w)
                        bv = bT[:, i, :].rearrange("p (n two w) -> p n two w", two=2, w=w)
                        ref = bv[:, :, 0, w - 1:w].broadcast_to([P, T // (2 * w), w])
                        nc.vector.tensor_tensor(e[:, :, 0, :], ref, bv[:, :, 0, :], ALU.subtract)
                        ins = nc.vector.tensor_tensor(e[:, :, 1, :], bv[:, :, 1, :], ref, ALU.subtract)
                    ins.then_inc(sems["ediff"], 1)
                elif kind == "gram":
                    for c in range(4):
                        n = 4 * i + c
                        v.wait_ge(sems["gram"], nth("gram", l, n + 1))
                        b = 2 + 2 * (n % 2)
                        nc.vector.tensor_tensor(gtmp[:, :], PS[:, b:b + 2, :].rearrange("p a b -> p (a b)"),
                                                      gmask[:, :, :].rearrange("p a b -> p (a b)"), ALU.mult
                                                      ).then_inc(v_ch, 1)
                        v.wait_ge(v_ch, v_step())
                        nc.vector.tensor_reduce(AT[:, n, :], gtmp[:, :].rearrange("p (l t) -> p t l", t=P),
                                                AX.X, ALU.add).then_inc(sems["at"], 1)
                        v.wait_ge(sems["at"], nth("at", l, n + 1))
                elif kind == "qk":
                    v.wait_ge(sems["kqexp"], nth("kqexp", l, i + 1))
                    v.wait_ge(sems["e"], nth("e", l, i + 1))
                    v.wait_ge(sems["gram"], nth("gram", l, 4 * i + 4))
                    nc.vector.tensor_copy(ebl[:, i, :], ebuf[:, i % 2, :].rearrange("p (c t) -> p c t", t=P)[:, :, P - 1])
                    nc.vector.tensor_tensor(qT[:, i, :], qT[:, i, :], ebuf[:, i % 2, :], ALU.mult)
                    nc.vector.tensor_tensor(kT[:, i, :], kT[:, i, :], kdb[:, i % 2, :], ALU.mult
                                            ).then_inc(sems["qk"], 1)
                elif kind == "rs":
                    n = T if i < 6 else CMP_N
                    v.wait_ge(sems["rrstd"], nth("rrstd", l, i + 1))
                    if i >= 2:
                        v.wait_ge(sems["rope"], nth("rope", l, i - 1))
                    nc.vector.tensor_tensor(qnb[:, i % 2, 0:n], qg[:, i % 2, 0:n], rrs[:, i % 2, 0:n], ALU.mult
                                            ).then_inc(sems["qn"], 1)
                elif kind == "rr":
                    n = T if i < 6 else CMP_N
                    cs, sn = (cos, sin) if i < 6 else (cos[:, 31::16], sin[:, 31::16])
                    dst = qr[:, i, :] if i < 4 else kr[:, i - 4, :] if i < 6 else kcr[:, 0:CMP_N]
                    v.wait_ge(sems["rot"], nth("rot", l, i + 1))

                    if i == 6:
                        v.wait_ge(sems["dbuild"], nth("dbuild", l, 2))
                    nc.vector.tensor_tensor(gtmp[:, 0:n], PS[:, 7, 0:n], sn, ALU.mult)
                    nc.vector.tensor_tensor(gtmp[:, T:T + n], qnb[:, i % 2, 0:n], cs, ALU.mult).then_inc(v_ch, 1)
                    v.wait_ge(v_ch, v_step())
                    nc.vector.tensor_tensor(dst, gtmp[:, 0:n], gtmp[:, T:T + n], ALU.add).then_inc(sems["rope"], 1)
                    v.wait_ge(sems["rope"], nth("rope", l, i + 1))
                elif kind == "dbuild":
                    v.wait_ge(sems["evac"], nth("evac", l, 19 + i))
                    for part in range(2):
                        for g in range(2):
                            for hf in range(2):
                                src = craw[64 * g:64 * g + 64, i, :].rearrange("p (s j two) -> p s j two", j=8, two=2)
                                pc = C_PE + 32 * i + 16 * hf + 8 * part
                                pe = lcol[64 * g:64 * g + 64, pc:pc + 8].unsqueeze(1).broadcast_to([64, 32, 8])
                                dst = DB[64 * hf:64 * hf + 64, i, part, g, :].rearrange("p (s j) -> p s j", j=8)
                                ins = nc.vector.tensor_tensor(dst, src[:, :, :, hf], pe, ALU.add)
                    ins.then_inc(sems["dbuild"], 1)
                elif kind == "cmpo":
                    v.wait_ge(sems["vc"], nth("vc", l, 1))
                    for j in range(4):
                        ins = nc.vector.tensor_copy(VC[32 * j:32 * j + CMP_N, :, j, :],
                                                    PS[32 * j:32 * j + CMP_N, 3, 0:P].rearrange("p (g d) -> p g d", d=64))
                    ins.then_inc(sems["vcc"], 1)
                elif kind == "vczero":
                    v.wait_ge(sems["evac"], nth("evac", l, 12))
                    nc.vector.memset(VC[:, :, :, :], 0.0).then_inc(v_ch, 1)
                    v.wait_ge(v_ch, v_step())
                elif kind == "state":
                    if i < 3:
                        v.wait_ge(sems["ds"], nth("ds", l, i + 1))
                        if i:
                            v.wait_ge(sems["osum"], nth("osum", l, i + 1))
                        for h in range(4):
                            d = PS[:, 5, P * h:P * h + P]
                            if i == 0:
                                ins = nc.vector.tensor_copy(Sst[:, h, :], d)
                            else:
                                ins = nc.vector.scalar_tensor_tensor(out=Sst[:, h, :], in0=Sst[:, h, :],
                                                                     scalar=ebl[:, h, i:i + 1], in1=d,
                                                                     op0=ALU.mult, op1=ALU.add)
                        ins.then_inc(sems["s"], 1)
                        v.wait_ge(sems["s"], l * 3 + (i + 1))
                elif kind == "hn":
                    v.wait_ge(sems["hrs"], nth("hrs", l, i + 1))
                    nc.vector.scalar_tensor_tensor(out=mixT[:, i, :], in0=mixT[:, i, :],
                                                         scalar=lcol[:, C_GN:C_GN + 1], in1=rrs[:, i % 2, :],
                                                         op0=ALU.mult, op1=ALU.mult).then_inc(v_ch, 1)
                    v.wait_ge(v_ch, v_step())
                    nc.vector.tensor_tensor(mixT[:, i, :], mixT[:, i, :], sgT[:, i, :], ALU.mult
                                            ).then_inc(sems["hn"], 1)
                elif kind == "attention":
                    attend(l, NSA, nsa_combine)
                elif kind == "wout":
                    residual(l, 0, T_WO + 8)
                elif kind == "ffn":
                    with v.Fori(0, FFC // 2) as j:
                        for u in range(2):
                            v.wait_ge(sems["silu"], l * FFC + j * 2 + (u + 1))
                            v.wait_ge(sems["tile"], l * T_LAYER + j * 4 + (T_FFI + 2 * u + 2 + RING))
                            nc.vector.tensor_tensor(act[:, j * 2 + u, :], sq2[:, u, :], PS[:, 2 * u + 1, :], ALU.mult
                                                    ).then_inc(sems["act"], 1)
                    residual(l, 1, T_FFO + FFC)

            def step2(kind, i):
                l = DEPTH
                if kind == "norm":
                    n = NORMS2[i][0]
                    v.wait_ge(sems["rstd"], nth("rstd", l, n + 1))
                    for c in range(KO):
                        g = (M_MIX, M_MEM, M_CROSS, M_FFN)[i] + c
                        buf, src, w = (memn, memn, MEM) if i == 1 else (xn, xT, T)
                        nc.vector.scalar_tensor_tensor(out=buf[:, c, :], in0=src[:, c, :], scalar=par[:, g:g + 1],
                                                       in1=rstd[:, 0:w], op0=ALU.mult, op1=ALU.mult
                                                       ).then_inc(sems["xn"], 1)
                elif kind == "trig":
                    ang, kf = gtmp[:, 0:T], gtmp[:, T:2 * T]
                    nc.vector.tensor_copy(kf, ang.bitcast(I32)).then_inc(v_ch, 1)
                    v.wait_ge(v_ch, v_step())
                    nc.vector.tensor_scalar(ang, kf, par[:, M_FREQ:M_FREQ + 1], None, ALU.mult).then_inc(v_ch, 1)
                    v.wait_ge(v_ch, v_step())
                    c1 = 6.28125
                    c2 = float(np.float32(np.round((TWO_PI - c1) * 2 ** 21) / 2 ** 21))
                    c3 = float(np.float32(TWO_PI - c1 - c2))
                    magic = 12582912.0
                    for shift, dst in ((0.25, cos), (0.0, sin)):
                        nc.vector.tensor_scalar(kf, ang, 1 / TWO_PI, shift, ALU.mult, ALU.add).then_inc(v_ch, 1)
                        v.wait_ge(v_ch, v_step())
                        nc.vector.tensor_scalar(kf, kf, magic, None, ALU.add).then_inc(v_ch, 1)
                        v.wait_ge(v_ch, v_step())
                        nc.vector.tensor_scalar(kf, kf, -magic, None, ALU.add).then_inc(v_ch, 1)
                        v.wait_ge(v_ch, v_step())
                        nc.vector.scalar_tensor_tensor(out=dst, in0=kf, scalar=-c1, in1=ang,
                                                             op0=ALU.mult, op1=ALU.add).then_inc(v_ch, 1)
                        v.wait_ge(v_ch, v_step())
                        nc.vector.scalar_tensor_tensor(out=dst, in0=kf, scalar=-c2, in1=dst,
                                                             op0=ALU.mult, op1=ALU.add).then_inc(v_ch, 1)
                        v.wait_ge(v_ch, v_step())
                        nc.vector.scalar_tensor_tensor(out=dst, in0=kf, scalar=-c3, in1=dst,
                                                             op0=ALU.mult, op1=ALU.add).then_inc(v_ch, 1)
                        v.wait_ge(v_ch, v_step())
                        if shift:
                            nc.vector.tensor_scalar(dst, dst, TWO_PI / 4, None, ALU.add).then_inc(v_ch, 1)
                            v.wait_ge(v_ch, v_step())
                    nc.vector.tensor_scalar(tabs[:, :], tabs[:, :], 3.1415925, -3.1415925, ALU.min, ALU.max
                                            ).then_inc(sems["trig"], 1)
                    v.wait_ge(sems["trig"], 1)
                elif kind == "lam":
                    la = [par[:, M_LAM + 64 * j:M_LAM + 64 * j + 64] for j in range(4)]
                    nc.vector.tensor_tensor(lnl[:, 0, :], la[0], la[1], ALU.mult)
                    nc.vector.tensor_tensor(lnl[:, 1, :], la[2], la[3], ALU.mult).then_inc(v_ch, 1)
                    v.wait_ge(v_ch, v_step())
                    nc.vector.tensor_reduce(small[:, 0:2], lnl[:, :, :], AX.X, ALU.add).then_inc(sems["lam"], 1)
                    v.wait_ge(sems["lams"], nth("lams", 0, 1))
                    nc.vector.tensor_tensor(small[:, 2:3], small[:, 0:1], small[:, 1:2], ALU.subtract).then_inc(v_ch, 1)
                    v.wait_ge(v_ch, v_step())
                    nc.vector.tensor_scalar(small[:, 3:4], small[:, 2:3], 0.8 - 0.6, None, ALU.add).then_inc(v_ch, 1)
                    v.wait_ge(v_ch, v_step())
                elif kind == "flog":
                    nc.vector.memset(negc, 0.0).then_inc(v_ch, 1)
                    v.wait_ge(v_ch, v_step())
                    for c in range(4):
                        nc.vector.memset(cmask[:, c * P:c * P + 1], 1.0).then_inc(v_ch, 1)
                        v.wait_ge(v_ch, v_step())
                    v.wait_ge(sems["fls"], nth("fls", 0, 1))
                    nc.vector.tensor_scalar(lnb[0:8, :], lnb[0:8, :], 0.0, None, ALU.min).then_inc(v_ch, 1)
                    v.wait_ge(v_ch, v_step())
                    nc.vector.tensor_tensor(lnb[0:8, :], lnb[0:8, :], qg[0:8, 1, :], ALU.subtract).then_inc(v_ch, 1)
                    v.wait_ge(v_ch, v_step())
                    nc.vector.tensor_tensor_scan(qg[0:8, 0, :], cmask[0:8, :], lnb[0:8, :], 0.0,
                                                       ALU.mult, ALU.add).then_inc(v_ch, 1)
                    v.wait_ge(v_ch, v_step())
                    nc.vector.tensor_scalar(negc[0:8, :], qg[0:8, 0, :], -1.0, None, ALU.mult).then_inc(sems["nck"], 1)
                    v.wait_ge(sems["nck"], 1)
                elif kind == "rr":
                    v.wait_ge(sems["rot"], nth("rot", l, i + 1))
                    if i == 0:
                        v.wait_ge(sems["trigs"], nth("trigs", 0, 1))
                    dst = dq[:, i, :] if i < 4 else dk[:, i - 4, :]
                    nc.vector.tensor_tensor(gtmp[:, 0:T], PS[:, 7, :], sin, ALU.mult)
                    nc.vector.tensor_tensor(gtmp[:, T:2 * T], qnb[:, i % 2, :], cos, ALU.mult).then_inc(v_ch, 1)
                    v.wait_ge(v_ch, v_step())
                    nc.vector.tensor_tensor(dst, gtmp[:, 0:T], gtmp[:, T:2 * T], ALU.add).then_inc(sems["rope"], 1)
                    v.wait_ge(sems["rope"], nth("rope", l, i + 1))
                elif kind == "attention":
                    attend(l, BL2, block2_combine)
                elif kind == "cross":
                    attend(l, CROSS, cross_combine)
                elif kind == "merge":
                    for c in range(8):
                        v.wait_ge(sems["tile"], nth("tile", l, B_AB + c + 1))
                        v.wait_ge(sems["evac"], nth("evac", l, 32))
                        b = 2 * (c % 2)
                        nc.vector.tensor_tensor(gtmp[:, 0:T], sga[:, c, :], PS[:, b, :], ALU.mult)
                        nc.vector.tensor_tensor(gtmp[:, T:2 * T], sga[:, 8 + c, :], PS[:, b + 1, :], ALU.mult
                                        ).then_inc(v_ch, 1)
                        v.wait_ge(v_ch, v_step())
                        nc.vector.tensor_tensor(merged[:, c, :], gtmp[:, 0:T], gtmp[:, T:2 * T], ALU.add
                                                ).then_inc(sems["mrg"], 1)
                        v.wait_ge(sems["mrg"], c + 1)
                elif kind == "kouter":
                    residual(l, i, (B_WO + 8, B_CO + 2)[i])

            def by_head(x, d):
                return x.rearrange("p (h d) -> p h d", d=d)

            def block2_combine(l, qt):
                nc.vector.reciprocal(Rc[:, 0:16], Lt[:, qt % 2, 0:16]).then_inc(v_ch, 1)
                v.wait_ge(v_ch, v_step())
                nc.vector.tensor_scalar(Rc[:, 12:16], Rc[:, 12:16], small[:, 3:4], None, ALU.mult).then_inc(v_ch, 1)
                v.wait_ge(v_ch, v_step())
                nc.vector.tensor_tensor(by_head(ftmp[:, 0, :], 64), by_head(PS[:, 5, :], 64),
                                              Rc[:, 0:8].unsqueeze(2).broadcast_to([P, 8, 64]), ALU.mult
                                              ).then_inc(v_ch, 1)
                v.wait_ge(v_ch, v_step())
                nc.vector.sem_inc(sems["mixtok"], 1)
                for c in range(2):
                    ins = nc.vector.tensor_tensor(by_head(oa[:, c, :], P), by_head(PS[:, 6 + c, :], P),
                                                  Rc[:, 8 + 4 * c:12 + 4 * c].unsqueeze(2).broadcast_to([P, 4, P]),
                                                  ALU.mult)
                ins.then_inc(sems["ofree"], 1)
                v.wait_ge(sems["ofree"], nth("ofree", l, qt + 1))
                nc.vector.tensor_tensor(oa[:, 0, :], oa[:, 0, :], oa[:, 1, :], ALU.subtract).then_inc(v_ch, 1)
                v.wait_ge(v_ch, v_step())
                nc.vector.tensor_tensor(oa[:, 1, :], oa[:, 0, :], oa[:, 0, :], ALU.mult).then_inc(v_ch, 1)
                v.wait_ge(v_ch, v_step())
                nc.vector.tensor_reduce(small[:, 4:8], by_head(oa[:, 1, :], P), AX.X, ALU.add).then_inc(sems["ms"], 1)

            def block2_rest(l, qt):
                v.wait_ge(sems["msr"], nth("msr", 0, qt + 1))
                nc.vector.tensor_tensor(by_head(ftmp[:, 1, :], P), by_head(oa[:, 0, :], P),
                                        small[:, 8:12].unsqueeze(2).broadcast_to([P, 4, P]), ALU.mult
                                        ).then_inc(sems["mixtok"], 1)
                v.wait_ge(sems["mixtok"], nth("mixtok", l, 2 * qt + 2))

            def cross_combine(l, qt):
                nc.vector.reciprocal(Rc[:, 0:4], Lt[:, qt % 2, 0:4]).then_inc(v_ch, 1)
                v.wait_ge(v_ch, v_step())
                nc.vector.tensor_tensor(by_head(ftmp[:, 0, 0:256], 64), by_head(PS[:, 5, 0:256], 64),
                                              Rc[:, 0:4].unsqueeze(2).broadcast_to([P, 4, 64]), ALU.mult
                                              ).then_inc(v_ch, 1)
                v.wait_ge(v_ch, v_step())
                nc.vector.sem_inc(sems["mixtok"], 1)
                nc.vector.sem_inc(sems["ofree"], 1)

            def residual(l, n, last_tile):
                for c in range(KO):
                    if c < 7:
                        v.wait_ge(sems["res"], nth("res", l, 7 * n + c + 1))
                    else:
                        v.wait_ge(sems["tile"], nth("tile", l, last_tile))
                    nc.vector.tensor_tensor(xT[:, c, :], xT[:, c, :], PS[:, c, :], ALU.add).then_inc(sems["h"], 1)

            def nsa_combine(l, qt):
                if qt:
                    v.wait_ge(sems["mixtok"], nth("mixtok", l, qt))
                nc.vector.reciprocal(Rc[:, :], Lt[:, qt % 2, :]).then_inc(v_ch, 1)
                v.wait_ge(v_ch, v_step())
                nc.vector.tensor_tensor(Rc[:, :].rearrange("p (b h) -> p b h", b=3),
                                              Rc[:, :].rearrange("p (b h) -> p b h", b=3),
                                              gates[:, qt, :].rearrange("p (h b) -> p b h", b=3), ALU.mult
                                              ).then_inc(v_ch, 1)
                v.wait_ge(v_ch, v_step())
                if qt == 0:
                    nc.vector.tensor_scalar(Rc[:, 0:8], Rc[:, 0:8], valid0, None, ALU.mult).then_inc(v_ch, 1)
                    v.wait_ge(v_ch, v_step())

                def r(b):
                    return Rc[:, 8 * b:8 * b + 8].unsqueeze(2).broadcast_to([P, 8, 64])

                def o(bank):
                    return PS[:, bank, :].rearrange("p (h d) -> p h d", d=64)

                def w(x):
                    return x.rearrange("p (h d) -> p h d", d=64)

                nc.vector.tensor_tensor(w(oa[:, 0, :]), o(5), r(1), ALU.mult)
                nc.vector.tensor_tensor(w(oa[:, 1, :]), o(6), r(2), ALU.mult).then_inc(v_ch, 1)
                v.wait_ge(v_ch, v_step())
                nc.vector.tensor_tensor(oa[:, 0, :], oa[:, 0, :], oa[:, 1, :], ALU.add).then_inc(v_ch, 1)
                v.wait_ge(v_ch, v_step())
                ins = nc.vector.tensor_tensor(w(oa[:, 1, :]), o(7), r(0), ALU.mult)
                ins.then_inc(sems["ofree"], 1)
                v.wait_ge(sems["ofree"], l * 4 + (qt + 1))
                nc.vector.tensor_tensor(mixtok, oa[:, 0, :], oa[:, 1, :], ALU.add).then_inc(sems["mixtok"], 1)

            def attend(l, items, combine):
                for s in range(len(items) + LAG_V):
                    it = items[s] if s < len(items) else None
                    if it and it["kind"] != "mix":
                        k = it["k"]
                        v.wait_ge(sems["sc"], nth("sc", l, k + 1))
                        if k >= 4:
                            v.wait_ge(sems["mx"], nth("mx", l, k - 3))
                        if it["kind"] == "cmp":
                            if "t3" in it:
                                v.wait_ge(sems["tr"], nth("tr", l, it["t3"] + 1))
                            scores = PS[:, k % 3, 0:P].rearrange("p (h n) -> p h n", n=32)
                            nc.vector.tensor_reduce(nmx[:, k % 4, :], scores, AX.X, ALU.max).then_inc(v_ch, 1)
                            v.wait_ge(v_ch, v_step())
                            nc.vector.tensor_tensor(
                                Pr[:, k % 3, 0:P].rearrange("p (h n) -> p h n", n=32), scores,
                                nmx[:, k % 4, :].unsqueeze(2).broadcast_to([P, 4, 32]), ALU.subtract
                            ).then_inc(sems["mx"], 1)
                        else:
                            nc.vector.tensor_reduce(nmx[:, k % 4, 0:1], PS[:, k % 3, 0:it["n"]], AX.X, ALU.max,
                                                    negate=True).then_inc(sems["mx"], 1)
                    it = items[s - LAG_T] if 0 <= s - LAG_T < len(items) else None
                    if it:
                        t = it["t"]
                        v.wait_ge(sems["tr"], nth("tr", l, t + 1))
                        if "pv2" in it:
                            v.wait_ge(sems["pv"], nth("pv", l, it["pv2"] + 1))
                        n = it["nb"] * P
                        if it["kind"] == "mix":
                            src = PS[:, 3 + t % 2, 0:n].rearrange("p (a b) -> p a b", b=P)
                            if "sub" in it:
                                ins = nc.vector.tensor_scalar(it["dst"], src, par[:, M_SUB:M_SUB + 1], 0.8,
                                                              ALU.mult, ALU.mult)
                            else:
                                ins = nc.vector.tensor_copy(it["dst"], src)
                        else:
                            if it["kind"] == "cmp":
                                nc.vector.tensor_reduce(it["L"], Pr[:, it["k"] % 3, 0:P].rearrange(
                                    "p (h n) -> p h n", n=32), AX.X, ALU.add)
                            ins = nc.vector.tensor_copy(PTs[:, t % 2, 0:n], PS[:, 3 + t % 2, 0:n])
                        ins.then_inc(sems["pt"], 1)
                    it = items[s - LAG_V] if 0 <= s - LAG_V < len(items) else None
                    if it and "last" in it:
                        v.wait_ge(sems["pv"], nth("pv", l, it["k"] + 1))
                        if it["t"] >= 0:
                            v.wait_ge(sems["pt"], nth("pt", l, it["t"] + 1))
                        combine(l, it["last"])
                    it = items[s - LAG_V - 2] if 0 <= s - LAG_V - 2 < len(items) else None
                    if items is BL2 and it and "last" in it:
                        block2_rest(l, it["last"])

            nc.vector.memset(cmask[:, :], 1.0).then_inc(s_pre, 1)
            v.wait_ge(s_pre, 1)
            for c in range(4):
                nc.vector.memset(cmask[:, c * P:c * P + 1], 0.0)
            nc.vector.memset(eps[:, 0:1], 1e-6)
            nc.vector.memset(eps[:, 1:2], 1e-5)
            nc.vector.memset(kcr[:, :], 0.0)
            nc.vector.memset(lb[:, 0, :], 0.0)
            v.wait_ge(s_in, 16 * (NIN + 1))
            nc.vector.tensor_tensor(lbl[:, 0:4], cols[:, 1, C_LB:C_LB + 4], cols[:, 0, C_LB:C_LB + 4], ALU.subtract
                                    ).then_inc(s_pre, 1)
            v.wait_ge(s_pre, 3)
            nc.vector.tensor_copy(cols[:, :, C_LB:C_LB + 4], lb[:, :, :])
            nc.vector.tensor_scalar(cols[:, :, C_LB + 4:C_LB + 8], lb[:, :, :], -1.0, 1.0, ALU.mult, ALU.add)
            nc.vector.tensor_scalar(cols[:, :, C_QG:C_QG + 1], cols[:, :, C_QG:C_QG + 1], 0.125, None, ALU.mult
                                    ).then_inc(s_pre, 1)
            v.wait_ge(s_pre, 4)
            v.sem_inc(sems["tile"], RING)
            v.sem_inc(sems["evac"], 2)
            v.sem_inc(sems["rrstd"], 1)
            v.sem_inc(sems["rope"], 1)
            v.sem_inc(sems["h"], 8)
            v.sem_inc(sems["act"], 2)
            with v.Fori(0, DEPTH_RUN) as l:
                ch["n"] = 0
                ch["base"] = l * V_CH
                nc.vector.tensor_copy(lcol[:, :], cols[:, l, :]).then_inc(sems["params"], 1)
                nc.vector.tensor_copy(misc[:, :], misc_all[:, l, :]).then_inc(sems["params"], 1)
                v.wait_ge(sems["params"], nth("params", l, 2))
                for kind, i in STEPS:
                    step(l, kind, i)
                assert ch["n"] == V_CH, ch["n"]
            ch["n"] = 0
            ch["base"] = DEPTH * V_CH
            v.wait_ge(sems["b_in"], 64)
            for kind, i in STEPS2:
                step2(kind, i)

            tt, ts, red = nc.vector.tensor_tensor, nc.vector.tensor_scalar, nc.vector.tensor_reduce
            E_ = par[:, M_E:M_E + NEXP]

            def over(x, shape):
                return (x.unsqueeze(2) if x.shape[1] == shape[0] and shape[0] != shape[1] else x.unsqueeze(1)
                        ).broadcast_to([P, *shape])

            gm, gs, prm, v1, v2, dd = (rt[:, 16 + 4 * j:20 + 4 * j] for j in (0, 2, 3, 4, 5, 1))
            e1 = dd
            desc = rt[:, 48:80]
            cnt, ovc, incl, ovs, addr = (rt[:, 80 + 32 * j:112 + 32 * j] for j in range(5))
            g4 = lg[:, :, 0:4]
            v.wait_ge(MS["lg"], 1)
            tt(lg[:, :, :], PS[:, 0, 0:144].rearrange("p (q e) -> p q e", e=36),
                     over(par[:, M_BGE:M_BGE + 36], (QT, 36)), ALU.add).then_inc(v_ch, 1)
            v.wait_ge(v_ch, v_step())
            red(gm, g4, AX.X, ALU.max).then_inc(v_ch, 1)
            v.wait_ge(v_ch, v_step())
            ge = rt[:, 0:16].rearrange("p (q g) -> p q g", g=4)
            tt(ge, g4, gm.unsqueeze(2).broadcast_to([P, 4, 4]), ALU.subtract).then_inc(MS["rq"], 1)
            goh = tmpe[:, 0, 0:16].rearrange("p (q g) -> p q g", g=4)
            pri = tmpe[:, 0, 16:32].rearrange("p (q g) -> p q g", g=4)
            ts(desc, E_, -1.0, 32.0, ALU.mult, ALU.add).then_inc(v_ch, 1)
            v.wait_ge(v_ch, v_step())
            tt(pri, g4, gm.unsqueeze(2).broadcast_to([P, 4, 4]), ALU.is_equal).then_inc(v_ch, 1)
            v.wait_ge(v_ch, v_step())
            tt(pri, pri, desc[:, 0:4].unsqueeze(1).broadcast_to([P, 4, 4]), ALU.mult).then_inc(v_ch, 1)
            v.wait_ge(v_ch, v_step())
            red(prm, pri, AX.X, ALU.max).then_inc(v_ch, 1)
            v.wait_ge(v_ch, v_step())
            tt(goh, pri, prm.unsqueeze(2).broadcast_to([P, 4, 4]), ALU.is_equal).then_inc(v_ch, 1)
            v.wait_ge(v_ch, v_step())
            ts(goh, goh, -1.0, 1e30, ALU.add, ALU.mult).then_inc(v_ch, 1)
            v.wait_ge(v_ch, v_step())
            for qt in range(QT):
                ins = tt(em[:, qt, :].rearrange("p (g e) -> p g e", e=8), lg[:, qt, 4:36].rearrange(
                    "p (g e) -> p g e", e=8), goh[:, qt, :].unsqueeze(2).broadcast_to([P, 4, 8]), ALU.add)
            ins.then_inc(v_ch, 1)
            v.wait_ge(v_ch, v_step())

            def bc(x):
                return x.unsqueeze(2).broadcast_to([P, QT, NEXP])

            def row(x):
                return x.unsqueeze(1).broadcast_to([P, QT, NEXP])

            def first_best(vmax, oh):
                red(vmax, em[:, :, :], AX.X, ALU.max).then_inc(v_ch, 1)
                v.wait_ge(v_ch, v_step())
                tt(tmpe[:, :, :], em[:, :, :], bc(vmax), ALU.is_equal).then_inc(v_ch, 1)
                v.wait_ge(v_ch, v_step())
                tt(tmpe[:, :, :], tmpe[:, :, :], row(desc), ALU.mult).then_inc(v_ch, 1)
                v.wait_ge(v_ch, v_step())
                red(prm, tmpe[:, :, :], AX.X, ALU.max).then_inc(v_ch, 1)
                v.wait_ge(v_ch, v_step())
                tt(oh[:, :, :], tmpe[:, :, :], bc(prm), ALU.is_equal).then_inc(v_ch, 1)
                v.wait_ge(v_ch, v_step())

            first_best(v1, oh1)
            nc.vector.scalar_tensor_tensor(out=em[:, :, :], in0=oh1[:, :, :], scalar=-2e30, in1=em[:, :, :],
                                                 op0=ALU.mult, op1=ALU.add).then_inc(v_ch, 1)
            v.wait_ge(v_ch, v_step())
            first_best(v2, oh2)
            tt(Ab[:, :, :], oh1[:, :, :], oh2[:, :, :], ALU.add).then_inc(MS["A"], 1)
            tt(dd, v2, v1, ALU.subtract).then_inc(MS["rq"], 1)
            v.wait_ge(MS["rp"], 2)
            red(gs, ge, AX.X, ALU.add).then_inc(v_ch, 1)
            v.wait_ge(v_ch, v_step())
            nc.vector.reciprocal(gs, gs).then_inc(v_ch, 1)
            v.wait_ge(v_ch, v_step())
            ts(prm, e1, 1.0, None, ALU.add).then_inc(v_ch, 1)
            v.wait_ge(v_ch, v_step())
            nc.vector.reciprocal(prm, prm).then_inc(v_ch, 1)
            v.wait_ge(v_ch, v_step())
            tt(wts[:, 0, :], prm, gs, ALU.mult).then_inc(v_ch, 1)
            v.wait_ge(v_ch, v_step())
            tt(wts[:, 1, :], wts[:, 0, :], e1, ALU.mult).then_inc(v_ch, 1)
            v.wait_ge(v_ch, v_step())
            v.wait_ge(MS["rk"], 1)
            ps_rank = PS[:, 1, 0:128].rearrange("p (q e) -> p q e", e=NEXP)
            nc.vector.tensor_copy(cnt, PS[:, 1, 128:160]).then_inc(v_ch, 1)
            v.wait_ge(v_ch, v_step())
            ts(ovc, cnt, 128.5, None, ALU.is_ge).then_inc(v_ch, 1)
            v.wait_ge(v_ch, v_step())
            for lim in (256.5, 384.5):
                ts(ovs, cnt, lim, None, ALU.is_ge).then_inc(v_ch, 1)
                v.wait_ge(v_ch, v_step())
                tt(ovc, ovc, ovs, ALU.add).then_inc(v_ch, 1)
                v.wait_ge(v_ch, v_step())
            nc.vector.memset(addr, 1.0).then_inc(v_ch, 1)
            v.wait_ge(v_ch, v_step())
            nc.vector.tensor_tensor_scan(incl, addr, ovc, 0.0, ALU.mult, ALU.add).then_inc(v_ch, 1)
            v.wait_ge(v_ch, v_step())
            tt(ovs, incl, ovc, ALU.subtract).then_inc(v_ch, 1)
            v.wait_ge(v_ch, v_step())
            tt(addr, ovs, E_, ALU.subtract).then_inc(v_ch, 1)
            v.wait_ge(v_ch, v_step())
            ts(addr, addr, float(NEXP - 1), float(P), ALU.add, ALU.mult).then_inc(v_ch, 1)
            v.wait_ge(v_ch, v_step())
            ts(tmpe[:, :, :], ps_rank, float(P) - 0.5, None, ALU.is_ge).then_inc(v_ch, 1)
            v.wait_ge(v_ch, v_step())
            tt(tmpe[:, :, :], tmpe[:, :, :], row(addr), ALU.mult).then_inc(v_ch, 1)
            v.wait_ge(v_ch, v_step())
            tt(rnk[:, :, :], tmpe[:, :, :], ps_rank, ALU.add).then_inc(v_ch, 1)
            v.wait_ge(v_ch, v_step())
            ts(addr, E_, float(P), None, ALU.mult).then_inc(v_ch, 1)
            v.wait_ge(v_ch, v_step())
            tt(rnk[:, :, :], rnk[:, :, :], row(addr), ALU.add).then_inc(v_ch, 1)
            v.wait_ge(v_ch, v_step())
            for k, oh in enumerate((oh1, oh2)):
                tt(tmpe[:, :, :], rnk[:, :, :], oh[:, :, :], ALU.mult).then_inc(v_ch, 1)
                v.wait_ge(v_ch, v_step())
                red(pos[:, k, :], tmpe[:, :, :], AX.X, ALU.add).then_inc(v_ch, 1)
                v.wait_ge(v_ch, v_step())
            nc.vector.tensor_copy(posi[:, :], pos[:, :, :].rearrange("p k q -> p (k q)"))
            nc.vector.tensor_copy(prel[:, :, :], pos[:, :, :]).then_inc(v_ch, 1)
            v.wait_ge(v_ch, v_step())
            j8 = gtmp[:, 0:256].rearrange("p (j e) -> p j e", e=NEXP)
            j8b = gtmp[:, 256:512].rearrange("p (j e) -> p j e", e=NEXP)
            jj = E_[:, 0:8].unsqueeze(2).broadcast_to([P, 8, NEXP])

            def er(x):
                return x.unsqueeze(1).broadcast_to([P, 8, NEXP])

            tt(j8, jj, er(ovs), ALU.is_ge).then_inc(v_ch, 1)
            v.wait_ge(v_ch, v_step())
            tt(j8b, jj, er(incl), ALU.is_lt).then_inc(v_ch, 1)
            v.wait_ge(v_ch, v_step())
            tt(j8, j8, j8b, ALU.mult).then_inc(v_ch, 1)
            v.wait_ge(v_ch, v_step())
            tt(j8, j8, er(E_), ALU.mult).then_inc(v_ch, 1)
            v.wait_ge(v_ch, v_step())
            red(small[:, 0:8], j8, AX.X, ALU.add).then_inc(v_ch, 1)
            v.wait_ge(v_ch, v_step())
            nc.vector.tensor_copy(ovi[:, 0:8], small[:, 0:8]).then_inc(v_ch, 1)
            v.wait_ge(v_ch, v_step())
            nc.vector.tensor_copy(ovi[:, 8:9], incl[:, 31:32]).then_inc(MS["ro"], 1)

            iota = par[:, M_IOTA:M_IOTA + P]

            def onehot(i, u):
                v.wait_ge(MS["ix"], lin(i, u, 1, -1))
                v.wait_ge(MS["od"], lin(i, u, 1, 0))
                for qt in range(QT):
                    ins = ts(Ob[u % 2][:, qt, :], iota, prel[:, 0, qt:qt + 1], None, ALU.is_equal)
                ins.then_inc(MS["odh"], 1)
                v.wait_ge(MS["odh"], lin(i, u, 2, 1))
                for qt in range(QT):
                    ins = nc.vector.scalar_tensor_tensor(out=Ob[u % 2][:, qt, :], in0=iota,
                                                         scalar=prel[:, 1, qt:qt + 1], in1=Ob[u % 2][:, qt, :],
                                                         op0=ALU.is_equal, op1=ALU.add)
                ins.then_inc(MS["odh"], 1)
                v.wait_ge(MS["odh"], lin(i, u, 2, 2))
                ts(prel[:, :, :], prel[:, :, :], -float(P), None, ALU.add).then_inc(MS["od"], 1)

            def index(i, u):
                v.wait_ge(MS["ix"], lin(i, u, 1, 1))
                v.wait_ge(MS["xg"][(u - 2) % 2], dma_of(i, u - 2))
                nc.vector.tensor_copy(idxi[:, u % 2:u % 2 + 1], PS[:, 7, 0:1]).then_inc(MS["ii"], 1)

            def xgt_v(i, u):
                v.wait_ge(MS["xt"], lin(i, u, 1, 1))
                v.wait_ge(MS["gu"], lin(i, u, 1, -1))
                nc.vector.tensor_copy(xgT[u % 2][:, 4:8, :], PS[:, 1, :].rearrange("p (a b) -> p a b", b=P)
                                      ).then_inc(MS["xev"], 1)

            def hidden(i, u):
                v.wait_ge(MS["sl"], lin(i, u, 1, 1))
                v.wait_ge(MS["gu"], lin(i, u, 1, 1))
                v.wait_ge(MS["ht"], lin(i, u, 1, -1))
                tt(hsb[u % 2], hsilu, PS[:, 3, :], ALU.mult).then_inc(MS["hm"], 1)

            def y_v(i, u):
                v.wait_ge(MS["dn"], lin(i, u, 2, 2))
                v.wait_ge(MS["yd"][(u - 2) % 2], dma_of(i, u - 2))
                nc.vector.tensor_copy(ysb[u % 2][:, T:D], PS[:, 6, :]).then_inc(MS["yev"], 1)

            def moe_v(i, u, prev=True):
                index(i, u + 2)
                onehot(i, u + 3)
                xgt_v(i, u + 1)
                hidden(i, u)
                if prev:
                    y_v(i, u - 1)

            v.wait_ge(MS["ro"], 1)
            onehot(0, 0)
            onehot(0, 1)
            index(0, 0)
            index(0, 1)
            onehot(0, 2)
            xgt_v(0, 0)
            moe_v(0, 0, False)
            moe_v(0, 1)
            with v.Fori(1, NEXP // 2) as i:
                moe_v(i, 0)
                moe_v(i, 1)
            y_v(NEXP // 2 - 1, 1)
            with overflow(v):
                i0 = NEXP // 2
                moe_v(i0, 0, False)
                moe_v(i0, 1)
                with v.Fori(i0 + 1, i0 + OVB // 2) as i:
                    moe_v(i, 0)
                    moe_v(i, 1)
                y_v(i0 + OVB // 2 - 1, 1)
            v.wait_ge(MS["te"], 16)
            v.wait_ge(MS["gf"], 16)
            for qt in range(QT):
                v.wait_ge(MS["yg"][qt], 32)
                y1, y2 = yg[2 * qt], yg[2 * qt + 1]
                nc.vector.scalar_tensor_tensor(out=y1, in0=y1, scalar=wts[:, 0, qt:qt + 1], in1=xtok[:, qt, :],
                                                     op0=ALU.mult, op1=ALU.add).then_inc(v_ch, 1)
                v.wait_ge(v_ch, v_step())
                nc.vector.scalar_tensor_tensor(out=y1, in0=y2, scalar=wts[:, 1, qt:qt + 1], in1=y1,
                                               op0=ALU.mult, op1=ALU.add).then_inc(MS["fa"], 1)
            for qt in range(QT):
                v.wait_ge(MS["fs"], qt + 1)
                nc.vector.scalar_tensor_tensor(out=yg[2 * qt], in0=yg[2 * qt], scalar=small[:, 8 + qt:9 + qt],
                                               in1=gfin, op0=ALU.mult, op1=ALU.mult).then_inc(MS["ff"], 1)

        @block.tensor
        def _(pe):
            mm = nc.tensor.matmul

            def slot_ready(l, t):
                pe.wait_ge(slot[t % RING], l * (16 * T_LAYER // RING) + 16 * (t // RING + 1))

            def step(l, kind, i):
                if kind == "norm":
                    if i == 0:
                        pass
                    for c in range(KO):
                        pe.wait_ge(sems["sq"], nth("sq", l, 8 * i + c + 1))
                        mm(PS[:, 0, :], ones_d, sq2[:, c % 2, :], start=(c == 0), stop=(c == 7)
                           ).then_inc(sems["sqsum"], 1)
                elif kind == "feat":
                    t = tile_of(i)
                    slot_ready(l, t)
                    pe.wait_ge(sems["evac"], nth("evac", l, i - 1))
                    for c in range(KO):
                        if i == 0:
                            pe.wait_ge(sems["xn"], nth("xn", l, c + 1))
                        ins = mm(PS[:, i % 2, :], ring[:, t % RING, c * P:c * P + P], xn[:, c, :],
                                 start=(c == 0), stop=(c == 7))
                    ins.then_inc(sems["tile"], 1)
                elif kind in ("hi", "v"):
                    t0, nt, w = (T_HI, 4, 512) if kind == "hi" else (T_V, 2, 256)
                    if kind == "v":
                        pe.wait_ge(sems["at"], nth("at", l, 12))
                    for q in range(nt):
                        slot_ready(l, t0 + q)
                        per = 1024 // w
                        for k in range(per):
                            ko = per * q + k
                            for st in range(4):
                                ins = mm(PS[:, 2 + st, 0:w], xn[:, ko, st * P:st * P + P],
                                         ring[:, (t0 + q) % RING, k * w:k * w + w], start=(ko == 0), stop=(ko == 7))
                        ins.then_inc(sems["tile"], 1)
                elif kind == "gram":
                    pe.wait_ge(sems["e"], nth("e", l, i + 1))
                    if i == 0:
                        pe.wait_ge(sems["vh"], nth("vh", l, 4))
                    if i == 3:
                        pe.wait_ge(sems["vn"], nth("vn", l, 4))
                    for c in range(4):
                        n = 4 * i + c
                        if n >= 2:
                            pe.wait_ge(sems["at"], nth("at", l, n - 1))
                        b = 2 + 2 * (n % 2)
                        t = slice(c * P, c * P + P)
                        for j in range(LEVELS):
                            mm(PS[:, b + j // 4, (j % 4) * P:(j % 4) * P + P], E[:, j, t], E[:, j, t],
                               start=True, stop=True)
                        mm(PS[:, b + 1, 3 * P:4 * P], kT[:, i, t], qT[:, i, t], start=True, stop=True
                           ).then_inc(sems["gram"], 1)
                elif kind == "rs":
                    n = T if i < 6 else CMP_N
                    if i < 6:
                        pe.wait_ge(sems["evac"], nth("evac", l, 12 + i + 1))
                    else:
                        pe.wait_ge(sems["kce"], nth("kce", l, 1))
                    pe.wait_ge(sems["rrstd"], nth("rrstd", l, i))
                    mm(PS[:, 6, 0:n], ones_64, sq2[:, i % 2, 0:n], start=True, stop=True).then_inc(sems["stat"], 1)
                elif kind == "rr":
                    n = T if i < 6 else CMP_N
                    pe.wait_ge(sems["qn"], nth("qn", l, i + 1))
                    pe.wait_ge(sems["rope"], nth("rope", l, i))
                    mm(PS[:, 7, 0:n], rotm, qnb[:, i % 2, 0:n], start=True, stop=True).then_inc(sems["rot"], 1)
                elif kind == "gatem":
                    pe.wait_ge(sems["at"], nth("at", l, 16))
                    for qt in range(QT):
                        for c in range(KO):
                            ins = mm(PS[:, 2, 24 * qt:24 * qt + 24], xn[:, c, qt * P:qt * P + P],
                                     misc[:, 24 * c:24 * c + 24], start=(c == 0), stop=(c == 7))
                    ins.then_inc(sems["gatem"], 1)
                elif kind == "cmph":
                    pe.wait_ge(sems["gate"], nth("gate", l, 1))
                    for kv in range(2):
                        pe.wait_ge(sems["dbuild"], nth("dbuild", l, kv + 1))
                        for pr in range(16):
                            t = T_CMP + 4 * kv + pr // 4
                            if pr % 4 == 0:
                                slot_ready(l, t)
                            part, j = pr // 8, pr % 8
                            rhs = DB[:, kv, part, :, :].rearrange("p g (s j) -> p g s j", j=8)[:, :, part:part + CMP_N, j]
                            for hc in range(2):
                                ins = mm(PS[:, 2 + 2 * kv + hc, 0:62],
                                         ring[:, t % RING, (pr % 4) * 256 + hc * P:(pr % 4) * 256 + hc * P + P],
                                         rhs, start=(pr == 0), stop=(pr == 15))
                            if pr % 4 == 3:
                                ins.then_inc(sems["tile"], 1)
                elif kind == "cmpo":
                    pe.wait_ge(sems["hid"], nth("hid", l, 4))
                    w2k, w2v = misc[:, 192:320], misc[:, 320:448]
                    for g in range(2):
                        for hc in range(2):
                            ins = mm(PS[64 * g:64 * g + 64, 2, 0:CMP_N], w2k[:, 64 * hc:64 * hc + 64],
                                     hid[:, 0, hc, CMP_N * g:CMP_N * g + CMP_N], start=(hc == 0), stop=(hc == 1))
                    ins.then_inc(sems["kc"], 1)
                    for j in range(4):
                        for g in range(2):
                            for hc in range(2):
                                ins = mm(PS[32 * j:32 * j + CMP_N, 3, 64 * g:64 * g + 64],
                                         hid[:, 1, hc, CMP_N * g:CMP_N * g + CMP_N], w2v[:, 64 * hc:64 * hc + 64],
                                         start=(hc == 0), stop=(hc == 1))
                    ins.then_inc(sems["vc"], 1)
                elif kind == "ket":
                    if i == 0:
                        pe.wait_ge(sems["qk"], nth("qk", l, 4))
                        pe.wait_ge(sems["kce"], nth("kce", l, 1))
                    if i == 1:
                        pe.wait_ge(sems["vcc"], nth("vcc", l, 1))
                    for h in range(4):
                        ins = nc.tensor.transpose(PS[:, 2 + i, h * P:h * P + P], kT[:, h, i * P:i * P + P], ident)
                    ins.then_inc(sems["ket"], 1)
                elif kind == "state":
                    if i == 0:
                        pe.wait_ge(sems["rope"], nth("rope", l, 7))
                        pe.wait_ge(sems["rrstd"], nth("rrstd", l, 7))
                    if i >= 1:
                        pe.wait_ge(sems["s"], nth("s", l, i))
                    if i >= 2:
                        pe.wait_ge(sems["oc"], nth("oc", l, i - 1))
                    if i < 3:
                        pe.wait_ge(sems["kec"], nth("kec", l, i + 1))
                        for h in range(4):
                            ins = mm(PS[:, 5, h * P:h * P + P], keT[:, i, h, :], Vh[:, i, h * P:h * P + P],
                                     start=True, stop=True)
                        ins.then_inc(sems["ds"], 1)
                    for h in range(4):
                        o = PS[:, 6 + i % 2, h * P:h * P + P]
                        ins = mm(o, Vh[:, i, h * P:h * P + P], AT[:, 4 * h + i, :], start=True, stop=(i == 0))
                        if i:
                            ins = mm(o, Sst[:, h, :], qT[:, h, i * P:i * P + P], start=False, stop=True)
                    ins.then_inc(sems["osum"], 1)
                elif kind == "hn":
                    pe.wait_ge(sems["hsq"], nth("hsq", l, i + 1))
                    if i == 0:
                        pe.wait_ge(sems["evac"], nth("evac", l, 20))
                    if i >= 2:
                        pe.wait_ge(sems["hrs"], nth("hrs", l, i - 1))
                    mm(PS[:, i % 2, :], ones_h, sq2[:, i % 2, :], start=True, stop=True).then_inc(sems["hst"], 1)
                elif kind == "attention":
                    pe.wait_ge(sems["hrs"], nth("hrs", l, 4))
                    pe.wait_ge(sems["s"], nth("s", l, 3))
                    pe.wait_ge(sems["oc"], nth("oc", l, 4))
                    attend(l, NSA)
                elif kind == "wout":
                    pe.wait_ge(sems["hn"], nth("hn", l, 4))
                    pe.wait_ge(sems["p"], nth("p", l, EV["p"]))
                    pe.wait_ge(sems["pt"], nth("pt", l, EV["pt"]))
                    pe.wait_ge(sems["ofree"], nth("ofree", l, 4))
                    for k in range(8):
                        kouter(l, T_WO + k, T_WO + k, mixT[:, k, :], k == 0, k == 7)
                elif kind == "ffn":
                    with pe.Fori(0, FFC // 2) as j:
                        for u in range(4):
                            t = T_FFI + u
                            pe.wait_ge(slot[t % RING], l * (16 * T_LAYER // RING) + j * 16 + 16 * (t // RING + 1))
                            if u % 2 == 0:
                                pe.wait_ge(sems["act"], l * FFC + j * 2 + (u // 2 + 1))
                            for c in range(KO):
                                if u == 0:
                                    pe.wait_ge(sems["xn"], nth("xn", l, 8 + c + 1))
                                ins = mm(PS[:, u, :], ring[:, t % RING, c * P:c * P + P], xn[:, c, :],
                                         start=(c == 0), stop=(c == 7))
                            ins.then_inc(sems["tile"], 1)
                    pe.wait_ge(sems["act"], nth("act", l, FFC))
                    kouter(l, T_FFO, T_FFO, act[:, 0, :], True, False)
                    with pe.Fori(0, 5) as j:
                        for u in range(4):
                            t = T_FFO + 1 + u
                            pe.wait_ge(slot[t % RING], l * (16 * T_LAYER // RING) + j * 16 + 16 * (t // RING + 1))
                            kouter(l, None, t, act[:, j * 4 + (1 + u), :], False, False)
                    kouter(l, T_FFO + FFC - 1, T_FFO + FFC - 1, act[:, FFC - 1, :], False, True)

            def step2(kind, i):
                l = DEPTH
                if kind == "norm":
                    n, w = NORMS2[i][0], MEM if i == 1 else T
                    if i == 1:
                        pe.wait_ge(sems["fls"], nth("fls", 0, 1))
                    for c in range(KO):
                        pe.wait_ge(sems["sq"], nth("sq", l, 8 * n + c + 1))
                        mm(PS[:, 6 if i == 1 else 0, 0:w], ones_d, sq2[:, c % 2, 0:w], start=(c == 0), stop=(c == 7)
                           ).then_inc(sems["sqsum"], 1)
                elif kind == "feat":
                    t = tile2_of(i)
                    src, w = (memn, MEM) if 32 <= i < 34 else (xn, T)
                    slot_ready(l, t)
                    pe.wait_ge(sems["evac"], nth("evac", l, i - 1))
                    for c in range(KO):
                        if i in (0, 32, 34):
                            pe.wait_ge(sems["xn"], nth("xn", l, {0: 0, 32: 8, 34: 16}[i] + c + 1))
                        ins = mm(PS[:, i % 2, 0:w], ring[:, t % RING, c * P:c * P + P], src[:, c, :],
                                 start=(c == 0), stop=(c == 7))
                    ins.then_inc(sems["tile"], 1)
                elif kind == "flog":
                    for c in range(KO):
                        ins = mm(PS[0:8, 6, :], par[:, M_WF + 8 * c:M_WF + 8 * c + 8], xn[:, c, :],
                                 start=(c == 0), stop=(c == 7))
                    ins.then_inc(sems["fl"], 1)
                elif kind == "tok":
                    t0, nt, _, sem = TOK2[i]
                    if i == 1:
                        pe.wait_ge(sems["fv"], nth("fv", 0, 4))
                    if i == 2:
                        pe.wait_ge(sems["dv"], nth("dv", 0, 4))
                        pe.wait_ge(sems["xn"], nth("xn", l, 16))
                    src, n, w = (xn, 4, T) if sem != "cv" else (memn, 2, MEM)
                    per = 1024 // w
                    for q in range(nt):
                        slot_ready(l, t0 + q)
                        for k in range(per):
                            ko = per * q + k
                            for st in range(n):
                                ins = mm(PS[:, 2 + st, 0:w], src[:, ko, st * P:st * P + P],
                                         ring[:, (t0 + q) % RING, k * w:k * w + w], start=(ko == 0), stop=(ko == 7))
                        ins.then_inc(sems["tile"], 1)
                elif kind == "rr":
                    pe.wait_ge(sems["evac"], nth("evac", l, 8 + i + 1))
                    pe.wait_ge(sems["rope"], nth("rope", l, i))
                    mm(PS[:, 7, :], rotm, qnb[:, i % 2, :], start=True, stop=True).then_inc(sems["rot"], 1)
                elif kind == "attention":
                    pe.wait_ge(sems["evac"], nth("evac", l, 34))
                    pe.wait_ge(sems["cv"], nth("cv", 0, 2))
                    pe.wait_ge(sems["nck"], nth("nck", 0, 1))
                    pe.wait_ge(sems["fls"], nth("fls", 0, 1))
                    pe.wait_ge(sems["rope"], nth("rope", l, 8))
                    attend(l, BL2)
                elif kind == "cross":
                    pe.wait_ge(sems["evac"], nth("evac", l, 36))
                    attend(l, CROSS)
                elif kind == "merge":
                    pe.wait_ge(sems["pt"], nth("pt", l, 72))
                    pe.wait_ge(sems["p"], nth("p", l, 64))
                    for c in range(8):
                        slot_ready(l, B_AB + c)
                        if c >= 2:
                            pe.wait_ge(sems["mrg"], nth("mrg", 0, c - 1))
                        b = 2 * (c % 2)
                        for j, y in enumerate((yaT, ybT)):
                            for k in range(4):
                                ins = mm(PS[:, b + j, :], ring[:, (B_AB + c) % RING, (4 * j + k) * P:(4 * j + k + 1) * P],
                                         y[:, k, :], start=(k == 0), stop=(k == 3))
                        ins.then_inc(sems["tile"], 1)
                elif kind == "kouter":
                    if i == 0:
                        pe.wait_ge(sems["mrg"], nth("mrg", 0, 8))
                        pe.wait_ge(sems["ofree"], nth("ofree", l, 4))
                        for k in range(8):
                            kouter(l, B_WO + k, B_WO + k, merged[:, k, :], k == 0, k == 7)
                    else:
                        pe.wait_ge(sems["p"], nth("p", l, 80))
                        pe.wait_ge(sems["pt"], nth("pt", l, 72 + 20))
                        pe.wait_ge(sems["ofree"], nth("ofree", l, 8))
                        for k in range(2):
                            kouter(l, B_CO + k, B_CO + k, coT[:, k, :], k == 0, k == 1)

            def kouter(l, wait_t, t, rhs, first, last):
                if wait_t is not None:
                    slot_ready(l, wait_t)
                for c in range(8):
                    ins = mm(PS[:, c, :], ring[:, t % RING, c * P:c * P + P], rhs, start=first, stop=last)
                    if c == 7:
                        ins.then_inc(sems["tile"], 1)
                    elif last:
                        ins.then_inc(sems["res"], 1)

            def attend(l, items):
                for s in range(len(items) + LAG_V):
                    it = items[s] if s < len(items) else None
                    if it and it["kind"] != "mix":
                        k = it["k"]
                        if k >= 3:
                            pe.wait_ge(sems["p"], nth("p", l, k - 2))
                        if items is CROSS and k == 64:
                            pe.wait_ge(sems["pt"], nth("pt", l, 72))
                        for j, (lo, hi, lhsT, rhs) in enumerate(it["sc"]):
                            ins = mm(PS[:, k % 3, lo:hi], lhsT, rhs, start=(j == 0), stop=(j == len(it["sc"]) - 1),
                                     skip_group_check=True)
                        ins.then_inc(sems["sc"], 1)
                    it = items[s - LAG_T] if 0 <= s - LAG_T < len(items) else None
                    if it:
                        t = it["t"]
                        if t >= 2:
                            pe.wait_ge(sems["pt"], nth("pt", l, t - 1))
                        if it["kind"] == "mix":
                            pe.wait_ge(sems["mixtok"], nth("mixtok", l, it["mixn"]))
                            for b in range(it["nb"]):
                                ins = nc.tensor.transpose(PS[:, 3 + t % 2, b * P:b * P + P],
                                                          it["src"][:, b * P:b * P + P], ident)
                        else:
                            pe.wait_ge(sems["p"], nth("p", l, it["k"] + 1))
                            for b in range(it["nb"]):
                                ins = nc.tensor.transpose(PS[:, 3 + t % 2, b * P:b * P + P],
                                                          Pr[:, it["k"] % 3, b * P:b * P + P], ident)
                        ins.then_inc(sems["tr"], 1)
                    it = items[s - LAG_V] if 0 <= s - LAG_V < len(items) else None
                    if it and it["kind"] != "mix":
                        pe.wait_ge(sems["pt"], nth("pt", l, it["t"] + 1))
                        if it.get("first", 0):
                            pe.wait_ge(sems["ofree"], nth("ofree", l, it["first"]))
                        for o, b, rhs, start, stop in it["pv"]:
                            ins = mm(o, PTs[:, it["t"] % 2, b * P:b * P + P], rhs, start=start, stop=stop)
                        ins.then_inc(sems["pv"], 1)

            pe.wait_ge(s_in, 16 * (NIN + 1))
            with pe.Fori(0, DEPTH_RUN) as l:
                pe.wait_ge(sems["params"], nth("params", l, 2))
                for kind, i in STEPS:
                    step(l, kind, i)
            pe.wait_ge(sems["b_in"], 64)
            for kind, i in STEPS2:
                step2(kind, i)

            ones_b, before_b = maskb[:, K_ONES:K_ONES + P], maskb[:, K_BEFORE:K_BEFORE + P]
            pe.wait_ge(sems["xn"], nth("xn", DEPTH, 32))
            for qt in range(QT):
                for c in range(KO):
                    ins = mm(PS[:, 0, 36 * qt:36 * qt + 36], xn[:, c, qt * P:qt * P + P],
                             par[:, M_WGE + 36 * c:M_WGE + 36 * c + 36], start=(c == 0), stop=(c == 7))
            ins.then_inc(MS["lg"], 1)
            for g in range(16):
                qt, half = g % 8 // 2, g % 2
                if g >= 4:
                    pe.wait_ge(MS["te"], g - 3)
                src = xn if g < 8 else xT
                for c in range(4):
                    ins = nc.tensor.transpose(PS[:, 4 + g % 4, c * P:c * P + P],
                                              src[:, 4 * half + c, qt * P:qt * P + P], ident)
                ins.then_inc(MS["tr"], 1)
            pe.wait_ge(MS["A"], 1)
            for qt in range(QT):
                for q in range(qt):
                    mm(PS[:, 1, 32 * qt:32 * qt + 32], ones_b, Ab[:, q, :], start=(q == 0), stop=False)
                mm(PS[:, 1, 32 * qt:32 * qt + 32], before_b, Ab[:, qt, :], start=(qt == 0), stop=True)
            for q in range(QT):
                ins = mm(PS[:, 1, 128:160], ones_b, Ab[:, q, :], start=(q == 0), stop=(q == 3))
            ins.then_inc(MS["rk"], 1)

            def index(i, u):
                pe.wait_ge(MS["od"], lin(i, u, 1, 1))
                pe.wait_ge(MS["ii"], lin(i, u, 1, 0))
                for qt in range(QT):
                    mm(PS[:, 7, 0:1], Ob[u % 2][:, qt, :], maskb[:, K_TID:K_TID + 1], start=(qt == 0), stop=False)
                    ins = mm(PS[:, 7, 0:1], Ob[u % 2][:, qt, :], maskb[:, K_TID + 1 + qt:K_TID + 2 + qt],
                             start=False, stop=(qt == 3))
                ins.then_inc(MS["ix"], 1)

            def turn_x(i, u):
                pe.wait_ge(MS["xg"][u % 2], dma_of(i, u))
                pe.wait_ge(MS["xea"], lin(i, u, 1, 0))
                pe.wait_ge(MS["xev"], lin(i, u, 1, 0))
                for c in range(KO):
                    ins = nc.tensor.transpose(PS[:, c // 4, (c % 4) * P:(c % 4) * P + P],
                                              xg[u % 2][:, c * P:c * P + P], ident)
                ins.then_inc(MS["xt"], 1)

            def gate_up(i, u):
                pe.wait_ge(MS["xea"], lin(i, u, 1, 1))
                pe.wait_ge(MS["xev"], lin(i, u, 1, 1))
                for j, (w, name, free, done) in enumerate(((wg, "wg", "sl", "gg"), (wu, "wu", "hm", "gu"))):
                    pe.wait_ge(MS[name][u % 2], dma_of(i, u))
                    pe.wait_ge(MS[free], lin(i, u, 1, 0))
                    for c in range(KO):
                        ins = mm(PS[:, 2 + j, :], xgT[u % 2][:, c, :], w[u % 2][:, c, :], start=(c == 0), stop=(c == 7))
                    ins.then_inc(MS[done], 1)

            def turn_h(i, u):
                pe.wait_ge(MS["hm"], lin(i, u, 1, 1))
                pe.wait_ge(MS["he"], lin(i, u, 1, 0))
                for c in range(4):
                    ins = nc.tensor.transpose(PS[:, 4, c * P:c * P + P], hsb[u % 2][:, c * P:c * P + P], ident)
                ins.then_inc(MS["ht"], 1)

            def down(i, u):
                pe.wait_ge(MS["he"], lin(i, u, 1, 1))
                pe.wait_ge(MS["wd"][u % 2], dma_of(i, u))
                pe.wait_ge(MS["yea"], lin(i, u, 1, 0))
                pe.wait_ge(MS["yev"], lin(i, u, 1, 0))
                for j in range(2):
                    for c in range(4):
                        ins = mm(PS[:, 5 + j, :], hT[u % 2][:, c, :], wd[u % 2][:, c, T * j:T * j + T],
                                 start=(c == 0), stop=(c == 3))
                    ins.then_inc(MS["dn"], 1)

            def moe_p(i, u, prev=True):
                index(i, u + 2)
                turn_x(i, u + 1)
                if prev:
                    turn_h(i, u - 1)
                gate_up(i, u)
                if prev:
                    down(i, u - 1)

            pe.wait_ge(MS["te"], 16)
            index(0, 0)
            index(0, 1)
            turn_x(0, 0)
            moe_p(0, 0, False)
            moe_p(0, 1)
            with pe.Fori(1, NEXP // 2) as i:
                moe_p(i, 0)
                moe_p(i, 1)
            turn_h(NEXP // 2 - 1, 1)
            down(NEXP // 2 - 1, 1)
            with overflow(pe):
                i0 = NEXP // 2
                moe_p(i0, 0, False)
                moe_p(i0, 1)
                with pe.Fori(i0 + 1, i0 + OVB // 2) as i:
                    moe_p(i, 0)
                    moe_p(i, 1)
                turn_h(i0 + OVB // 2 - 1, 1)
                down(i0 + OVB // 2 - 1, 1)


def tile_of(t):
    return t if t < 12 else t + 4 if t < 18 else T_C + t - 18


STEPS = (
    [("norm", 0)]
    + [("feat", 0), ("feat", 1), ("gate_h", 0), ("feat", 2), ("gate_h", 1), ("scan", 0), ("feat", 3), ("scan", 1),
       ("gate_h", 2), ("feat", 4), ("gate_h", 3), ("decay", 0), ("feat", 5), ("feat", 6), ("feat", 7)]
    + [("feat", 8), ("feat", 9), ("feat", 10), ("feat", 11), ("vczero", 0), ("hi", 0), ("gram", 0), ("decay", 1),
       ("qk", 0), ("scan", 2)]
    + [("feat", 12), ("feat", 13), ("rs", 0), ("feat", 14), ("rs", 1), ("rr", 0), ("gram", 1), ("decay", 2), ("qk", 1),
       ("scan", 3), ("feat", 15), ("rs", 2), ("rr", 1), ("feat", 16), ("rs", 3), ("rr", 2), ("feat", 17), ("rs", 4),
       ("rr", 3), ("gram", 2), ("decay", 3), ("qk", 2), ("v", 0), ("rs", 5), ("rr", 4), ("gram", 3), ("qk", 3),
       ("feat", 18), ("rr", 5), ("dbuild", 0), ("feat", 19), ("dbuild", 1), ("gatem", 0), ("cmph", 0), ("cmpo", 0),
       ("rs", 6), ("ket", 0), ("ket", 1), ("ket", 2), ("rr", 6)]
    + [("state", c) for c in range(4)] + [("hn", h) for h in range(4)]
    + [("attention", 0), ("wout", 0), ("norm", 1), ("ffn", 0)])
def tile2_of(f):
    return f if f < 8 else f + 4 if f < 16 else f + 8 if f < 34 else B_CQ + f - 34


NORMS2 = [(0, 0), (1, None), (2, 1), (3, 2)]
TOK2 = [(B_FV, 4, "fv", "fv"), (B_DV, 4, "dv", "dv"), (B_CV, 2, "cv", "cv")]
STEPS2 = (
    [("lam", 0), ("trig", 0), ("norm", 0)] + [("feat", i) for i in range(8)] + [("flog", 0), ("tok", 0)]
    + [("feat", 8), ("feat", 9), ("rr", 0)]
    + [x for i in range(10, 16) for x in (("feat", i), ("rr", i - 9))] + [("tok", 1), ("rr", 7)]
    + [("norm", 1)] + [("feat", i) for i in range(16, 32)] + [("feat", 32), ("feat", 33), ("tok", 2)]
    + [("attention", 0), ("merge", 0), ("kouter", 0), ("norm", 2), ("feat", 34), ("feat", 35), ("cross", 0),
       ("kouter", 1), ("norm", 3)])
A_CH = 2 + ROPES + 4
V_CH = 61
DEPTH_RUN = DEPTH
NTILES_RUN = NTILES


def lhs_tile(w):
    return w.reshape(KO, P, -1).transpose(1, 0, 2)


def ring_tiles(a):
    out = np.zeros((NTILES, P, 1024), np.float32)
    for l in range(DEPTH):
        w, base = a["w_in"][l], l * T_LAYER
        hq, hf, hi, hg, nq, kc, vc, ks, vs, kw, vw = (w[:, o:o + n] for o, n in (
            (0, 512), (512, 512), (1024, 512), (1536, 512), (2048, 512), (2560, 128), (2688, 128), (2816, 128),
            (2944, 128), (3072, 128), (3200, 128)))
        for i in range(4):
            for j, x in enumerate((hf, hq, hg)):
                out[base + 4 * j + i] = lhs_tile(x[:, i * P:i * P + P]).reshape(P, -1)
            out[base + T_HI + i] = hi.reshape(4, 2, P, 512)[i].transpose(1, 0, 2).reshape(P, -1)
            pair = np.concatenate([nq[:, 64 * i:64 * i + 64], nq[:, 64 * (i + 4):64 * (i + 4) + 64]], 1)
            out[base + T_NQ + i] = lhs_tile(pair).reshape(P, -1)
        for t, x in ((T_NQ + 4, ks), (T_NQ + 5, kw), (T_C, kc), (T_C + 1, vc)):
            out[base + t] = lhs_tile(x).reshape(P, -1)
        vv = np.concatenate([vs, vw], 1).reshape(2, 4, P, 256)
        for i in range(2):
            out[base + T_V + i] = vv[i].transpose(1, 0, 2).reshape(P, -1)
        for j, x in enumerate((a["cmp_w1_k"][l], a["cmp_w1_v"][l])):
            x = x.reshape(4, 4, P, 256)
            for i in range(4):
                out[base + T_CMP + 4 * j + i] = x[i].transpose(1, 0, 2).reshape(P, -1)
        out[base + T_WO:base + T_WO + 8] = a["w_out"][l].reshape(8, P, 1024)
        g = a["w_ffn_in"][l].reshape(KO, P, 2, FFC, P).transpose(3, 2, 1, 0, 4)
        out[base + T_FFI:base + T_FFI + 2 * FFC] = g.reshape(2 * FFC, P, 1024)
        out[base + T_FFO:base + T_LAYER] = a["w_ffn_out"][l].reshape(FFC, P, 1024)
    block2_tiles(a, out)
    return out


def block2_tiles(a, out):
    w = a["w_in_2"][0]
    base = DEPTH * T_LAYER
    fq, fk, fv, _, dq, dk, dv, ga, gb = (w[:, o:o + n] for o, n in (
        (0, 512), (512, 512), (1024, 512), (1536, 8), (1544, 512), (2056, 512), (2568, 512), (3080, 1024),
        (4104, 1024)))
    for t, x in ((B_FQ, fq), (B_FK, fk), (B_DQ, dq), (B_DK, dk), (B_GA, ga), (B_GA + 8, gb),
                 (B_CK, a["w_ckv_2"][0][:, 0:256]), (B_CQ, a["w_cq_2"][0])):
        for i in range(x.shape[1] // P):
            out[base + t + i] = lhs_tile(x[:, i * P:i * P + P]).reshape(P, -1)
    for t, x in ((B_FV, fv), (B_DV, dv)):
        for i in range(4):
            out[base + t + i] = x.reshape(4, 2, P, 512)[i].transpose(1, 0, 2).reshape(P, -1)
    x = a["w_ckv_2"][0][:, 256:512].reshape(2, 4, P, 256)
    for i in range(2):
        out[base + B_CV + i] = x[i].transpose(1, 0, 2).reshape(P, -1)
    ab = np.stack([a["w_branch_a_2"][0], a["w_branch_b_2"][0]]).reshape(2, 4, P, 8, P)
    out[base + B_AB:base + B_AB + 8] = ab.transpose(3, 2, 0, 1, 4).reshape(8, P, 1024)
    out[base + B_WO:base + B_WO + 8] = a["w_out_2"][0].reshape(8, P, 1024)
    out[base + B_CO:base + B_CO + 2] = a["w_co_2"][0].reshape(2, P, 1024)


def block2_params(a):
    out = np.zeros((P, M_END), np.float32)
    for c, name in ((M_MIX, "g_mix_2"), (M_MEM, "g_mem_2"), (M_CROSS, "g_cross_2"), (M_FFN, "g_ffn_2")):
        out[:, c:c + 8] = a[name][0].reshape(8, P).T
    out[:, M_SUB] = a["g_diff_sub_2"][0]
    freq = np.float32(10000.0) ** (-np.arange(32, dtype=np.float32) * np.float32(2.0) / np.float32(64))
    out[:, M_FREQ] = freq[np.arange(P) % 32]
    out[0:8, M_BF] = a["b_fgate_2"][0]
    out[:, M_WF:M_WF + 64] = lhs_tile(a["w_in_2"][0][:, 1536:1544]).reshape(P, 64)
    for j, name in enumerate(("lambda_q1_2", "lambda_k1_2", "lambda_q2_2", "lambda_k2_2")):
        out[:, M_LAM + 64 * j:M_LAM + 64 * j + 64] = a[name][0]
    wge = np.concatenate([a["w_group_2"][0], a["w_expert_2"][0]], 1)
    out[:, M_WGE:M_WGE + 288] = lhs_tile(wge).reshape(P, 288)
    out[:, M_BGE:M_BGE + 36] = np.concatenate([a["b_group_2"][0], a["b_expert_2"][0]])
    out[:, M_IOTA:M_IOTA + P] = np.arange(P)
    out[:, M_E:M_E + NEXP] = np.arange(NEXP)
    return out


def layer_columns(a):
    out = np.zeros((P, DEPTH, NCOL), np.float32)
    for l in range(DEPTH):
        out[:, l, C_MIX:C_MIX + 8] = a["norm_mix"][l].reshape(8, P).T
        out[:, l, C_FFN:C_FFN + 8] = a["norm_ffn"][l].reshape(8, P).T
        out[:, l, C_GN] = a["hg_gnorm"][l]
        out[:, l, C_QG] = np.tile(a["q_gain"][l], 2)
        for j, br in enumerate((1, 2, 0)):
            out[:, l, C_KG + (j + 1) % 3] = np.tile(a["k_gain"][l][br], 2)
        for j, pe in enumerate((a["cmp_pe_k"][l], a["cmp_pe_v"][l])):
            x = pe.reshape(16, 2, 64).transpose(2, 1, 0).reshape(64, 32)
            out[:, l, C_PE + 32 * j:C_PE + 32 * j + 32] = np.concatenate([x, x], 0)
        out[:, l, C_LB:C_LB + 4] = a["hg_lb_logits"][l].reshape(4, P).T
    return out


def misc_weights(a):
    out = np.zeros((P, DEPTH, MISC), np.float32)
    for l in range(DEPTH):
        out[:, l, 0:192] = lhs_tile(a["w_in"][l][:, 3328:3352]).reshape(P, 192)
        out[:, l, 192:320] = a["cmp_w2_k"][l].reshape(2, P, 64).transpose(1, 0, 2).reshape(P, P)
        out[:, l, 320:448] = a["cmp_w2_v"][l].reshape(2, P, 64).transpose(1, 0, 2).reshape(P, P)
    return out


def constants():
    half = 32
    freqs = (np.float32(10000.0) ** (-np.arange(half, dtype=np.float32) / np.float32(half))).astype(np.float32)
    ang = np.arange(T, dtype=np.float32)[None, :] * freqs[np.arange(P) % half][:, None]
    p = np.arange(P)
    ones_64 = ((p[:, None] // 64) == (p[None, :] // 64)) / 64.0
    rot = np.zeros((P, P))
    for m in range(P):
        if m % 64 < 32:
            rot[m + 32, m] = -1.0
        else:
            rot[m - 32, m] = 1.0
    valid = np.zeros((P, P))
    valid[31:, 0] = 1.0
    mats = [np.full((P, P), 1.0 / D), np.full((P, P), 1.0 / P), ones_64, rot, np.eye(P), valid]
    s, t = p[:, None], p[None, :]
    gm = []
    for j in range(LEVELS):
        w = 64 >> j
        gm.append((s // (2 * w) == t // (2 * w)) & (s // w % 2 == 0) & (t // w % 2 == 1))
    gm.append(s == t)
    tabs = np.concatenate([np.cos(ang), np.sin(ang)] + mats + [g.astype(np.float32) for g in gm], 1).astype(np.float32)
    tok = np.arange(T).reshape(QT, P)
    masks = [np.eye(P), np.where(t > s, NEG, 0.0)]
    for qt in range(QT):
        n = np.arange(P) % 32
        ok = (n[None, :] < CMP_N) & (n[None, :] * 16 + 31 <= tok[qt][:, None])
        masks.append(np.where(ok, 0.0, NEG))
    masks += [np.ones((P, P)), s < t]
    tid = np.zeros((P, 8))
    tid[:, 0] = p
    tid[:, 1:1 + QT] = np.arange(QT) * P
    masks.append(tid)
    masks = np.ascontiguousarray(np.concatenate(masks, 1).astype(np.float32))
    return tabs, (masks.view(np.uint32) >> 16).astype(np.uint16)


def kernel(**inputs):
    import concourse.bacc as _bacc
    from concourse.bass_utils import run_bass_kernel_spmd as _run

    a = {k: np.asarray(x) for k, x in inputs.items()}
    nc = _bacc.Bacc("TRN2", target_bir_lowering=False, num_devices=1)
    tabs, masks = constants()
    arrays = {
        "ring_w": ring_tiles(a),
        "xT_in": np.ascontiguousarray(a["x"][0].T).reshape(KO, P, T),
        "cols_in": layer_columns(a),
        "misc_in": misc_weights(a),
        "tabs_in": tabs,
        "masks_in": masks,
        "par_in": block2_params(a),
        "sel_in": np.ascontiguousarray(np.broadcast_to((np.arange(P)[:, None, None] == np.arange(8)[None, :, None]),
                                                       (P, 8, P))).astype(np.float32),
        "pos_in": np.ascontiguousarray(np.broadcast_to(a["positions_2"], (P, T))).astype(np.int32),
        "gfin_in": np.ascontiguousarray(np.broadcast_to(a["g_final_2"], (P, D))),
        "w_gate": a["w_exp_gate_2"][0], "w_up": a["w_exp_up_2"][0], "w_down": a["w_exp_down_2"][0],
        "memT_in": np.ascontiguousarray(a["mem_2"][0].T.reshape(KO, P, MEM).transpose(1, 0, 2)),
    }
    aps = {k: nc.dram_tensor(k, x.shape, mybir.dt.from_np(x.dtype), kind="ExternalInput").ap()
           for k, x in arrays.items()}
    hm_dram = nc.dram_tensor("hm_dram", (T, D), F32, kind="Internal").ap()
    y_dram = nc.dram_tensor("y_dram", (YROWS // P // 2, 2, P, D), F32, kind="Internal").ap()
    out = nc.dram_tensor("out", (QT, P, D), F32, kind="ExternalOutput").ap()
    build(nc, **aps, hm_dram=hm_dram, y_dram=y_dram, out=out)
    r = _run(nc, [arrays], core_ids=[0])
    return r.results[0]["out"].reshape(1, T, D)
```

```python
from contextlib import ExitStack

import numpy as np

import concourse.bass as bass
from concourse import mybir

F32 = mybir.dt.float32
F32R = mybir.dt.float32r
BF16 = mybir.dt.bfloat16
I32 = mybir.dt.int32
ALU = mybir.AluOpType
ACT = mybir.ActivationFunctionType
AX = mybir.AxisListType

P = 128
T = 512
D = 1024
KO = D // P
QT = T // P
DEPTH = 2
HEADS = 8
CMP_N = (T - 32) // 16 + 1
FF = 2816
FFC = FF // P
RING = 4
MEM = 256
NEXP = 32
OVER = 7
NEG = -1e30

T_HF, T_HQ, T_HG = 0, 4, 8
T_HI = 12
T_NQ = 16
T_V = 22
T_C = 24
T_CMP = 26
T_WO = 34
T_FFI = 42
T_FFO = 86
T_LAYER = 108
B_FQ, B_FK, B_FV, B_DQ, B_DK, B_DV, B_CK, B_CV = 0, 4, 8, 12, 16, 20, 24, 26
B_GA, B_AB, B_WO, B_CQ, B_CO, B_TILES = 28, 44, 52, 60, 62, 64
NTILES = DEPTH * T_LAYER + B_TILES

C_MIX, C_FFN, C_GN, C_QG, C_KG, C_PE, C_LB, NCOL = 0, 8, 16, 17, 18, 21, 85, 93
ARENA = 20480
LEVELS = 7
MISC = 8 * 24 + 2 * 2 * 64
M_MIX, M_MEM, M_CROSS, M_FFN, M_SUB, M_FREQ, M_BF, M_WF, M_LAM, M_WGE, M_BGE, M_IOTA, M_E, M_END = (
    0, 8, 16, 24, 32, 33, 34, 35, 99, 355, 643, 679, 807, 839)
YROWS = (NEXP + OVER + 1) * P
OVB = OVER + 1
K_ONES, K_BEFORE, K_TID = (2 + QT) * P, (3 + QT) * P, (4 + QT) * P
K_GRAM = K_TID + 8
TWO_PI = 2 * np.pi

ROPES = 7
EV = dict(
    tile=T_LAYER,
    whi=T_LAYER, split=T_LAYER,
    sq=16, sqsum=16, rstd=2, xr=16, xh=16, xn=16,
    xs=30, xsh=FFC,
    res=14, h=16,
    params=2,
    evac=20,
    f=4, ln=4, kd=4, kqexp=4, ediff=4, eexp=4, e=4, gram=16, at=16, qk=4,
    vh=4, vn=4,
    stat=ROPES, rrstd=ROPES, qn=ROPES, rot=ROPES, rope=ROPES,
    gatem=1, gate=1, gatet=1, gates=1,
    dbuild=2, hid=4, kc=1, kce=1, vc=1, vcc=1,
    ket=3, kec=3, osum=4, oc=4, ds=3, s=3,
    hsq=4, hst=4, hrs=4, hn=4,
    sc=72, mx=72, p=72, tr=76, pt=76, pv=72,
    ofree=4, mixtok=4,
    silu=FFC, act=FFC,
    b_in=0, sel=0, trig=0, trigs=0, fl=0, fls=0, nck=0, lam=0, lams=0, fv=0, dv=0, cv=0, mrg=0, ms=0, msr=0)
CREDIT = dict(tile=RING, evac=2, rrstd=1, rope=1, h=8, act=2)


def build(nc, ring_w, xT_in, cols_in, misc_in, tabs_in, masks_in, par_in, sel_in, pos_in, memT_in, gfin_in,
          w_gate, w_up, w_down, hm_dram, y_dram, out):
    ctx = ExitStack()
    with ctx:
        def sb(name, shape, dt=F32):
            return ctx.enter_context(nc.sbuf_tensor(name, shape, dt))

        PS = ctx.enter_context(nc.psum_tensor("PS", [P, 8, 512], F32))

        xT = sb("xT", [P, KO, T])

        def aliased(dt, *shapes):
            with ExitStack() as scope:
                return [scope.enter_context(nc.sbuf_tensor(name, shape, dt)) for name, shape in shapes]

        xh, xl = aliased(F32R, ("xh", [P, KO, T]), ("xl", [P, KO, T]))
        xraw = sb("xraw", [P, 2 * KO * T])
        xn = xraw[:, 0:KO * T].rearrange("p (a b) -> p a b", b=T)
        xr = xraw[:, KO * T:].rearrange("p (a b) -> p a b", b=T)
        wlo, = aliased(F32R, ("wlo", [P, RING, 1024]))
        ring = sb("ring", [P, RING, 1024])
        whi = sb("whi", [P, 2, 1024], F32R)
        wsm = sb("wsm", [P, 2, 7 * 24 + P], F32R)
        cols = sb("cols", [P, DEPTH, NCOL])
        lcol = sb("lcol", [P, NCOL])
        misc_all = sb("misc_all", [P, DEPTH, MISC])
        misc = sb("misc", [P, MISC])
        tabs = sb("tabs", [P, 2 * T])
        mats = sb("mats", [P, 5 * P + 1])
        maskb = sb("maskb", [P, K_GRAM + 8 * P], BF16)
        eps = sb("eps", [P, 2])
        sq2 = sb("sq2", [P, 2, T])
        lnb = sb("lnb", [P, T])
        cos, sin = tabs[:, 0:T], tabs[:, T:2 * T]
        ones_d, ones_h, ones_64, rotm, ident = (mats[:, i * P:i * P + P] for i in range(5))
        valid0 = mats[:, 5 * P:5 * P + 1]
        ident_b = maskb[:, 0:P]
        causal_b = maskb[:, P:2 * P]

        arena_r, = aliased(F32R, ("arena_r", [P, ARENA]))
        arena = sb("arena", [P, ARENA])

        def at_(off, *shape):
            n = int(np.prod(shape))
            assert off + n <= ARENA, (off, n)
            v = arena[:, off:off + n]
            if len(shape) == 2:
                v = v.rearrange("p (a b) -> p a b", b=shape[1])
            elif len(shape) == 3:
                v = v.rearrange("p (a b c) -> p a b c", b=shape[1], c=shape[2])
            elif len(shape) == 4:
                v = v.rearrange("p (a b c d) -> p a b c d", b=shape[1], c=shape[2], d=shape[3])
            return v

        kT = at_(3584, 4, T)
        qT = at_(5632, 4, T)
        mixT = at_(3584, 8, T)
        bT = at_(7680, 4, T)
        sgT = at_(9728, 4, T)
        Vh = at_(11776, 4, T)
        AT = at_(13824, 16, P)
        qr = at_(15872, 4, T)
        kr = at_(17920, 2, T)
        Vn = at_(18944, 4, 256)
        VC = at_(19968, 2, 4, 64)
        E = at_(0, LEVELS, T)
        craw = at_(0, 2, T)
        keT = at_(7680, 3, 4, P)
        Sst = at_(7680 + 1536, 4, P)
        act = at_(0, FFC, T)
        fq, fk, fv = at_(0, 4, T), at_(2048, 4, T), at_(4096, 4, T)
        dq, dk, dv = at_(6144, 4, T), at_(8192, 4, T), at_(10240, 4, T)
        sga = at_(12288, 16, T)
        memn = at_(12288, KO, MEM)
        merged = sga[:, 0:8, :]
        LOADED = dict(G=8192, U=12288, D=16384)
        HIGH = dict(G=arena_r[:, 0:4096], U=arena_r[:, 4096:8192], D=xl[:, :, :].rearrange("p a b -> p (a b)"))

        def loaded(w, k):
            return arena[:, LOADED[w] + 1024 * k:LOADED[w] + 1024 * k + 1024]

        def high(w, k):
            return HIGH[w][:, 1024 * k:1024 * k + 1024]

        def low(w, k):
            return arena_r[:, LOADED[w] + 1024 * k:LOADED[w] + 1024 * k + 1024]

        yg = [at_(1024 * i, D) for i in range(2 * QT)]
        xtok = ring
        xflat = xT[:, :, :].rearrange("p a b -> p (a b)")
        xg = (xflat[:, 0:D], xflat[:, D:2 * D])
        ysb = (xflat[:, 2 * D:3 * D], xflat[:, 3 * D:4 * D])
        xgT = [[xh[:, 4 * u + 2 * j:4 * u + 2 * j + 2, :].rearrange("p a b -> p (a b)").rearrange(
            "p (a b) -> p a b", b=P) for j in range(2)] for u in range(2)]
        hT = [[whi[:, u, T * j:T * j + T].rearrange("p (a b) -> p a b", b=P) for j in range(2)] for u in range(2)]

        ftmp = sb("ftmp", [P, 2, T])
        ekb = sb("ekb", [P, 4, T])
        ebuf, kdb = ekb[:, 0:2, :], ekb[:, 2:4, :]
        ebl = sb("ebl", [P, 4, 4])
        gmask = maskb[:, K_GRAM:K_GRAM + 8 * P]
        one = sb("one", [P, 1])
        gtmp = sb("gtmp", [P, 8 * P])
        xs, = aliased(F32R, ("xs", [P, 2, 2, T]))
        qgn = sb("qgn", [P, 4, T])
        qg, qnb = qgn[:, 0:2, :], qgn[:, 2:4, :]
        rrs = sb("rrs", [P, 2, T])
        rstd = rrs[:, 0, :]
        hsb = (rrs[:, 0, :], rrs[:, 1, :])
        Pr = (rrs[:, 0, :], rrs[:, 1, :], lnb)
        PTs = (sq2[:, 0, :], sq2[:, 1, :])
        DB = ekb[:, :, :].rearrange("p (v a) (g s) -> p v a g s", a=2, g=2)
        hid = sb("hid", [P, 2, 2, 62])
        kcr = sb("kcr", [P, 32])
        nmx = sb("nmx", [P, 4, 4])
        Lt = sb("Lt", [P, 2, 24])
        Rc = sb("Rc", [P, 24])
        gates = sb("gates", [P, QT, 24])
        oa = qg
        mixtok = ftmp[:, 0, :]
        lb = sb("lb", [P, DEPTH, 4])
        lbl = sb("lbl", [P, 8])
        lnl = sq2[:, 0, 0:P].rearrange("p (a b) -> p a b", b=64)

        sems = {k: ctx.enter_context(nc.semaphore(k)) for k in EV}
        slot = [ctx.enter_context(nc.semaphore(f"slot{i}")) for i in range(RING)]
        s_in = ctx.enter_context(nc.semaphore("s_in"))
        s_tab = ctx.enter_context(nc.semaphore("s_tab"))
        s_out = ctx.enter_context(nc.semaphore("s_out"))
        s_pre = ctx.enter_context(nc.semaphore("s_pre"))
        a_ch = ctx.enter_context(nc.semaphore("a_ch"))
        v_ch = ctx.enter_context(nc.semaphore("v_ch"))
        g_ch = ctx.enter_context(nc.semaphore("g_ch"))
        NIN = 4
        par = misc_all[:, :, :].rearrange("p a b -> p (a b)")
        sel = tabs[:, :].rearrange("p (a b) -> p a b", b=P)
        negc = ekb[:, 0, :]
        ckT = ekb[:, 1, :].rearrange("p (a b) -> p a b", b=MEM)
        cvt = ekb[:, 2, :].rearrange("p (a b) -> p a b", b=MEM)
        small = sb("small", [P, 16])
        cqT = gtmp[:, :].rearrange("p (a b) -> p a b", b=T)
        coT = tabs[:, :].rearrange("p (a b) -> p a b", b=T)
        gfin = ekb[:, 0:2, :].rearrange("p a b -> p (a b)")
        hmt = (ekb[:, 0:2, :].rearrange("p a b -> p (a b)"), ekb[:, 2:4, :].rearrange("p a b -> p (a b)"),
               qg[:, :, :].rearrange("p a b -> p (a b)"), qnb[:, :, :].rearrange("p a b -> p (a b)"))
        lg = tabs[:, 0:144].rearrange("p (q e) -> p q e", e=36)
        em, oh1, oh2, rnk, tmpe = (tabs[:, 144 + 128 * i:272 + 128 * i].rearrange("p (q e) -> p q e", e=NEXP)
                                   for i in range(5))
        rt = tabs[:, 784:1024]
        pos = sb("pos", [P, 2, QT])
        prel = sb("prel", [P, 2, QT])
        wts = sb("wts", [P, 2, QT])
        posi = sb("posi", [P, 2 * QT], I32)
        idxi = sb("idxi", [P, 2], I32)
        ovi = sb("ovi", [P, 16], I32)
        Ab = sb("Ab", [P, QT, NEXP], BF16)
        Ob = [sq2[:, u, 0:256].bitcast(BF16).rearrange("p (q s) -> p q s", s=P) for u in range(2)]
        hsilu = ftmp[:, 0, :]
        MS = {k: ctx.enter_context(nc.semaphore("m_" + k)) for k in (
            "gather", "lgT", "lgs", "tr", "te", "hd", "lg", "rq", "rp", "A", "rk", "ro", "odh",
            "od", "ix", "ii", "xt", "xea", "xev", "sl", "hm", "ht", "he", "hl", "yea", "yev", "gf", "fa", "fs", "ff",
            "useG", "useU", "useD", "highG", "highU", "highD", "vlowG", "vlowU", "vlowD", "glowG", "glowU", "glowD")}
        MS.update({k: [ctx.enter_context(nc.semaphore(f"m_{k}{u}")) for u in range(n)]
                   for k, n in (("xg", 2), ("wG", 2), ("wU", 2), ("wD", 2), ("yd", 2), ("yg", QT))})

        def lin(i, u, mult=1, c=0):
            v = i * (2 * mult) + (u * mult + c)
            return max(v, 0) if isinstance(v, int) else v

        def dma_of(i, u):
            v = (i + u // 2) * 16 + 16
            return max(v, 0) if isinstance(v, int) else v

        def blocks(eng, body, first, end):
            body(first // 2, 0, False, True)
            body(first // 2, 1, True, True)
            with eng.Fori(first // 2 + 1, end // 2 - 1) as i:
                body(i, 0, True, True)
                body(i, 1, True, True)
            body(end // 2 - 1, 0, True, True)
            body(end // 2 - 1, 1, True, False)

        def overflow(eng):
            return eng.If(eng.value_load(ovi[0:1, 8:9], min_val=0, max_val=OVER) > 0)

        def nth(name, l, n):
            return l * EV[name] + (n + CREDIT.get(name, 0))

        def nsa_items():
            items = []
            for qt in range(QT):
                q = slice(qt * P, qt * P + P)
                this = []
                for g in range(2):
                    half = slice(64 * g, 64 * g + 64)
                    sc = [(0, P, ident_b, maskb[:, 2 * P + qt * P:3 * P + qt * P])]
                    for j in range(4):
                        sc.append((32 * j, 32 * j + CMP_N, qr[half, j, q], kcr[half, 0:CMP_N]))
                    pv = [(PS[:, 7, 256 * g:256 * g + 256], 0, VC[:, g].rearrange("p j d -> p (j d)"), True, True)]
                    this.append(dict(kind="cmp", n=P, sc=sc, nb=1, pv=pv, L=Lt[:, qt % 2, 4 * g:4 * g + 4]))
                for br in range(2):
                    for h in range(HEADS):
                        g = h // 4
                        half = slice(64 * g, 64 * g + 64)
                        n = P * (qt + 1)
                        sc = [(0, n, qr[half, h % 4, q], kr[half, br, 0:n]), (n - P, n, ident_b, causal_b)]
                        pv = [(PS[:, 5 + br, 64 * h:64 * h + 64], kb,
                               Vn[:, kb, 128 * br + 64 * g:128 * br + 64 * g + 64], kb == 0, kb == qt)
                              for kb in range(qt + 1)]
                        this.append(dict(kind="full", n=n, sc=sc, nb=qt + 1, pv=pv,
                                         L=Lt[:, qt % 2, 8 + 8 * br + h:9 + 8 * br + h]))
                this[0]["first"] = qt
                this[-1]["last"] = qt
                mix = dict(kind="mix", mixn=qt, nb=4, src=mixtok,
                           dst=mixT[:, 4:8, (qt - 1) * P:qt * P])
                items += this[:7] + ([mix] if qt else []) + this[7:]
            items += [None, dict(kind="mix", mixn=QT, nb=4, src=mixtok, dst=mixT[:, 4:8, (QT - 1) * P:QT * P])]
            return number(items)

        def causal_item(kind, qt, q, kk, pv, L, extra=()):
            n = P * (qt + 1)
            sc = [(0, n, q, kk)] + list(extra) + [(n - P, n, ident_b, causal_b)]
            return dict(kind=kind, n=n, sc=sc, nb=qt + 1, pv=pv, L=L)

        def block2_items():
            items = []
            for qt in range(QT):
                qs, n = slice(qt * P, qt * P + P), P * (qt + 1)
                this = []
                for h in range(8):
                    half = slice(64 * (h % 2), 64 * (h % 2) + 64)
                    pv = [(PS[:, 5, 64 * h:64 * h + 64], kb, fv[:, kb, 64 * h:64 * h + 64], kb == 0, kb == qt)
                          for kb in range(qt + 1)]
                    this.append(causal_item("full", qt, fq[half, h // 2, qs], fk[half, h // 2, 0:n], pv,
                                            Lt[:, qt % 2, h:h + 1], [(0, n, sel[:, h, :], negc[:, 0:n])]))
                for i in range(4):
                    for c in range(2):
                        half = slice(64 * c, 64 * c + 64)
                        pv = [(PS[:, 6 + c, P * i:P * i + P], kb, dv[:, kb, P * i:P * i + P], kb == 0, kb == qt)
                              for kb in range(qt + 1)]
                        this.append(causal_item("full", qt, dq[half, i, qs], dk[half, i, 0:n], pv,
                                                Lt[:, qt % 2, 8 + 4 * c + i:9 + 4 * c + i]))
                this[0]["first"] = qt
                this[-1]["last"] = qt

                def mixes(q):
                    s = slice(q * P, q * P + P)
                    return [dict(kind="mix", mixn=2 * q + 1, nb=4, src=ftmp[:, 0, :], dst=slice(0, 4), cols=s),
                            dict(kind="mix", mixn=2 * q + 2, nb=4, src=ftmp[:, 1, :], dst=slice(4, 8), cols=s,
                                 sub=True)]
                items += this[:8] + (mixes(qt - 1) if qt else []) + this[8:]
            items += [None] * 5 + mixes(QT - 1)
            return number(items)

        def cross_items(k0, t0):
            items = []
            for qt in range(QT):
                this = []
                for h in range(4):
                    half = slice(64 * (h % 2), 64 * (h % 2) + 64)
                    pv = [(PS[:, 5, 64 * h:64 * h + 64], kb, cvt[:, kb, 64 * h:64 * h + 64], kb == 0, kb == 1)
                          for kb in range(2)]
                    this.append(dict(kind="full", n=MEM, nb=2, pv=pv, L=Lt[:, qt % 2, h:h + 1],
                                     sc=[(0, MEM, cqT[half, h // 2, qt * P:qt * P + P], ckT[half, h // 2, :])]))
                this[0]["first"] = 4 + qt
                this[-1]["last"] = qt

                def mix(q):
                    return dict(kind="mix", mixn=8 + q + 1, nb=2, src=ftmp[:, 0, 0:256], dst=coT[:, :, q * P:q * P + P])
                items += this[:3] + ([mix(qt - 1)] if qt else []) + this[3:]
            items += [None, mix(QT - 1)]
            return number(items, k0, t0)

        def number(items, k0=0, t0=0):
            k, t = k0, t0
            for it in items:
                if it is None:
                    continue
                it["t"] = t
                t += 1
                if it["kind"] != "mix":
                    it["k"] = k
                    k += 1
            byk = {it["k"]: it for it in items if it and "k" in it}
            for it in items:
                if it and it.get("k", 0) >= k0 + 3:
                    it["t3"] = byk[it["k"] - 3]["t"]
                    it["sum3"] = byk[it["k"] - 3]["kind"] == "cmp"
                if it and "t" in it:
                    j = [x for x in items if x and x["t"] == it["t"] - 2 and x["kind"] != "mix"]
                    if j:
                        it["pv2"] = j[0]["k"]
            return items

        NSA = nsa_items()
        BL2 = block2_items()
        CROSS = cross_items(64, 72)
        LAG_T, LAG_V = 3, 4

        block = ctx.enter_context(nc.Block())

        @block.sync
        def _(sp):
            sp.dma_start(xT[:, :, :], xT_in.rearrange("c p t -> p c t")).then_inc(s_in, 16)
            sp.dma_start(mats[:, :], tabs_in[:, 2 * T:2 * T + 5 * P + 1]).then_inc(s_in, 16)
            sp.dma_start(cols[:, :, :], cols_in).then_inc(s_in, 16)
            sp.dma_start(misc_all[:, :, :], misc_in).then_inc(s_in, 16)

            def load_tiles(first, end):
                with sp.Fori(first // RING, end // RING) as i:
                    for s in range(RING):
                        sp.wait_ge(sems["tile"], i * RING + (s + 1))
                        sp.dma_start(ring[:, s, :], ring_w[i * RING + s]).then_inc(slot[s], 16)

            load_tiles(0, RING)
            sp.dma_start(tabs[:, :], tabs_in[:, 0:2 * T]).then_inc(s_tab, 16)
            sp.dma_start(maskb[:, :].bitcast(mybir.dt.uint16), masks_in).then_inc(s_tab, 16)
            load_tiles(RING, PARAMS2_AT)
            sp.dma_start(par[:, 0:M_END], par_in).then_inc(sems["b_in"], 16)
            sp.dma_start(gtmp[:, 0:T].bitcast(I32), pos_in).then_inc(sems["b_in"], 16)
            sp.dma_start(memn[:, :, :], memT_in).then_inc(sems["b_in"], 16)
            load_tiles(PARAMS2_AT, NTILES)
            sp.wait_ge(sems["xs"], nth("xs", DEPTH, 8))

            def load(w, i, u, e):
                for h in range(2):
                    sp.wait_ge(MS["use" + w], lin(i, u, 2, h - 1))
                    src = {"G": w_gate, "U": w_up, "D": w_down}[w][e].rearrange("(k p) n -> p k n", p=P)
                    n, lo = src.shape[1] // 2, LOADED[w] + 2048 * h
                    sp.dma_start(arena[:, lo:lo + 2048].rearrange("p (k n) -> p k n", k=n), src[:, n * h:n * h + n, :]
                                 ).then_inc(MS["w" + w][h], 16)

            def store_y(i, u):
                sp.wait_ge(MS["yea"], lin(i, u, 1, 1))
                sp.wait_ge(MS["yev"], lin(i, u, 1, 1))
                sp.dma_start(y_dram[i + u // 2, u % 2], ysb[u % 2]).then_inc(MS["yd"][u % 2], 16)

            def feed(i, u, expert, prev, next_):
                if prev:
                    load("U", i, u, expert(0))
                    if prev != "first":
                        store_y(i, u - 2)
                        load("D", i, u - 1, expert(-1))
                if next_:
                    load("G", i, u + 1, expert(1))

            def first_loads(i, e):
                for w in "GUD":
                    load(w, i, 0, e)

            first_loads(0, 0)
            feed(0, 0, lambda d: d, False, True)
            feed(0, 1, lambda d: 1 + d, "first", True)
            with sp.Fori(1, NEXP // 2 - 1) as i:
                for u in range(2):
                    feed(i, u, lambda d: i * 2 + (u + d), True, True)
            i = NEXP // 2 - 1
            feed(i, 0, lambda d: NEXP - 2 + d, True, True)
            feed(i, 1, lambda d: NEXP - 1 + d, True, False)
            store_y(i, 0)
            load("D", i, 1, NEXP - 1)
            store_y(i, 1)
            sp.wait_ge(MS["ro"], 1)
            with overflow(sp):
                ex = [sp.value_load(ovi[0:1, j:j + 1], min_val=0, max_val=NEXP - 1) for j in range(OVB)]
                i = NEXP // 2
                first_loads(i, ex[0])
                for j in range(OVB):
                    feed(i, j, lambda d: ex[j + d], False if j == 0 else "first" if j == 1 else True, j + 1 < OVB)
                store_y(i, OVB - 2)
                load("D", i, OVB - 1, ex[OVB - 1])
                store_y(i, OVB - 1)
                sp.wait_ge(MS["yd"][(OVB - 2) % 2], dma_of(i, OVB - 2))
                sp.wait_ge(MS["yd"][(OVB - 1) % 2], dma_of(i, OVB - 1))
            sp.wait_ge(MS["yd"][0], dma_of(NEXP // 2 - 1, 0))
            sp.wait_ge(MS["yd"][1], dma_of(NEXP // 2 - 1, 1))
            for qt in range(QT):
                sp.wait_ge(MS["ff"], qt + 1)
                sp.dma_start(out[qt], yg[2 * qt]).then_inc(s_out, 16)
            sp.wait_ge(s_out, 16 * QT)

        @block.gpsimd
        def _(pool):
            def split(base, t):
                pool.wait_ge(slot[t % RING], base * (16 // RING) + 16 * (t // RING + 1))
                pool.wait_ge(sems["tile"], base + (t - 1 + RING))
                pool.sem_inc(g_ch, 1)
                nc.gpsimd.tensor_scalar(whi[:, t % 2, :], ring[:, t % RING, :], 1.0, 0.0, ALU.mult, ALU.add
                                        ).then_inc(sems["whi"], 1)
                pool.wait_ge(sems["whi"], base + (t + 1))
                nc.gpsimd.tensor_tensor(wlo[:, t % RING, :], ring[:, t % RING, :], whi[:, t % 2, :], ALU.subtract
                                        ).then_inc(sems["split"], 1)

            def unsplit(base, t):
                pool.wait_ge(slot[t % RING], base * (16 // RING) + 16 * (t // RING + 1))
                pool.wait_ge(sems["split"], base + t)
                pool.sem_inc(sems["whi"], 1)
                pool.sem_inc(sems["split"], 1)

            def decayed(l, h):
                pool.wait_ge(sems["eexp"], nth("eexp", l, h + 1))
                pool.wait_ge(sems["evac"], nth("evac", l, 5 + h))
                for j in range(LEVELS):
                    w = 64 >> j
                    e = E[:, j, :].rearrange("p (n two w) -> p n two w", two=2, w=w)
                    kv = kT[:, h, :].rearrange("p (n two w) -> p n two w", two=2, w=w)
                    qv = qT[:, h, :].rearrange("p (n two w) -> p n two w", two=2, w=w)
                    nc.gpsimd.tensor_tensor(e[:, :, 0, :], e[:, :, 0, :], kv[:, :, 0, :], ALU.mult)
                    ins = nc.gpsimd.tensor_tensor(e[:, :, 1, :], e[:, :, 1, :], qv[:, :, 1, :], ALU.mult)
                ins.then_inc(sems["e"], 1)

            with pool.Fori(0, DEPTH) as l:
                base = l * T_LAYER
                for t in range(T_FFI):
                    if t in DECAYED_AT:
                        decayed(l, DECAYED_AT.index(t))
                    (unsplit if T_CMP <= t < T_WO else split)(base, t)
                split(base, T_FFI)
                split(base, T_FFI + 1)
                with pool.Fori(0, 16) as j:
                    for u in range(4):
                        split(base + j * 4, T_FFI + 2 + u)
            with pool.Fori(0, 6) as j:
                for u in range(4):
                    split(j * 4 + DEPTH * T_LAYER, u)
            for t in range(B_CK, B_GA):
                unsplit(DEPTH * T_LAYER, t)
            with pool.Fori(0, (B_TILES - B_GA) // 4) as j:
                for u in range(4):
                    split(j * 4 + DEPTH * T_LAYER, B_GA + u)

            def gather(i, u):
                pool.wait_ge(MS["ii"], lin(i, u, 1, 1))
                pool.wait_ge(MS["xt"], lin(i, u, 1, -1))
                pool.sem_inc(MS["gather"], 1)
                pool.indirect_dma_start(xg[u % 2], None, hm_dram, bass.IndirectOffsetOnAxis(
                    ap=idxi[:, u % 2:u % 2 + 1], axis=0)).then_inc(MS["xg"][u % 2], 16)

            pool.wait_ge(MS["hd"], 16 * QT)
            gather(0, 0)
            gather(0, 1)

            def lows(w, i, u):
                for k in (1, 3):
                    pool.wait_ge(MS["high" + w], lin(i, u, 4, k + 1))
                    nc.gpsimd.tensor_tensor(low(w, k), loaded(w, k), high(w, k), ALU.subtract
                                            ).then_inc(MS["glow" + w], 1)

            def moe_g(i, u, prev, next_):
                gather(i, u + 2)
                lows("U", i, u)
                if prev:
                    lows("D", i, u - 1)
                if next_:
                    lows("G", i, u + 1)

            lows("G", 0, 0)
            blocks(pool, moe_g, 0, NEXP)
            lows("D", NEXP // 2 - 1, 1)

            def back(rows):
                for qt in range(QT):
                    for k in range(2):
                        pool.indirect_dma_start(yg[2 * qt + k], None, y_dram[0:rows // (2 * P)].rearrange(
                            "a b p d -> (a b p) d"), bass.IndirectOffsetOnAxis(
                                ap=posi[:, QT * k + qt:QT * k + qt + 1], axis=0)).then_inc(MS["yg"][qt], 16)

            pool.wait_ge(MS["yd"][0], dma_of(NEXP // 2 - 1, 0))
            pool.wait_ge(MS["yd"][1], dma_of(NEXP // 2 - 1, 1))
            with overflow(pool):
                lows("G", NEXP // 2, 0)
                blocks(pool, moe_g, NEXP, NEXP + OVB)
                lows("D", (NEXP + OVB) // 2 - 1, 1)
                pool.wait_ge(MS["yd"][0], dma_of((NEXP + OVB) // 2 - 1, 0))
                pool.wait_ge(MS["yd"][1], dma_of((NEXP + OVB) // 2 - 1, 1))
                back(YROWS)
            with pool.Else():
                back(NEXP * P)

        @block.scalar
        def _(act_e):
            def ln_exp_tables():
                if tables["set"] != "ln exp":
                    act_e.preload_act_table_set("natural_log_exp_and_others")
                tables["set"] = "ln exp"

            tables = {"set": None}

            def norm_rstd(l, n, hn, m, src=xT, w=T, bank=0):
                ln_exp_tables()
                for c in range(KO):
                    if hn is not None:
                        act_e.wait_ge(sems["h"], nth("h", l, 8 * hn + c + 1 - 8))
                    i = 8 * n + c
                    if c >= 2:
                        act_e.wait_ge(sems["sqsum"], nth("sqsum", l, i - 1))
                    nc.scalar.activation(sq2[:, c % 2, 0:w], src[:, c, :], ACT.Square).then_inc(sems["sq"], 1)
                act_e.wait_ge(sems["sqsum"], nth("sqsum", l, 8 * n + 8))
                nc.scalar.activation(lnb[:, 0:w], PS[:, bank, 0:w], ACT.Ln, bias=eps[:, 0:1]).then_inc(a_ch, 1)
                act_e.wait_ge(a_ch, a_step())
                nc.scalar.activation(rstd[:, 0:w], lnb[:, 0:w], ACT.Exp, scale=-0.5).then_inc(sems["rstd"], 1)
                if m is not None:
                    for c in range(KO):
                        act_e.wait_ge(sems["xr"], nth("xr", l, 8 * m + c + 1))
                        nc.scalar.activation(xh[:, c, :], xr[:, c, :], ACT.Identity).then_inc(sems["xh"], 1)

            ch = {"base": 0, "n": 0}

            def a_step():
                ch["n"] += 1
                return ch["base"] + ch["n"]

            def head_squares(l, h):
                if h >= 2:
                    act_e.wait_ge(sems["hst"], nth("hst", l, h - 1))
                nc.scalar.activation(sq2[:, h % 2, :], mixT[:, h, :], ACT.Square).then_inc(sems["hsq"], 1)

            def rope_evac(l, r, src, n):
                if r >= 2:
                    act_e.wait_ge(sems["qn"], nth("qn", l, r - 1))
                gain = lcol[:, C_QG:C_QG + 1] if r < 4 else lcol[:, C_KG + (r - 3) % 3:C_KG + (r - 3) % 3 + 1]
                nc.scalar.activation(qg[:, r % 2, 0:n], src, ACT.Identity, scale=gain)
                return nc.scalar.activation(sq2[:, r % 2, 0:n], src, ACT.Square)

            def evac(l, t):
                act_e.wait_ge(sems["tile"], nth("tile", l, tile_of(t) + 1))
                src = PS[:, t % 2, :]
                if t < 12:
                    tables["set"] = None
                if t < 4:
                    ins = nc.scalar.activation(kT[:, t, :], src, ACT.Sigmoid)
                elif t < 8:
                    ins = nc.scalar.activation(qT[:, t - 4, :], src, ACT.Silu)
                elif t < 12:
                    ins = nc.scalar.activation(sgT[:, t - 8, :], src, ACT.Silu)
                elif t < 18:
                    ins = rope_evac(l, t - 12, src, T)
                else:
                    ins = nc.scalar.activation(craw[:, t - 18, :], src, ACT.Identity)
                ins.then_inc(sems["evac"], 1)

            def step(l, kind, i):
                if kind == "norm":
                    norm_rstd(l, i, i, i)
                    if i == 0:
                        act_e.wait_ge(sems["params"], nth("params", l, 2))
                elif kind == "feat":
                    evac(l, i)
                elif kind == "gate_h":
                    ln_exp_tables()
                    act_e.wait_ge(sems["f"], nth("f", l, i + 1))
                    nc.scalar.activation(ftmp[:, i % 2, :], ftmp[:, i % 2, :], ACT.Ln).then_inc(sems["ln"], 1)
                elif kind == "scan":
                    ln_exp_tables()
                    act_e.wait_ge(sems["kd"], nth("kd", l, i + 1))
                    if i >= 2:
                        act_e.wait_ge(sems["qk"], nth("qk", l, i - 1))
                    nc.scalar.activation(ebuf[:, i % 2, :], bT[:, i, :], ACT.Exp)
                    nc.scalar.activation(kdb[:, i % 2, :], kdb[:, i % 2, :], ACT.Exp).then_inc(sems["kqexp"], 1)
                elif kind == "decay":
                    ln_exp_tables()
                    act_e.wait_ge(sems["ediff"], nth("ediff", l, i + 1))
                    nc.scalar.activation(E[:, :, :], E[:, :, :], ACT.Exp).then_inc(sems["eexp"], 1)
                elif kind == "hi":
                    act_e.wait_ge(sems["tile"], nth("tile", l, T_HI + 4))
                    for st in range(4):
                        nc.scalar.activation(Vh[:, st, :], PS[:, 2 + st, :], ACT.Identity).then_inc(sems["vh"], 1)
                elif kind == "v":
                    act_e.wait_ge(sems["tile"], nth("tile", l, T_V + 2))
                    for st in range(4):
                        nc.scalar.activation(Vn[:, st, :], PS[:, 2 + st, 0:256], ACT.Identity).then_inc(sems["vn"], 1)
                elif kind == "rs":
                    n = T if i < 6 else CMP_N
                    ln_exp_tables()
                    act_e.wait_ge(sems["stat"], nth("stat", l, i + 1))
                    act_e.wait_ge(sems["rrstd"], nth("rrstd", l, i))
                    nc.scalar.activation(lnb[:, 0:n], PS[:, 6, 0:n], ACT.Ln, bias=eps[:, 0:1]).then_inc(a_ch, 1)
                    act_e.wait_ge(a_ch, a_step())
                    nc.scalar.activation(rrs[:, i % 2, 0:n], lnb[:, 0:n], ACT.Exp, scale=-0.5
                                         ).then_inc(sems["rrstd"], 1)
                elif kind == "gatem":
                    act_e.wait_ge(sems["gatem"], nth("gatem", l, 1))
                    tables["set"] = None
                    act_e.wait_ge(sems["kqexp"], nth("kqexp", l, 4))
                    nc.scalar.activation(ftmp[0:24, 0, :], PS[0:24, 2, :], ACT.Sigmoid).then_inc(sems["gate"], 1)
                elif kind == "gatet":
                    act_e.wait_ge(sems["gatet"], nth("gatet", l, 1))
                    nc.scalar.activation(gates[:, :, :], PS[:, 5, :].rearrange("p (a b) -> p a b", b=P)[:, :, 0:24],
                                         ACT.Identity).then_inc(sems["gates"], 1)
                elif kind == "cmph":
                    act_e.wait_ge(sems["tile"], nth("tile", l, T_CMP + 8))
                    tables["set"] = None
                    for kv in range(2):
                        for hc in range(2):
                            nc.scalar.activation(hid[:, kv, hc, :], PS[:, 2 + 2 * kv + hc, 0:62], ACT.Silu
                                                 ).then_inc(sems["hid"], 1)
                elif kind == "cmpo":
                    act_e.wait_ge(sems["kc"], nth("kc", l, 1))
                    rope_evac(l, 6, PS[:, 2, 0:CMP_N], CMP_N).then_inc(sems["kce"], 1)
                elif kind == "ket":
                    act_e.wait_ge(sems["ket"], nth("ket", l, i + 1))
                    nc.scalar.activation(keT[:, i, :, :], PS[:, 2 + i, :].rearrange("p (a b) -> p a b", b=P),
                                         ACT.Identity).then_inc(sems["kec"], 1)
                elif kind == "state":
                    act_e.wait_ge(sems["osum"], nth("osum", l, i + 1))
                    nc.scalar.activation(mixT[:, 0:4, i * P:(i + 1) * P],
                                         PS[:, 6 + i % 2, :].rearrange("p (a b) -> p a b", b=P),
                                         ACT.Identity).then_inc(sems["oc"], 1)
                elif kind == "hn":
                    ln_exp_tables()
                    if i == 0:
                        act_e.wait_ge(sems["oc"], nth("oc", l, 4))
                        head_squares(l, 0)
                    if i < 3:
                        head_squares(l, i + 1)
                    act_e.wait_ge(sems["hst"], nth("hst", l, i + 1))
                    if i >= 1:
                        act_e.wait_ge(sems["hrs"], nth("hrs", l, i))
                    if i >= 2:
                        act_e.wait_ge(sems["hn"], nth("hn", l, i - 1))
                    nc.scalar.activation(lnb[:, :], PS[:, i % 2, :], ACT.Ln, bias=eps[:, 0:1]).then_inc(a_ch, 1)
                    act_e.wait_ge(a_ch, a_step())
                    nc.scalar.activation(rrs[:, i % 2, :], lnb[:, :], ACT.Exp, scale=-0.5).then_inc(sems["hrs"], 1)
                elif kind == "attention":
                    attend(l, NSA)
                elif kind == "ffn":
                    def body(j):
                        for u in range(2):
                            act_e.wait_ge(sems["tile"], l * T_LAYER + j * 4 + (T_FFI + 2 * u + 1 + RING))
                            act_e.wait_ge(sems["act"], l * FFC + j * 2 + (u + 1))
                            nc.scalar.activation(sq2[:, u, :], PS[:, 2 * u, :], ACT.Silu).then_inc(sems["silu"], 1)
                    tables["set"] = None
                    with act_e.Fori(0, FFC // 2) as j:
                        body(j)

            def step2(kind, i):
                l = DEPTH
                if kind == "norm":
                    norm_rstd(l, *NORMS2[i], **(dict(src=memn, w=MEM, bank=6) if i == 1 else {}))
                elif kind == "trig":
                    act_e.wait_ge(sems["trig"], nth("trig", 0, 1))
                    tables["set"] = None
                    nc.scalar.activation(tabs[:, :], tabs[:, :], ACT.Sin).then_inc(sems["trigs"], 1)
                elif kind == "lam":
                    act_e.wait_ge(sems["lam"], nth("lam", 0, 1))
                    nc.scalar.activation(small[:, 0:2], small[:, 0:2], ACT.Exp).then_inc(sems["lams"], 1)
                elif kind == "feat":
                    act_e.wait_ge(sems["tile"], nth("tile", l, tile2_of(i) + 1))
                    src = PS[:, i % 2, :]
                    if i < 4:
                        ins = nc.scalar.activation(fq[:, i, :], src, ACT.Identity, scale=0.125)
                    elif i < 8:
                        ins = nc.scalar.activation(fk[:, i - 4, :], src, ACT.Identity)
                    elif i < 16:
                        r = i - 8
                        act_e.wait_ge(sems["rope"], nth("rope", l, max(r - 1, 0)))
                        ins = nc.scalar.activation(qnb[:, r % 2, :], src, ACT.Identity, scale=0.125 if r < 4 else 1.0)
                    elif i < 18:
                        ins = nc.scalar.activation(ckT[:, i - 16, :], src[:, 0:MEM], ACT.Identity)
                    elif i < 34:
                        tables["set"] = None
                        ins = nc.scalar.activation(sga[:, i - 18, :], src, ACT.Sigmoid)
                    else:
                        ins = nc.scalar.activation(cqT[:, i - 34, :], src, ACT.Identity, scale=0.125)
                    ins.then_inc(sems["evac"], 1)
                elif kind == "flog":
                    act_e.wait_ge(sems["fl"], nth("fl", 0, 1))
                    nc.scalar.activation(lnb[0:8, :], PS[0:8, 6, :], ACT.Identity, bias=par[0:8, M_BF:M_BF + 1]
                                    ).then_inc(a_ch, 1)
                    act_e.wait_ge(a_ch, a_step())
                    nc.scalar.activation(qg[0:8, 0, :], lnb[0:8, :], ACT.Abs).then_inc(a_ch, 1)
                    act_e.wait_ge(a_ch, a_step())
                    nc.scalar.activation(qg[0:8, 0, :], qg[0:8, 0, :], ACT.Exp, scale=-1.0).then_inc(a_ch, 1)
                    act_e.wait_ge(a_ch, a_step())
                    nc.scalar.activation(qg[0:8, 1, :], qg[0:8, 0, :], ACT.Ln, bias=one[0:8, :]
                                         ).then_inc(sems["fls"], 1)
                elif kind == "tok":
                    t0, nt, dst, sem = TOK2[i]
                    act_e.wait_ge(sems["tile"], nth("tile", l, t0 + nt))
                    buf = {"fv": fv, "dv": dv, "cv": cvt}[sem]
                    n, w = (4, T) if sem != "cv" else (2, MEM)
                    for st in range(n):
                        nc.scalar.activation(buf[:, st, :], PS[:, 2 + st, 0:w], ACT.Identity).then_inc(sems[sem], 1)
                elif kind == "sel":
                    act_e.wait_ge(sems["rope"], nth("rope", l, 8))
                    act_e.dma_start(sel, sel_in).then_inc(sems["sel"], 16)
                elif kind == "attention":
                    attend(l, BL2)
                elif kind == "cross":
                    attend(l, CROSS)

            def attend(l, items):
                ln_exp_tables()
                for s in range(len(items) + 5):
                    last = items[s - LAG_V - 1] if 0 <= s - LAG_V - 1 < len(items) else None
                    if items is BL2 and last and "last" in last:
                        act_e.wait_ge(sems["ms"], nth("ms", 0, last["last"] + 1))
                        nc.scalar.activation(small[:, 4:8], small[:, 4:8], ACT.Ln, scale=1.0 / P,
                                                   bias=eps[:, 1:2]).then_inc(a_ch, 1)
                        act_e.wait_ge(a_ch, a_step())
                        nc.scalar.activation(small[:, 8:12], small[:, 4:8], ACT.Exp, scale=-0.5
                                             ).then_inc(sems["msr"], 1)
                    it = items[s] if s < len(items) else None
                    if it is None or it["kind"] == "mix":
                        continue
                    k = it["k"]
                    act_e.wait_ge(sems["mx"], nth("mx", l, k + 1))
                    if "t3" in it:
                        act_e.wait_ge(sems["tr"], nth("tr", l, it["t3"] + 1))
                        if it["sum3"]:
                            act_e.wait_ge(sems["pt"], nth("pt", l, it["t3"] + 1))
                    if it["kind"] == "cmp":
                        ins = nc.scalar.activation(Pr[k % 3][:, 0:P], Pr[k % 3][:, 0:P], ACT.Exp)
                    else:
                        n = it["n"]
                        ins = nc.scalar.activation(Pr[k % 3][:, 0:n], PS[:, k % 3, 0:n], ACT.Exp,
                                                   bias=nmx[:, k % 4, 0:1], accum_out=it["L"])
                    ins.then_inc(sems["p"], 1)

            act_e.wait_ge(s_in, 16 * NIN)
            act_e.wait_ge(s_pre, 2)
            nc.scalar.activation(lb[:, 1, :], lbl[:, 0:4], ACT.Sigmoid).then_inc(s_pre, 1)
            with act_e.Fori(0, DEPTH) as l:
                ch["n"] = 0
                ch["base"] = l * A_CH
                tables["set"] = None
                ln_exp_tables()
                for kind, i in STEPS:
                    step(l, kind, i)
                assert ch["n"] == A_CH, ch["n"]
            ch["n"] = 0
            ch["base"] = DEPTH * A_CH
            tables["set"] = None
            ln_exp_tables()
            act_e.wait_ge(sems["b_in"], 48)
            for kind, i in STEPS2:
                step2(kind, i)

            act_e.wait_ge(sems["h"], nth("h", DEPTH, 16))
            act_e.wait_ge(MS["lgT"], 1)
            nc.scalar.activation(lnb[0:36, :], PS[0:36, 0, :], ACT.Identity).then_inc(MS["lgs"], 1)
            for g in range(16):
                act_e.wait_ge(MS["tr"], g + 1)
                qt, half = g % 8 // 2, g % 2
                dst = (hmt[qt] if g < 8 else xtok[:, qt, :])[:, half * T:half * T + T]
                nc.scalar.activation(dst, PS[:, 4 + g % 4, :], ACT.Identity).then_inc(MS["te"], 1)
                if g < 8 and half:
                    act_e.wait_ge(MS["te"], g + 1)
                    act_e.dma_start(hm_dram[qt * P:qt * P + P, :], hmt[qt]).then_inc(MS["hd"], 16)
            act_e.wait_ge(MS["hd"], 16 * QT)
            act_e.dma_start(gfin, gfin_in).then_inc(MS["gf"], 16)
            act_e.wait_ge(MS["rq"], 1)
            nc.scalar.activation(rt[:, 0:16], rt[:, 0:16], ACT.Exp).then_inc(MS["rp"], 1)
            act_e.wait_ge(MS["rq"], 2)
            nc.scalar.activation(rt[:, 20:24], rt[:, 20:24], ACT.Exp).then_inc(MS["rp"], 1)

            def highs(w, i, u):
                for k in range(4):
                    act_e.wait_ge(MS["w" + w][k // 2], lin(i, u, 16, 16))
                    nc.scalar.activation(high(w, k), loaded(w, k), ACT.Identity).then_inc(MS["high" + w], 1)

            def xgt_a(i, u):
                act_e.wait_ge(MS["xt"], lin(i, u, 1, 1))
                act_e.wait_ge(MS["useU"], lin(i, u, 2, -2))
                nc.scalar.activation(xgT[u % 2][0], PS[:, 0:2, :].rearrange("p c (a b) -> p (c a) b", b=P),
                                     ACT.Identity).then_inc(MS["xea"], 1)

            def silu(i, u):
                act_e.wait_ge(MS["useG"], lin(i, u, 2, 2))
                act_e.wait_ge(MS["hm"], lin(i, u, 1, 0))
                nc.scalar.activation(hsilu, PS[:, 2, :], ACT.Silu).then_inc(MS["sl"], 1)

            def ht_copy(i, u):
                act_e.wait_ge(MS["ht"], lin(i, u, 1, 1))
                act_e.wait_ge(MS["useD"], lin(i, u, 2, -2))
                nc.scalar.activation(hT[u % 2][0], PS[:, 4, :].rearrange("p (a b) -> p a b", b=P), ACT.Identity
                                     ).then_inc(MS["he"], 1)

            def y_a(i, u):
                act_e.wait_ge(MS["useD"], lin(i, u, 2, 2))
                act_e.wait_ge(MS["yd"][(u - 2) % 2], dma_of(i, u - 2))
                nc.scalar.activation(ysb[u % 2][:, 0:T], PS[:, 5, :], ACT.Identity).then_inc(MS["yea"], 1)

            def moe_a(i, u, prev, next_):
                xgt_a(i, u + 1)
                if prev:
                    ht_copy(i, u - 1)
                highs("U", i, u)
                if prev:
                    highs("D", i, u - 1)
                silu(i, u)
                if next_:
                    highs("G", i, u + 1)
                if prev:
                    y_a(i, u - 1)

            def last_a(i):
                ht_copy(i, 1)
                highs("D", i, 1)
                y_a(i, 1)

            highs("G", 0, 0)
            xgt_a(0, 0)
            blocks(act_e, moe_a, 0, NEXP)
            last_a(NEXP // 2 - 1)
            with overflow(act_e):
                highs("G", NEXP // 2, 0)
                blocks(act_e, moe_a, NEXP, NEXP + OVB)
                last_a((NEXP + OVB) // 2 - 1)
            for qt in range(QT):
                act_e.wait_ge(MS["fa"], qt + 1)
                nc.scalar.activation(yg[2 * qt + 1], yg[2 * qt], ACT.Square, accum_out=small[:, qt:qt + 1]
                                ).then_inc(a_ch, 1)
                act_e.wait_ge(a_ch, a_step())
                nc.scalar.activation(small[:, 4 + qt:5 + qt], small[:, qt:qt + 1], ACT.Ln, scale=1.0 / D,
                                           bias=eps[:, 0:1]).then_inc(a_ch, 1)
                act_e.wait_ge(a_ch, a_step())
                nc.scalar.activation(small[:, 8 + qt:9 + qt], small[:, 4 + qt:5 + qt], ACT.Exp, scale=-0.5
                                     ).then_inc(MS["fs"], 1)

        @block.vector
        def _(v):
            ch = {"base": 0, "n": 0}

            def v_step():
                ch["n"] += 1
                return ch["base"] + ch["n"]

            def low_parts(l, m):
                for c in range(KO):
                    v.wait_ge(sems["xh"], nth("xh", l, 8 * m + c + 1))
                    nc.vector.tensor_tensor(xl[:, c, :], xr[:, c, :], xh[:, c, :], ALU.subtract
                                            ).then_inc(sems["xn"], 1)

            def stream(l, k, tile, value):
                v.wait_ge(sems["tile"], tile)
                nc.vector.tensor_copy(xs[:, k % 2, 0, :], value).then_inc(v_ch, 1)
                v.wait_ge(v_ch, v_step())
                nc.vector.tensor_tensor(xs[:, k % 2, 1, :], value, xs[:, k % 2, 0, :], ALU.subtract
                                        ).then_inc(sems["xs"], 1)

            def step(l, kind, i):
                if kind == "norm":
                    v.wait_ge(sems["rstd"], nth("rstd", l, i + 1))
                    for c in range(KO):
                        g = (C_MIX if i == 0 else C_FFN) + c
                        nc.vector.scalar_tensor_tensor(out=xr[:, c, :], in0=xT[:, c, :], scalar=lcol[:, g:g + 1],
                                                       in1=rstd[:, :], op0=ALU.mult, op1=ALU.mult
                                                       ).then_inc(sems["xr"], 1)
                    low_parts(l, i)
                elif kind == "gate_h":
                    v.wait_ge(sems["evac"], nth("evac", l, i + 1))
                    nc.vector.tensor_scalar(ftmp[:, i % 2, :], kT[:, i, :], lcol[:, C_LB + 4 + i:C_LB + 5 + i],
                                                  lcol[:, C_LB + i:C_LB + i + 1], ALU.mult, ALU.add).then_inc(v_ch, 1)
                    v.wait_ge(v_ch, v_step())
                    nc.vector.tensor_scalar(kT[:, i, :], ftmp[:, i % 2, :], -1.0, 1.0, ALU.mult, ALU.add
                                            ).then_inc(sems["f"], 1)
                elif kind == "scan":
                    v.wait_ge(sems["ln"], nth("ln", l, i + 1))
                    if i >= 2:
                        v.wait_ge(sems["qk"], nth("qk", l, i - 1))
                    for c in range(QT):
                        ins = nc.vector.tensor_tensor_scan(
                            bT[:, i, c * P:c * P + P], one[:, :].broadcast_to([P, P]),
                            ftmp[:, i % 2, c * P:c * P + P], 0.0, ALU.mult, ALU.add)
                    ins.then_inc(v_ch, 1)
                    v.wait_ge(v_ch, v_step())
                    bv = bT[:, i, :].rearrange("p (c t) -> p c t", t=P)
                    kv = kdb[:, i % 2, :].rearrange("p (c t) -> p c t", t=P)
                    nc.vector.tensor_tensor(kv, bv[:, :, P - 1:P].broadcast_to([P, 4, P]), bv, ALU.subtract
                                            ).then_inc(sems["kd"], 1)
                elif kind == "decay":
                    if i >= 1:
                        v.wait_ge(sems["gram"], nth("gram", l, 4 * i))
                    for j in range(LEVELS):
                        w = 64 >> j
                        e = E[:, j, :].rearrange("p (n two w) -> p n two w", two=2, w=w)
                        bv = bT[:, i, :].rearrange("p (n two w) -> p n two w", two=2, w=w)
                        ref = bv[:, :, 0, w - 1:w].broadcast_to([P, T // (2 * w), w])
                        nc.vector.tensor_tensor(e[:, :, 0, :], ref, bv[:, :, 0, :], ALU.subtract)
                        ins = nc.vector.tensor_tensor(e[:, :, 1, :], bv[:, :, 1, :], ref, ALU.subtract)
                    ins.then_inc(sems["ediff"], 1)
                elif kind == "gram":
                    v.wait_ge(s_tab, 32)
                    for c in range(4):
                        n = 4 * i + c
                        v.wait_ge(sems["gram"], nth("gram", l, n + 1))
                        b = 2 + 2 * (n % 2)
                        nc.vector.tensor_tensor(gtmp[:, :], PS[:, b:b + 2, :].rearrange("p a b -> p (a b)"),
                                                      gmask, ALU.mult
                                                      ).then_inc(v_ch, 1)
                        v.wait_ge(v_ch, v_step())
                        nc.vector.tensor_reduce(AT[:, n, :], gtmp[:, :].rearrange("p (l t) -> p t l", t=P),
                                                AX.X, ALU.add).then_inc(sems["at"], 1)
                        v.wait_ge(sems["at"], nth("at", l, n + 1))
                elif kind == "qk":
                    v.wait_ge(sems["kqexp"], nth("kqexp", l, i + 1))
                    v.wait_ge(sems["e"], nth("e", l, i + 1))
                    v.wait_ge(sems["gram"], nth("gram", l, 4 * i + 4))
                    nc.vector.tensor_copy(ebl[:, i, :],
                                          ebuf[:, i % 2, :].rearrange("p (c t) -> p c t", t=P)[:, :, P - 1])
                    nc.vector.tensor_tensor(qT[:, i, :], qT[:, i, :], ebuf[:, i % 2, :], ALU.mult)
                    nc.vector.tensor_tensor(kT[:, i, :], kT[:, i, :], kdb[:, i % 2, :], ALU.mult
                                            ).then_inc(sems["qk"], 1)
                elif kind == "rs":
                    n = T if i < 6 else CMP_N
                    v.wait_ge(sems["rrstd"], nth("rrstd", l, i + 1))
                    if i >= 2:
                        v.wait_ge(sems["rope"], nth("rope", l, i - 1))
                    nc.vector.tensor_tensor(qnb[:, i % 2, 0:n], qg[:, i % 2, 0:n], rrs[:, i % 2, 0:n], ALU.mult
                                            ).then_inc(sems["qn"], 1)
                elif kind == "rr":
                    n = T if i < 6 else CMP_N
                    cs, sn = (cos, sin) if i < 6 else (cos[:, 31::16], sin[:, 31::16])
                    dst = qr[:, i, :] if i < 4 else kr[:, i - 4, :] if i < 6 else kcr[:, 0:CMP_N]
                    v.wait_ge(sems["rot"], nth("rot", l, i + 1))

                    if i == 6:
                        v.wait_ge(sems["dbuild"], nth("dbuild", l, 2))
                    nc.vector.tensor_tensor(gtmp[:, 0:n], PS[:, 7, 0:n], sn, ALU.mult)
                    nc.vector.tensor_tensor(gtmp[:, T:T + n], qnb[:, i % 2, 0:n], cs, ALU.mult).then_inc(v_ch, 1)
                    v.wait_ge(v_ch, v_step())
                    nc.vector.tensor_tensor(dst, gtmp[:, 0:n], gtmp[:, T:T + n], ALU.add).then_inc(sems["rope"], 1)
                    v.wait_ge(sems["rope"], nth("rope", l, i + 1))
                elif kind == "dbuild":
                    v.wait_ge(sems["evac"], nth("evac", l, 19 + i))
                    for part in range(2):
                        for g in range(2):
                            for hf in range(2):
                                src = craw[64 * g:64 * g + 64, i, :].rearrange("p (s j two) -> p s j two", j=8, two=2)
                                pc = C_PE + 32 * i + 16 * hf + 8 * part
                                pe = lcol[64 * g:64 * g + 64, pc:pc + 8].unsqueeze(1).broadcast_to([64, 32, 8])
                                dst = DB[64 * hf:64 * hf + 64, i, part, g, :].rearrange("p (s j) -> p s j", j=8)
                                ins = nc.vector.tensor_tensor(dst, src[:, :, :, hf], pe, ALU.add)
                    ins.then_inc(sems["dbuild"], 1)
                elif kind == "cmpo":
                    v.wait_ge(sems["vc"], nth("vc", l, 1))
                    for j in range(4):
                        rows = slice(32 * j, 32 * j + CMP_N)
                        ins = nc.vector.tensor_copy(VC[rows, :, j, :],
                                                    PS[rows, 3, 0:P].rearrange("p (g d) -> p g d", d=64))
                    ins.then_inc(sems["vcc"], 1)
                elif kind == "vczero":
                    v.wait_ge(sems["evac"], nth("evac", l, 12))
                    nc.vector.memset(VC[:, :, :, :], 0.0).then_inc(v_ch, 1)
                    v.wait_ge(v_ch, v_step())
                elif kind == "state":
                    if i < 3:
                        v.wait_ge(sems["ds"], nth("ds", l, i + 1))
                        if i:
                            v.wait_ge(sems["osum"], nth("osum", l, i + 1))
                        for h in range(4):
                            d = PS[:, 5, P * h:P * h + P]
                            if i == 0:
                                ins = nc.vector.tensor_copy(Sst[:, h, :], d)
                            else:
                                ins = nc.vector.scalar_tensor_tensor(out=Sst[:, h, :], in0=Sst[:, h, :],
                                                                     scalar=ebl[:, h, i:i + 1], in1=d,
                                                                     op0=ALU.mult, op1=ALU.add)
                        ins.then_inc(sems["s"], 1)
                        v.wait_ge(sems["s"], l * 3 + (i + 1))
                elif kind == "hn":
                    v.wait_ge(sems["hrs"], nth("hrs", l, i + 1))
                    nc.vector.scalar_tensor_tensor(out=mixT[:, i, :], in0=mixT[:, i, :],
                                                         scalar=lcol[:, C_GN:C_GN + 1], in1=rrs[:, i % 2, :],
                                                         op0=ALU.mult, op1=ALU.mult).then_inc(v_ch, 1)
                    v.wait_ge(v_ch, v_step())
                    nc.vector.tensor_tensor(mixT[:, i, :], mixT[:, i, :], sgT[:, i, :], ALU.mult
                                            ).then_inc(sems["hn"], 1)
                elif kind == "attention":
                    attend(l, NSA, nsa_combine)
                elif kind == "wout":
                    v.wait_ge(sems["pt"], nth("pt", l, EV["pt"]))
                    v.wait_ge(sems["mixtok"], nth("mixtok", l, 4))
                    for k in range(8):
                        stream(l, k, nth("tile", l, T_WO + k - 1), mixT[:, k, :])
                    residual(l, 0, T_WO + 8)
                elif kind == "ffn":
                    with v.Fori(0, FFC // 2) as j:
                        for u in range(2):
                            v.wait_ge(sems["silu"], l * FFC + j * 2 + (u + 1))
                            v.wait_ge(sems["tile"], l * T_LAYER + j * 4 + (T_FFI + 2 * u + 2 + RING))
                            nc.vector.tensor_tensor(act[:, j * 2 + u, :], sq2[:, u, :], PS[:, 2 * u + 1, :], ALU.mult
                                                    ).then_inc(sems["act"], 1)
                    with v.Fori(0, FFC // 2) as j:
                        v.wait_ge(sems["act"], nth("act", l, FFC))
                        for u in range(2):
                            v.wait_ge(sems["tile"], l * T_LAYER + j * 2 + (T_FFO + u - 1 + RING))
                            nc.vector.tensor_copy(xs[:, u, 0, :], act[:, j * 2 + u, :]).then_inc(sems["xsh"], 1)
                            v.wait_ge(sems["xsh"], l * FFC + j * 2 + (u + 1))
                            nc.vector.tensor_tensor(xs[:, u, 1, :], act[:, j * 2 + u, :], xs[:, u, 0, :], ALU.subtract
                                                    ).then_inc(sems["xs"], 1)
                    residual(l, 1, T_FFO + FFC)

            def step2(kind, i):
                l = DEPTH
                if kind == "norm":
                    n = NORMS2[i][0]
                    v.wait_ge(sems["rstd"], nth("rstd", l, n + 1))
                    for c in range(KO):
                        g = (M_MIX, M_MEM, M_CROSS, M_FFN)[i] + c
                        buf, src, w = (xr, xT, T) if i in (0, 2) else (memn, memn, MEM) if i == 1 else (xn, xT, T)
                        nc.vector.scalar_tensor_tensor(out=buf[:, c, :], in0=src[:, c, :], scalar=par[:, g:g + 1],
                                                       in1=rstd[:, 0:w], op0=ALU.mult, op1=ALU.mult
                                                       ).then_inc(sems["xr" if i in (0, 2) else "xn"], 1)
                    if i in (0, 2):
                        low_parts(l, i // 2)
                elif kind == "angles":
                    ang, kf = gtmp[:, 0:T], gtmp[:, T:2 * T]
                    nc.vector.tensor_copy(kf, ang.bitcast(I32)).then_inc(v_ch, 1)
                    v.wait_ge(v_ch, v_step())
                    nc.vector.tensor_scalar(ang, kf, par[:, M_FREQ:M_FREQ + 1], None, ALU.mult).then_inc(v_ch, 1)
                    v.wait_ge(v_ch, v_step())
                    c1 = 6.28125
                    c2 = float(np.float32(np.round((TWO_PI - c1) * 2 ** 21) / 2 ** 21))
                    c3 = float(np.float32(TWO_PI - c1 - c2))
                    magic = 12582912.0
                    for shift, dst in ((0.25, cos), (0.0, sin)):
                        nc.vector.tensor_scalar(kf, ang, 1 / TWO_PI, shift, ALU.mult, ALU.add).then_inc(v_ch, 1)
                        v.wait_ge(v_ch, v_step())
                        nc.vector.tensor_scalar(kf, kf, magic, None, ALU.add).then_inc(v_ch, 1)
                        v.wait_ge(v_ch, v_step())
                        nc.vector.tensor_scalar(kf, kf, -magic, None, ALU.add).then_inc(v_ch, 1)
                        v.wait_ge(v_ch, v_step())
                        nc.vector.scalar_tensor_tensor(out=dst, in0=kf, scalar=-c1, in1=ang,
                                                             op0=ALU.mult, op1=ALU.add).then_inc(v_ch, 1)
                        v.wait_ge(v_ch, v_step())
                        nc.vector.scalar_tensor_tensor(out=dst, in0=kf, scalar=-c2, in1=dst,
                                                             op0=ALU.mult, op1=ALU.add).then_inc(v_ch, 1)
                        v.wait_ge(v_ch, v_step())
                        nc.vector.scalar_tensor_tensor(out=dst, in0=kf, scalar=-c3, in1=dst,
                                                             op0=ALU.mult, op1=ALU.add).then_inc(v_ch, 1)
                        v.wait_ge(v_ch, v_step())
                        if shift:
                            nc.vector.tensor_scalar(dst, dst, TWO_PI / 4, None, ALU.add).then_inc(v_ch, 1)
                            v.wait_ge(v_ch, v_step())
                    nc.vector.tensor_scalar(tabs[:, :], tabs[:, :], 3.1415925, -3.1415925, ALU.min, ALU.max
                                            ).then_inc(sems["trig"], 1)
                    v.wait_ge(sems["trig"], 1)
                elif kind == "lam":
                    la = [par[:, M_LAM + 64 * j:M_LAM + 64 * j + 64] for j in range(4)]
                    nc.vector.tensor_tensor(lnl[:, 0, :], la[0], la[1], ALU.mult)
                    nc.vector.tensor_tensor(lnl[:, 1, :], la[2], la[3], ALU.mult).then_inc(v_ch, 1)
                    v.wait_ge(v_ch, v_step())
                    nc.vector.tensor_reduce(small[:, 0:2], lnl[:, :, :], AX.X, ALU.add).then_inc(sems["lam"], 1)
                    v.wait_ge(sems["lams"], nth("lams", 0, 1))
                    nc.vector.tensor_tensor(small[:, 2:3], small[:, 0:1], small[:, 1:2], ALU.subtract).then_inc(v_ch, 1)
                    v.wait_ge(v_ch, v_step())
                    nc.vector.tensor_scalar(small[:, 3:4], small[:, 2:3], 0.8 - 0.6, None, ALU.add).then_inc(v_ch, 1)
                    v.wait_ge(v_ch, v_step())
                elif kind == "flog":
                    nc.vector.memset(negc, 0.0).then_inc(v_ch, 1)
                    v.wait_ge(v_ch, v_step())
                    v.wait_ge(sems["fls"], nth("fls", 0, 1))
                    nc.vector.tensor_scalar(lnb[0:8, :], lnb[0:8, :], 0.0, None, ALU.min).then_inc(v_ch, 1)
                    v.wait_ge(v_ch, v_step())
                    nc.vector.tensor_tensor(lnb[0:8, :], lnb[0:8, :], qg[0:8, 1, :], ALU.subtract).then_inc(v_ch, 1)
                    v.wait_ge(v_ch, v_step())
                    nc.vector.tensor_tensor_scan(qg[0:8, 0, :], one[0:8, :].broadcast_to([8, T]), lnb[0:8, :], 0.0,
                                                       ALU.mult, ALU.add).then_inc(v_ch, 1)
                    v.wait_ge(v_ch, v_step())
                    nc.vector.tensor_scalar(negc[0:8, :], qg[0:8, 0, :], -1.0, None, ALU.mult).then_inc(sems["nck"], 1)
                    v.wait_ge(sems["nck"], 1)
                elif kind == "rr":
                    v.wait_ge(sems["rot"], nth("rot", l, i + 1))
                    if i == 0:
                        v.wait_ge(sems["trigs"], nth("trigs", 0, 1))
                    dst = dq[:, i, :] if i < 4 else dk[:, i - 4, :]
                    nc.vector.tensor_tensor(gtmp[:, 0:T], PS[:, 7, :], sin, ALU.mult)
                    nc.vector.tensor_tensor(gtmp[:, T:2 * T], qnb[:, i % 2, :], cos, ALU.mult).then_inc(v_ch, 1)
                    v.wait_ge(v_ch, v_step())
                    nc.vector.tensor_tensor(dst, gtmp[:, 0:T], gtmp[:, T:2 * T], ALU.add).then_inc(sems["rope"], 1)
                    v.wait_ge(sems["rope"], nth("rope", l, i + 1))
                elif kind == "attention":
                    attend(l, BL2, block2_combine)
                elif kind == "cross":
                    attend(l, CROSS, cross_combine)
                elif kind == "merge":
                    for c in range(8):
                        v.wait_ge(sems["tile"], nth("tile", l, B_AB + c + 1))
                        v.wait_ge(sems["evac"], nth("evac", l, 34))
                        b = 2 * (c % 2)
                        nc.vector.tensor_tensor(gtmp[:, 0:T], sga[:, c, :], PS[:, b, :], ALU.mult)
                        nc.vector.tensor_tensor(gtmp[:, T:2 * T], sga[:, 8 + c, :], PS[:, b + 1, :], ALU.mult
                                        ).then_inc(v_ch, 1)
                        v.wait_ge(v_ch, v_step())
                        nc.vector.tensor_tensor(merged[:, c, :], gtmp[:, 0:T], gtmp[:, T:2 * T], ALU.add
                                                ).then_inc(sems["mrg"], 1)
                        v.wait_ge(sems["mrg"], c + 1)
                elif kind == "kouter":
                    if i == 0:
                        for k in range(8):
                            stream(l, k, nth("tile", l, B_WO + k - 1), merged[:, k, :])
                    else:
                        v.wait_ge(sems["pt"], nth("pt", l, 72 + 20))
                        for k in range(2):
                            stream(l, k, nth("tile", l, B_CO + k - 1), coT[:, k, :])
                    residual(l, i, (B_WO + 8, B_CO + 2)[i])

            def by_head(x, d):
                return x.rearrange("p (h d) -> p h d", d=d)

            def block2_combine(l, qt):
                nc.vector.reciprocal(Rc[:, 0:16], Lt[:, qt % 2, 0:16]).then_inc(v_ch, 1)
                v.wait_ge(v_ch, v_step())
                nc.vector.tensor_scalar(Rc[:, 12:16], Rc[:, 12:16], small[:, 3:4], None, ALU.mult).then_inc(v_ch, 1)
                v.wait_ge(v_ch, v_step())
                nc.vector.tensor_tensor(by_head(ftmp[:, 0, :], 64), by_head(PS[:, 5, :], 64),
                                              Rc[:, 0:8].unsqueeze(2).broadcast_to([P, 8, 64]), ALU.mult
                                              ).then_inc(v_ch, 1)
                v.wait_ge(v_ch, v_step())
                nc.vector.sem_inc(sems["mixtok"], 1)
                for c in range(2):
                    ins = nc.vector.tensor_tensor(by_head(oa[:, c, :], P), by_head(PS[:, 6 + c, :], P),
                                                  Rc[:, 8 + 4 * c:12 + 4 * c].unsqueeze(2).broadcast_to([P, 4, P]),
                                                  ALU.mult)
                ins.then_inc(sems["ofree"], 1)
                v.wait_ge(sems["ofree"], nth("ofree", l, qt + 1))
                nc.vector.tensor_tensor(oa[:, 0, :], oa[:, 0, :], oa[:, 1, :], ALU.subtract).then_inc(v_ch, 1)
                v.wait_ge(v_ch, v_step())
                nc.vector.tensor_tensor(oa[:, 1, :], oa[:, 0, :], oa[:, 0, :], ALU.mult).then_inc(v_ch, 1)
                v.wait_ge(v_ch, v_step())
                nc.vector.tensor_reduce(small[:, 4:8], by_head(oa[:, 1, :], P), AX.X, ALU.add).then_inc(sems["ms"], 1)

            def block2_rest(l, qt):
                v.wait_ge(sems["msr"], nth("msr", 0, qt + 1))
                nc.vector.tensor_tensor(by_head(ftmp[:, 1, :], P), by_head(oa[:, 0, :], P),
                                        small[:, 8:12].unsqueeze(2).broadcast_to([P, 4, P]), ALU.mult
                                        ).then_inc(sems["mixtok"], 1)
                v.wait_ge(sems["mixtok"], nth("mixtok", l, 2 * qt + 2))

            def cross_combine(l, qt):
                nc.vector.reciprocal(Rc[:, 0:4], Lt[:, qt % 2, 0:4]).then_inc(v_ch, 1)
                v.wait_ge(v_ch, v_step())
                nc.vector.tensor_tensor(by_head(ftmp[:, 0, 0:256], 64), by_head(PS[:, 5, 0:256], 64),
                                              Rc[:, 0:4].unsqueeze(2).broadcast_to([P, 4, 64]), ALU.mult
                                              ).then_inc(v_ch, 1)
                v.wait_ge(v_ch, v_step())
                nc.vector.sem_inc(sems["mixtok"], 1)
                nc.vector.sem_inc(sems["ofree"], 1)

            def residual(l, n, last_tile):
                for c in range(KO):
                    if c < 7:
                        v.wait_ge(sems["res"], nth("res", l, 7 * n + c + 1))
                    else:
                        v.wait_ge(sems["tile"], nth("tile", l, last_tile))
                    nc.vector.tensor_tensor(xT[:, c, :], xT[:, c, :], PS[:, c, :], ALU.add).then_inc(sems["h"], 1)

            def nsa_combine(l, qt):
                if qt:
                    v.wait_ge(sems["mixtok"], nth("mixtok", l, qt))
                nc.vector.reciprocal(Rc[:, :], Lt[:, qt % 2, :]).then_inc(v_ch, 1)
                v.wait_ge(v_ch, v_step())
                nc.vector.tensor_tensor(Rc[:, :].rearrange("p (b h) -> p b h", b=3),
                                              Rc[:, :].rearrange("p (b h) -> p b h", b=3),
                                              gates[:, qt, :].rearrange("p (h b) -> p b h", b=3), ALU.mult
                                              ).then_inc(v_ch, 1)
                v.wait_ge(v_ch, v_step())
                if qt == 0:
                    nc.vector.tensor_scalar(Rc[:, 0:8], Rc[:, 0:8], valid0, None, ALU.mult).then_inc(v_ch, 1)
                    v.wait_ge(v_ch, v_step())

                def r(b):
                    return Rc[:, 8 * b:8 * b + 8].unsqueeze(2).broadcast_to([P, 8, 64])

                def o(bank):
                    return PS[:, bank, :].rearrange("p (h d) -> p h d", d=64)

                def w(x):
                    return x.rearrange("p (h d) -> p h d", d=64)

                nc.vector.tensor_tensor(w(oa[:, 0, :]), o(5), r(1), ALU.mult)
                nc.vector.tensor_tensor(w(oa[:, 1, :]), o(6), r(2), ALU.mult).then_inc(v_ch, 1)
                v.wait_ge(v_ch, v_step())
                nc.vector.tensor_tensor(oa[:, 0, :], oa[:, 0, :], oa[:, 1, :], ALU.add).then_inc(v_ch, 1)
                v.wait_ge(v_ch, v_step())
                ins = nc.vector.tensor_tensor(w(oa[:, 1, :]), o(7), r(0), ALU.mult)
                ins.then_inc(sems["ofree"], 1)
                v.wait_ge(sems["ofree"], l * 4 + (qt + 1))
                nc.vector.tensor_tensor(mixtok, oa[:, 0, :], oa[:, 1, :], ALU.add).then_inc(sems["mixtok"], 1)

            def attend(l, items, combine):
                for s in range(len(items) + LAG_V):
                    it = items[s] if s < len(items) else None
                    if it and it["kind"] != "mix":
                        k = it["k"]
                        v.wait_ge(sems["sc"], nth("sc", l, k + 1))
                        if k >= 4:
                            v.wait_ge(sems["mx"], nth("mx", l, k - 3))
                        if it["kind"] == "cmp":
                            if "t3" in it:
                                v.wait_ge(sems["tr"], nth("tr", l, it["t3"] + 1))
                            scores = PS[:, k % 3, 0:P].rearrange("p (h n) -> p h n", n=32)
                            nc.vector.tensor_reduce(nmx[:, k % 4, :], scores, AX.X, ALU.max).then_inc(v_ch, 1)
                            v.wait_ge(v_ch, v_step())
                            nc.vector.tensor_tensor(
                                Pr[k % 3][:, 0:P].rearrange("p (h n) -> p h n", n=32), scores,
                                nmx[:, k % 4, :].unsqueeze(2).broadcast_to([P, 4, 32]), ALU.subtract
                            ).then_inc(sems["mx"], 1)
                        else:
                            nc.vector.tensor_reduce(nmx[:, k % 4, 0:1], PS[:, k % 3, 0:it["n"]], AX.X, ALU.max,
                                                    negate=True).then_inc(sems["mx"], 1)
                    it = items[s - LAG_T] if 0 <= s - LAG_T < len(items) else None
                    if it:
                        t = it["t"]
                        v.wait_ge(sems["tr"], nth("tr", l, t + 1))
                        if "pv2" in it:
                            v.wait_ge(sems["pv"], nth("pv", l, it["pv2"] + 1))
                        n = it["nb"] * P
                        if it["kind"] == "mix":
                            src = PS[:, 3 + t % 2, 0:n].rearrange("p (a b) -> p a b", b=P)
                            if "cols" in it:
                                yh, yl = (x[:, it["dst"], it["cols"]] for x in (xh, xl))
                                if "sub" in it:
                                    nc.vector.tensor_scalar(gtmp[:, 0:T], PS[:, 3 + t % 2, :], par[:, M_SUB:M_SUB + 1],
                                                            0.8, ALU.mult, ALU.mult).then_inc(v_ch, 1)
                                    v.wait_ge(v_ch, v_step())
                                    src = gtmp[:, 0:T].rearrange("p (a b) -> p a b", b=P)
                                nc.vector.tensor_copy(yh, src).then_inc(v_ch, 1)
                                v.wait_ge(v_ch, v_step())
                                ins = nc.vector.tensor_tensor(yl, src, yh, ALU.subtract)
                            else:
                                ins = nc.vector.tensor_copy(it["dst"], src)
                        else:
                            if it["kind"] == "cmp":
                                nc.vector.tensor_reduce(it["L"], Pr[it["k"] % 3][:, 0:P].rearrange(
                                    "p (h n) -> p h n", n=32), AX.X, ALU.add)
                            ins = nc.vector.tensor_copy(PTs[t % 2][:, 0:n], PS[:, 3 + t % 2, 0:n])
                        ins.then_inc(sems["pt"], 1)
                    it = items[s - LAG_V] if 0 <= s - LAG_V < len(items) else None
                    if it and "last" in it:
                        v.wait_ge(sems["pv"], nth("pv", l, it["k"] + 1))
                        if it["t"] >= 0:
                            v.wait_ge(sems["pt"], nth("pt", l, it["t"] + 1))
                        combine(l, it["last"])
                    it = items[s - LAG_V - 2] if 0 <= s - LAG_V - 2 < len(items) else None
                    if items is BL2 and it and "last" in it:
                        block2_rest(l, it["last"])

            def small_parts(value, n):
                nc.vector.tensor_copy(wsm[:, 0, 0:n], value).then_inc(v_ch, 1)
                v.wait_ge(v_ch, v_step())
                nc.vector.tensor_tensor(wsm[:, 1, 0:n], value, wsm[:, 0, 0:n], ALU.subtract).then_inc(v_ch, 1)
                v.wait_ge(v_ch, v_step())

            nc.vector.memset(wsm[:, :, 192:].bitcast(F32), 0.0)
            nc.vector.memset(one[:, :], 1.0).then_inc(s_pre, 1)
            nc.vector.memset(eps[:, 0:1], 1e-6)
            nc.vector.memset(eps[:, 1:2], 1e-5)
            nc.vector.memset(kcr[:, :], 0.0)
            nc.vector.memset(lb[:, 0, :], 0.0)
            v.wait_ge(s_in, 16 * NIN)
            nc.vector.tensor_tensor(lbl[:, 0:4], cols[:, 1, C_LB:C_LB + 4], cols[:, 0, C_LB:C_LB + 4], ALU.subtract
                                    ).then_inc(s_pre, 1)
            v.wait_ge(s_pre, 3)
            nc.vector.tensor_copy(cols[:, :, C_LB:C_LB + 4], lb[:, :, :])
            nc.vector.tensor_scalar(cols[:, :, C_LB + 4:C_LB + 8], lb[:, :, :], -1.0, 1.0, ALU.mult, ALU.add)
            nc.vector.tensor_scalar(cols[:, :, C_QG:C_QG + 1], cols[:, :, C_QG:C_QG + 1], 0.125, None, ALU.mult
                                    ).then_inc(s_pre, 1)
            v.wait_ge(s_pre, 4)
            v.sem_inc(sems["tile"], RING)
            v.sem_inc(sems["evac"], 2)
            v.sem_inc(sems["rrstd"], 1)
            v.sem_inc(sems["rope"], 1)
            v.sem_inc(sems["h"], 8)
            v.sem_inc(sems["act"], 2)
            with v.Fori(0, DEPTH) as l:
                ch["n"] = 0
                ch["base"] = l * V_CH
                nc.vector.tensor_copy(lcol[:, :], cols[:, l, :]).then_inc(sems["params"], 1)
                nc.vector.tensor_copy(misc[:, :], misc_all[:, l, :]).then_inc(sems["params"], 1)
                v.wait_ge(sems["params"], nth("params", l, 2))
                small_parts(misc[:, 0:192], 192)
                for kind, i in STEPS:
                    step(l, kind, i)
                assert ch["n"] == V_CH, ch["n"]
            ch["n"] = 0
            ch["base"] = DEPTH * V_CH
            v.wait_ge(sems["b_in"], 48)
            small_parts(par[:, M_WF:M_WF + 64], 64)
            for kind, i in STEPS2:
                step2(kind, i)

            tt, ts, red = nc.vector.tensor_tensor, nc.vector.tensor_scalar, nc.vector.tensor_reduce
            E_ = par[:, M_E:M_E + NEXP]

            def over(x, shape):
                return (x.unsqueeze(2) if x.shape[1] == shape[0] and shape[0] != shape[1] else x.unsqueeze(1)
                        ).broadcast_to([P, *shape])

            gm, gs, prm, v1, v2, dd = (rt[:, 16 + 4 * j:20 + 4 * j] for j in (0, 2, 3, 4, 5, 1))
            e1 = dd
            desc = rt[:, 48:80]
            cnt, ovc, incl, ovs, addr = (rt[:, 80 + 32 * j:112 + 32 * j] for j in range(5))
            g4 = lg[:, :, 0:4]
            v.wait_ge(MS["lg"], 1)
            tt(lg[:, :, :], PS[:, 1, 0:144].rearrange("p (q e) -> p q e", e=36),
                     over(par[:, M_BGE:M_BGE + 36], (QT, 36)), ALU.add).then_inc(v_ch, 1)
            v.wait_ge(v_ch, v_step())
            red(gm, g4, AX.X, ALU.max).then_inc(v_ch, 1)
            v.wait_ge(v_ch, v_step())
            ge = rt[:, 0:16].rearrange("p (q g) -> p q g", g=4)
            tt(ge, g4, gm.unsqueeze(2).broadcast_to([P, 4, 4]), ALU.subtract).then_inc(MS["rq"], 1)
            goh = tmpe[:, 0, 0:16].rearrange("p (q g) -> p q g", g=4)
            pri = tmpe[:, 0, 16:32].rearrange("p (q g) -> p q g", g=4)
            ts(desc, E_, -1.0, 32.0, ALU.mult, ALU.add).then_inc(v_ch, 1)
            v.wait_ge(v_ch, v_step())
            tt(pri, g4, gm.unsqueeze(2).broadcast_to([P, 4, 4]), ALU.is_equal).then_inc(v_ch, 1)
            v.wait_ge(v_ch, v_step())
            tt(pri, pri, desc[:, 0:4].unsqueeze(1).broadcast_to([P, 4, 4]), ALU.mult).then_inc(v_ch, 1)
            v.wait_ge(v_ch, v_step())
            red(prm, pri, AX.X, ALU.max).then_inc(v_ch, 1)
            v.wait_ge(v_ch, v_step())
            tt(goh, pri, prm.unsqueeze(2).broadcast_to([P, 4, 4]), ALU.is_equal).then_inc(v_ch, 1)
            v.wait_ge(v_ch, v_step())
            ts(goh, goh, -1.0, 1e30, ALU.add, ALU.mult).then_inc(v_ch, 1)
            v.wait_ge(v_ch, v_step())
            for qt in range(QT):
                ins = tt(em[:, qt, :].rearrange("p (g e) -> p g e", e=8), lg[:, qt, 4:36].rearrange(
                    "p (g e) -> p g e", e=8), goh[:, qt, :].unsqueeze(2).broadcast_to([P, 4, 8]), ALU.add)
            ins.then_inc(v_ch, 1)
            v.wait_ge(v_ch, v_step())

            def bc(x):
                return x.unsqueeze(2).broadcast_to([P, QT, NEXP])

            def row(x):
                return x.unsqueeze(1).broadcast_to([P, QT, NEXP])

            def first_best(vmax, oh):
                red(vmax, em[:, :, :], AX.X, ALU.max).then_inc(v_ch, 1)
                v.wait_ge(v_ch, v_step())
                tt(tmpe[:, :, :], em[:, :, :], bc(vmax), ALU.is_equal).then_inc(v_ch, 1)
                v.wait_ge(v_ch, v_step())
                tt(tmpe[:, :, :], tmpe[:, :, :], row(desc), ALU.mult).then_inc(v_ch, 1)
                v.wait_ge(v_ch, v_step())
                red(prm, tmpe[:, :, :], AX.X, ALU.max).then_inc(v_ch, 1)
                v.wait_ge(v_ch, v_step())
                tt(oh[:, :, :], tmpe[:, :, :], bc(prm), ALU.is_equal).then_inc(v_ch, 1)
                v.wait_ge(v_ch, v_step())

            first_best(v1, oh1)
            nc.vector.scalar_tensor_tensor(out=em[:, :, :], in0=oh1[:, :, :], scalar=-2e30, in1=em[:, :, :],
                                                 op0=ALU.mult, op1=ALU.add).then_inc(v_ch, 1)
            v.wait_ge(v_ch, v_step())
            first_best(v2, oh2)
            tt(Ab[:, :, :], oh1[:, :, :], oh2[:, :, :], ALU.add).then_inc(MS["A"], 1)
            tt(dd, v2, v1, ALU.subtract).then_inc(MS["rq"], 1)
            v.wait_ge(MS["rp"], 2)
            red(gs, ge, AX.X, ALU.add).then_inc(v_ch, 1)
            v.wait_ge(v_ch, v_step())
            nc.vector.reciprocal(gs, gs).then_inc(v_ch, 1)
            v.wait_ge(v_ch, v_step())
            ts(prm, e1, 1.0, None, ALU.add).then_inc(v_ch, 1)
            v.wait_ge(v_ch, v_step())
            nc.vector.reciprocal(prm, prm).then_inc(v_ch, 1)
            v.wait_ge(v_ch, v_step())
            tt(wts[:, 0, :], prm, gs, ALU.mult).then_inc(v_ch, 1)
            v.wait_ge(v_ch, v_step())
            tt(wts[:, 1, :], wts[:, 0, :], e1, ALU.mult).then_inc(v_ch, 1)
            v.wait_ge(v_ch, v_step())
            v.wait_ge(MS["rk"], 1)
            ps_rank = PS[:, 1, 0:128].rearrange("p (q e) -> p q e", e=NEXP)
            nc.vector.tensor_copy(cnt, PS[:, 1, 128:160]).then_inc(v_ch, 1)
            v.wait_ge(v_ch, v_step())
            ts(ovc, cnt, 128.5, None, ALU.is_ge).then_inc(v_ch, 1)
            v.wait_ge(v_ch, v_step())
            for lim in (256.5, 384.5):
                ts(ovs, cnt, lim, None, ALU.is_ge).then_inc(v_ch, 1)
                v.wait_ge(v_ch, v_step())
                tt(ovc, ovc, ovs, ALU.add).then_inc(v_ch, 1)
                v.wait_ge(v_ch, v_step())
            nc.vector.memset(addr, 1.0).then_inc(v_ch, 1)
            v.wait_ge(v_ch, v_step())
            nc.vector.tensor_tensor_scan(incl, addr, ovc, 0.0, ALU.mult, ALU.add).then_inc(v_ch, 1)
            v.wait_ge(v_ch, v_step())
            tt(ovs, incl, ovc, ALU.subtract).then_inc(v_ch, 1)
            v.wait_ge(v_ch, v_step())
            tt(addr, ovs, E_, ALU.subtract).then_inc(v_ch, 1)
            v.wait_ge(v_ch, v_step())
            ts(addr, addr, float(NEXP - 1), float(P), ALU.add, ALU.mult).then_inc(v_ch, 1)
            v.wait_ge(v_ch, v_step())
            ts(tmpe[:, :, :], ps_rank, float(P) - 0.5, None, ALU.is_ge).then_inc(v_ch, 1)
            v.wait_ge(v_ch, v_step())
            tt(tmpe[:, :, :], tmpe[:, :, :], row(addr), ALU.mult).then_inc(v_ch, 1)
            v.wait_ge(v_ch, v_step())
            tt(rnk[:, :, :], tmpe[:, :, :], ps_rank, ALU.add).then_inc(v_ch, 1)
            v.wait_ge(v_ch, v_step())
            ts(addr, E_, float(P), None, ALU.mult).then_inc(v_ch, 1)
            v.wait_ge(v_ch, v_step())
            tt(rnk[:, :, :], rnk[:, :, :], row(addr), ALU.add).then_inc(v_ch, 1)
            v.wait_ge(v_ch, v_step())
            for k, oh in enumerate((oh1, oh2)):
                tt(tmpe[:, :, :], rnk[:, :, :], oh[:, :, :], ALU.mult).then_inc(v_ch, 1)
                v.wait_ge(v_ch, v_step())
                red(pos[:, k, :], tmpe[:, :, :], AX.X, ALU.add).then_inc(v_ch, 1)
                v.wait_ge(v_ch, v_step())
            nc.vector.tensor_copy(posi[:, :], pos[:, :, :].rearrange("p k q -> p (k q)"))
            nc.vector.tensor_copy(prel[:, :, :], pos[:, :, :]).then_inc(v_ch, 1)
            v.wait_ge(v_ch, v_step())
            j8 = gtmp[:, 0:256].rearrange("p (j e) -> p j e", e=NEXP)
            j8b = gtmp[:, 256:512].rearrange("p (j e) -> p j e", e=NEXP)
            jj = E_[:, 0:8].unsqueeze(2).broadcast_to([P, 8, NEXP])

            def er(x):
                return x.unsqueeze(1).broadcast_to([P, 8, NEXP])

            tt(j8, jj, er(ovs), ALU.is_ge).then_inc(v_ch, 1)
            v.wait_ge(v_ch, v_step())
            tt(j8b, jj, er(incl), ALU.is_lt).then_inc(v_ch, 1)
            v.wait_ge(v_ch, v_step())
            tt(j8, j8, j8b, ALU.mult).then_inc(v_ch, 1)
            v.wait_ge(v_ch, v_step())
            tt(j8, j8, er(E_), ALU.mult).then_inc(v_ch, 1)
            v.wait_ge(v_ch, v_step())
            red(small[:, 0:8], j8, AX.X, ALU.add).then_inc(v_ch, 1)
            v.wait_ge(v_ch, v_step())
            nc.vector.tensor_copy(ovi[:, 0:8], small[:, 0:8]).then_inc(v_ch, 1)
            v.wait_ge(v_ch, v_step())
            nc.vector.tensor_copy(ovi[:, 8:9], incl[:, 31:32]).then_inc(MS["ro"], 1)

            iota = par[:, M_IOTA:M_IOTA + P]

            def onehot(i, u):
                v.wait_ge(MS["ix"], lin(i, u, 1, -1))
                v.wait_ge(MS["od"], lin(i, u, 1, 0))
                for qt in range(QT):
                    ins = ts(Ob[u % 2][:, qt, :], iota, prel[:, 0, qt:qt + 1], None, ALU.is_equal)
                ins.then_inc(MS["odh"], 1)
                v.wait_ge(MS["odh"], lin(i, u, 2, 1))
                for qt in range(QT):
                    ins = nc.vector.scalar_tensor_tensor(out=Ob[u % 2][:, qt, :], in0=iota,
                                                         scalar=prel[:, 1, qt:qt + 1], in1=Ob[u % 2][:, qt, :],
                                                         op0=ALU.is_equal, op1=ALU.add)
                ins.then_inc(MS["odh"], 1)
                v.wait_ge(MS["odh"], lin(i, u, 2, 2))
                ts(prel[:, :, :], prel[:, :, :], -float(P), None, ALU.add).then_inc(MS["od"], 1)

            def index(i, u):
                v.wait_ge(MS["ix"], lin(i, u, 1, 1))
                v.wait_ge(MS["xg"][(u - 2) % 2], dma_of(i, u - 2))
                nc.vector.tensor_copy(idxi[:, u % 2:u % 2 + 1], PS[:, 7, 0:1]).then_inc(MS["ii"], 1)

            def lows(w, i, u):
                for k in (0, 2):
                    v.wait_ge(MS["high" + w], lin(i, u, 4, k + 1))
                    tt(low(w, k), loaded(w, k), high(w, k), ALU.subtract).then_inc(MS["vlow" + w], 1)

            def xgt_v(i, u):
                v.wait_ge(MS["xea"], lin(i, u, 1, 1))
                tt(xgT[u % 2][1], PS[:, 0:2, :].rearrange("p c (a b) -> p (c a) b", b=P), xgT[u % 2][0], ALU.subtract
                   ).then_inc(MS["xev"], 1)

            def ht_low(i, u):
                v.wait_ge(MS["he"], lin(i, u, 1, 1))
                tt(hT[u % 2][1], PS[:, 4, :].rearrange("p (a b) -> p a b", b=P), hT[u % 2][0], ALU.subtract
                   ).then_inc(MS["hl"], 1)

            def hidden(i, u):
                v.wait_ge(MS["sl"], lin(i, u, 1, 1))
                v.wait_ge(MS["useU"], lin(i, u, 2, 2))
                v.wait_ge(MS["ht"], lin(i, u, 1, -1))
                tt(hsb[u % 2], hsilu, PS[:, 3, :], ALU.mult).then_inc(MS["hm"], 1)

            def y_v(i, u):
                v.wait_ge(MS["useD"], lin(i, u, 2, 2))
                v.wait_ge(MS["yd"][(u - 2) % 2], dma_of(i, u - 2))
                nc.vector.tensor_copy(ysb[u % 2][:, T:D], PS[:, 6, :]).then_inc(MS["yev"], 1)

            def moe_v(i, u, prev, next_):
                index(i, u + 2)
                onehot(i, u + 3)
                xgt_v(i, u + 1)
                if prev:
                    ht_low(i, u - 1)
                lows("U", i, u)
                if prev:
                    lows("D", i, u - 1)
                hidden(i, u)
                if next_:
                    lows("G", i, u + 1)
                if prev:
                    y_v(i, u - 1)

            def last_v(i):
                ht_low(i, 1)
                lows("D", i, 1)
                y_v(i, 1)

            v.wait_ge(MS["ro"], 1)
            onehot(0, 0)
            onehot(0, 1)
            index(0, 0)
            index(0, 1)
            onehot(0, 2)
            lows("G", 0, 0)
            xgt_v(0, 0)
            blocks(v, moe_v, 0, NEXP)
            last_v(NEXP // 2 - 1)
            with overflow(v):
                lows("G", NEXP // 2, 0)
                blocks(v, moe_v, NEXP, NEXP + OVB)
                last_v((NEXP + OVB) // 2 - 1)
            v.wait_ge(MS["te"], 16)
            v.wait_ge(MS["gf"], 16)
            for qt in range(QT):
                v.wait_ge(MS["yg"][qt], 32)
                y1, y2 = yg[2 * qt], yg[2 * qt + 1]
                nc.vector.scalar_tensor_tensor(out=y1, in0=y1, scalar=wts[:, 0, qt:qt + 1], in1=xtok[:, qt, :],
                                                     op0=ALU.mult, op1=ALU.add).then_inc(v_ch, 1)
                v.wait_ge(v_ch, v_step())
                nc.vector.scalar_tensor_tensor(out=y1, in0=y2, scalar=wts[:, 1, qt:qt + 1], in1=y1,
                                               op0=ALU.mult, op1=ALU.add).then_inc(MS["fa"], 1)
            for qt in range(QT):
                v.wait_ge(MS["fs"], qt + 1)
                nc.vector.scalar_tensor_tensor(out=yg[2 * qt], in0=yg[2 * qt], scalar=small[:, 8 + qt:9 + qt],
                                               in1=gfin, op0=ALU.mult, op1=ALU.mult).then_inc(MS["ff"], 1)

        @block.tensor
        def _(pe):
            mm = nc.tensor.matmul

            def mm3(out, a, b, start, stop):
                mm(out, a[0], b[0], start=start, stop=False)
                mm(out, a[0], b[1], start=False, stop=False)
                return mm(out, a[1], b[0], start=False, stop=stop)

            def weights(t, cols):
                return whi[:, t % 2, cols], wlo[:, t % RING, cols]

            def feature_major(l, out, t, wait, wait_low=None):
                if wait is None:
                    for c in range(KO):
                        ins = mm3(out, weights(t, slice(c * P, c * P + P)), (xh[:, c, :], xl[:, c, :]),
                                  start=(c == 0), stop=(c == 7))
                    return ins
                for c in range(KO):
                    pe.wait_ge(sems["xh"], nth("xh", l, wait + c + 1))
                    for w in weights(t, slice(c * P, c * P + P)):
                        mm(out, w, xh[:, c, :], start=(c == 0 and w.name == whi.name), stop=False)
                for c in range(KO):
                    pe.wait_ge(sems["xn"], nth("xn", l, (wait if wait_low is None else wait_low) + c + 1))
                    ins = mm(out, whi[:, t % 2, c * P:c * P + P], xl[:, c, :], start=False, stop=(c == 7))
                return ins

            def step(l, kind, i):
                if kind == "norm":
                    for c in range(EARLY, KO):
                        square_sum(l, i, c)
                elif kind == "feat":
                    t = tile_of(i)
                    pe.wait_ge(sems["split"], nth("split", l, t + 1))
                    pe.wait_ge(sems["evac"], nth("evac", l, i - 1))
                    feature_major(l, PS[:, i % 2, :], t, 0 if i == 0 else None).then_inc(sems["tile"], 1)
                elif kind in ("hi", "v"):
                    t0, nt, w = (T_HI, 4, 512) if kind == "hi" else (T_V, 2, 256)
                    if kind == "v":
                        pe.wait_ge(sems["at"], nth("at", l, 12))
                    for q in range(nt):
                        pe.wait_ge(sems["split"], nth("split", l, t0 + q + 1))
                        per = 1024 // w
                        for k in range(per):
                            ko = per * q + k
                            for st in range(4):
                                ins = mm3(PS[:, 2 + st, 0:w], [x[:, ko, st * P:st * P + P] for x in (xh, xl)],
                                          weights(t0 + q, slice(k * w, k * w + w)), start=(ko == 0), stop=(ko == 7))
                        ins.then_inc(sems["tile"], 1)
                elif kind == "gram":
                    pe.wait_ge(sems["e"], nth("e", l, i + 1))
                    if i == 0:
                        pe.wait_ge(sems["vh"], nth("vh", l, 4))
                    if i == 3:
                        pe.wait_ge(sems["vn"], nth("vn", l, 4))
                    for c in range(4):
                        n = 4 * i + c
                        if n >= 2:
                            pe.wait_ge(sems["at"], nth("at", l, n - 1))
                        b = 2 + 2 * (n % 2)
                        t = slice(c * P, c * P + P)
                        for j in range(LEVELS):
                            mm(PS[:, b + j // 4, (j % 4) * P:(j % 4) * P + P], E[:, j, t], E[:, j, t],
                               start=True, stop=True)
                        mm(PS[:, b + 1, 3 * P:4 * P], kT[:, i, t], qT[:, i, t], start=True, stop=True
                           ).then_inc(sems["gram"], 1)
                elif kind == "rs":
                    n = T if i < 6 else CMP_N
                    if i < 6:
                        pe.wait_ge(sems["evac"], nth("evac", l, 12 + i + 1))
                    else:
                        pe.wait_ge(sems["kce"], nth("kce", l, 1))
                    pe.wait_ge(sems["rrstd"], nth("rrstd", l, i))
                    mm(PS[:, 6, 0:n], ones_64, sq2[:, i % 2, 0:n], start=True, stop=True).then_inc(sems["stat"], 1)
                elif kind == "rr":
                    n = T if i < 6 else CMP_N
                    pe.wait_ge(sems["qn"], nth("qn", l, i + 1))
                    pe.wait_ge(sems["rope"], nth("rope", l, i))
                    mm(PS[:, 7, 0:n], rotm, qnb[:, i % 2, 0:n], start=True, stop=True).then_inc(sems["rot"], 1)
                elif kind == "gatem":
                    pe.wait_ge(sems["at"], nth("at", l, 16))
                    for c in range(KO):
                        ins = mm3(PS[:, 2, :], [wsm[:, j, 24 * c:24 * c + P] for j in range(2)],
                                  (xh[:, c, :], xl[:, c, :]), start=(c == 0), stop=(c == 7))
                    ins.then_inc(sems["gatem"], 1)
                elif kind == "gatet":
                    pe.wait_ge(sems["hid"], nth("hid", l, 4))
                    for qt in range(QT):
                        ins = nc.tensor.transpose(PS[:, 5, qt * P:qt * P + P], ftmp[:, 0, qt * P:qt * P + P], ident)
                    ins.then_inc(sems["gatet"], 1)
                elif kind == "cmph":
                    pe.wait_ge(sems["gate"], nth("gate", l, 1))
                    for kv in range(2):
                        pe.wait_ge(sems["dbuild"], nth("dbuild", l, kv + 1))
                        for pr in range(16):
                            t = T_CMP + 4 * kv + pr // 4
                            if pr % 4 == 0:
                                pe.wait_ge(sems["split"], nth("split", l, t + 1))
                            part, j = pr // 8, pr % 8
                            rhs = DB[:, kv, part, :, :].rearrange("p g (s j) -> p g s j", j=8)[
                                :, :, part:part + CMP_N, j]
                            for hc in range(2):
                                ins = mm(PS[:, 2 + 2 * kv + hc, 0:62],
                                         ring[:, t % RING, (pr % 4) * 256 + hc * P:(pr % 4) * 256 + hc * P + P],
                                         rhs, start=(pr == 0), stop=(pr == 15))
                            if pr % 4 == 3:
                                ins.then_inc(sems["tile"], 1)
                elif kind == "cmpo":
                    pe.wait_ge(sems["hid"], nth("hid", l, 4))
                    w2k, w2v = misc[:, 192:320], misc[:, 320:448]
                    for g in range(2):
                        for hc in range(2):
                            ins = mm(PS[64 * g:64 * g + 64, 2, 0:CMP_N], w2k[:, 64 * hc:64 * hc + 64],
                                     hid[:, 0, hc, CMP_N * g:CMP_N * g + CMP_N], start=(hc == 0), stop=(hc == 1))
                    ins.then_inc(sems["kc"], 1)
                    for j in range(4):
                        for g in range(2):
                            for hc in range(2):
                                ins = mm(PS[32 * j:32 * j + CMP_N, 3, 64 * g:64 * g + 64],
                                         hid[:, 1, hc, CMP_N * g:CMP_N * g + CMP_N], w2v[:, 64 * hc:64 * hc + 64],
                                         start=(hc == 0), stop=(hc == 1))
                    ins.then_inc(sems["vc"], 1)
                elif kind == "ket":
                    if i == 0:
                        pe.wait_ge(sems["qk"], nth("qk", l, 4))
                        pe.wait_ge(sems["kce"], nth("kce", l, 1))
                    if i == 1:
                        pe.wait_ge(sems["vcc"], nth("vcc", l, 1))
                    for h in range(4):
                        ins = nc.tensor.transpose(PS[:, 2 + i, h * P:h * P + P], kT[:, h, i * P:i * P + P], ident)
                    ins.then_inc(sems["ket"], 1)
                elif kind == "state":
                    if i == 0:
                        pe.wait_ge(sems["gates"], nth("gates", l, 1))
                        pe.wait_ge(sems["rope"], nth("rope", l, 7))
                        pe.wait_ge(sems["rrstd"], nth("rrstd", l, 7))
                    if i >= 1:
                        pe.wait_ge(sems["s"], nth("s", l, i))
                    if i >= 2:
                        pe.wait_ge(sems["oc"], nth("oc", l, i - 1))
                    if i < 3:
                        pe.wait_ge(sems["kec"], nth("kec", l, i + 1))
                        for h in range(4):
                            ins = mm(PS[:, 5, h * P:h * P + P], keT[:, i, h, :], Vh[:, i, h * P:h * P + P],
                                     start=True, stop=True)
                        ins.then_inc(sems["ds"], 1)
                    for h in range(4):
                        o = PS[:, 6 + i % 2, h * P:h * P + P]
                        ins = mm(o, Vh[:, i, h * P:h * P + P], AT[:, 4 * h + i, :], start=True, stop=(i == 0))
                        if i:
                            ins = mm(o, Sst[:, h, :], qT[:, h, i * P:i * P + P], start=False, stop=True)
                    ins.then_inc(sems["osum"], 1)
                elif kind == "hn":
                    pe.wait_ge(sems["hsq"], nth("hsq", l, i + 1))
                    if i == 0:
                        pe.wait_ge(sems["evac"], nth("evac", l, 20))
                    if i >= 2:
                        pe.wait_ge(sems["hrs"], nth("hrs", l, i - 1))
                    mm(PS[:, i % 2, :], ones_h, sq2[:, i % 2, :], start=True, stop=True).then_inc(sems["hst"], 1)
                elif kind == "attention":
                    pe.wait_ge(s_tab, 32)
                    pe.wait_ge(sems["hrs"], nth("hrs", l, 4))
                    pe.wait_ge(sems["s"], nth("s", l, 3))
                    pe.wait_ge(sems["oc"], nth("oc", l, 4))
                    attend(l, NSA)
                elif kind == "wout":
                    pe.wait_ge(sems["hn"], nth("hn", l, 4))
                    pe.wait_ge(sems["p"], nth("p", l, EV["p"]))
                    pe.wait_ge(sems["pt"], nth("pt", l, EV["pt"]))
                    pe.wait_ge(sems["ofree"], nth("ofree", l, 4))
                    for k in range(8):
                        kouter(l, T_WO + k, T_WO + k, k, k == 0, k == 7 and (l, 1))
                elif kind == "ffn":
                    with pe.Fori(0, FFC // 2) as j:
                        for u in range(4):
                            t = T_FFI + u
                            pe.wait_ge(sems["split"], l * T_LAYER + j * 4 + (t + 1))
                            if u % 2 == 0:
                                pe.wait_ge(sems["act"], l * FFC + j * 2 + (u // 2 + 1))
                            feature_major(l, PS[:, u, :], t, 8 if u == 0 else None).then_inc(sems["tile"], 1)
                    pe.wait_ge(sems["act"], nth("act", l, FFC))
                    kouter(l, T_FFO, T_FFO, 8, True, False)
                    with pe.Fori(0, 5) as j:
                        for u in range(4):
                            t = T_FFO + 1 + u
                            pe.wait_ge(sems["split"], l * T_LAYER + j * 4 + (t + 1))
                            pe.wait_ge(sems["xs"], l * EV["xs"] + j * 4 + (8 + 2 + u))
                            kouter(l, None, t, 9 + u, False, False)
                    kouter(l, T_FFO + FFC - 1, T_FFO + FFC - 1, 8 + FFC - 1, False, (l + 1, 0))

            def step2(kind, i):
                l = DEPTH
                if kind == "norm":
                    n, w = NORMS2[i][0], MEM if i == 1 else T
                    if i == 1:
                        pe.wait_ge(sems["fls"], nth("fls", 0, 1))
                    for c in range(0 if i == 1 else EARLY, KO):
                        square_sum(l, n, c, 6 if i == 1 else 0, w)
                elif kind == "feat":
                    t = tile2_of(i)
                    pe.wait_ge(sems["split"], nth("split", l, t + 1))
                    pe.wait_ge(sems["evac"], nth("evac", l, i - 1))
                    if i in (16, 17):
                        for c in range(KO):
                            pe.wait_ge(sems["xn"], nth("xn", l, 8 + c + 1))
                            ins = mm(PS[:, i % 2, 0:MEM], ring[:, t % RING, c * P:c * P + P], memn[:, c, :],
                                     start=(c == 0), stop=(c == 7))
                    else:
                        ins = feature_major(l, PS[:, i % 2, :], t, {0: 0, 34: 8}.get(i), {0: 0, 34: 16}.get(i))
                    ins.then_inc(sems["tile"], 1)
                elif kind == "flog":
                    for c in range(KO):
                        ins = mm3(PS[:, 6, :], [wsm[:, j, 8 * c:8 * c + P] for j in range(2)],
                                  (xh[:, c, :], xl[:, c, :]), start=(c == 0), stop=(c == 7))
                    ins.then_inc(sems["fl"], 1)
                elif kind == "tok":
                    t0, nt, _, sem = TOK2[i]
                    if i == 1:
                        pe.wait_ge(sems["fv"], nth("fv", 0, 4))
                    if i == 2:
                        pe.wait_ge(sems["dv"], nth("dv", 0, 4))
                        pe.wait_ge(sems["xn"], nth("xn", l, 16))
                    n, w = (4, T) if sem != "cv" else (2, MEM)
                    per = 1024 // w
                    for q in range(nt):
                        pe.wait_ge(sems["split"], nth("split", l, t0 + q + 1))
                        for k in range(per):
                            ko = per * q + k
                            for st in range(n):
                                o, toks, of = PS[:, 2 + st, 0:w], slice(st * P, st * P + P), slice(k * w, k * w + w)
                                if sem == "cv":
                                    ins = mm(o, memn[:, ko, toks], ring[:, (t0 + q) % RING, of],
                                             start=(ko == 0), stop=(ko == 7))
                                else:
                                    ins = mm3(o, (xh[:, ko, toks], xl[:, ko, toks]), weights(t0 + q, of),
                                              start=(ko == 0), stop=(ko == 7))
                        ins.then_inc(sems["tile"], 1)
                elif kind == "rr":
                    pe.wait_ge(sems["evac"], nth("evac", l, 8 + i + 1))
                    pe.wait_ge(sems["rope"], nth("rope", l, i))
                    mm(PS[:, 7, :], rotm, qnb[:, i % 2, :], start=True, stop=True).then_inc(sems["rot"], 1)
                elif kind == "attention":
                    pe.wait_ge(sems["evac"], nth("evac", l, 34))
                    pe.wait_ge(sems["cv"], nth("cv", 0, 2))
                    pe.wait_ge(sems["nck"], nth("nck", 0, 1))
                    pe.wait_ge(sems["sel"], 16)
                    pe.wait_ge(sems["fls"], nth("fls", 0, 1))
                    pe.wait_ge(sems["rope"], nth("rope", l, 8))
                    attend(l, BL2)
                elif kind == "cross":
                    pe.wait_ge(sems["evac"], nth("evac", l, 36))
                    attend(l, CROSS)
                elif kind == "merge":
                    pe.wait_ge(sems["pt"], nth("pt", l, 72))
                    pe.wait_ge(sems["p"], nth("p", l, 64))
                    for c in range(8):
                        pe.wait_ge(sems["split"], nth("split", l, B_AB + c + 1))
                        if c >= 2:
                            pe.wait_ge(sems["mrg"], nth("mrg", 0, c - 1))
                        b = 2 * (c % 2)
                        for k in range(8):
                            ins = mm3(PS[:, b + k // 4, :], weights(B_AB + c, slice(k * P, k * P + P)),
                                      (xh[:, k, :], xl[:, k, :]), start=(k % 4 == 0), stop=(k % 4 == 3))
                        ins.then_inc(sems["tile"], 1)
                elif kind == "kouter":
                    if i == 0:
                        pe.wait_ge(sems["ofree"], nth("ofree", l, 4))
                        for k in range(8):
                            kouter(l, B_WO + k, B_WO + k, k, k == 0, k == 7 and (l, 2))
                    else:
                        pe.wait_ge(sems["p"], nth("p", l, 80))
                        pe.wait_ge(sems["pt"], nth("pt", l, 72 + 20))
                        pe.wait_ge(sems["ofree"], nth("ofree", l, 8))
                        for k in range(2):
                            kouter(l, B_CO + k, B_CO + k, 8 + k, k == 0, k == 1 and (l, 3))

            def square_sum(l, n, c, bank=0, w=T):
                pe.wait_ge(sems["sq"], nth("sq", l, 8 * n + c + 1))
                mm(PS[:, bank, 0:w], ones_d, sq2[:, c % 2, 0:w], start=(c == 0), stop=(c == 7)
                   ).then_inc(sems["sqsum"], 1)

            def kouter(l, wait_t, t, k, first, last):
                if wait_t is not None:
                    pe.wait_ge(sems["split"], nth("split", l, wait_t + 1))
                    pe.wait_ge(sems["xs"], nth("xs", l, k + 1))
                for c in range(8):
                    ins = mm3(PS[:, c, :], weights(t, slice(c * P, c * P + P)),
                              (xs[:, k % 2, 0, :], xs[:, k % 2, 1, :]),
                              start=first, stop=bool(last))
                    if c == 7:
                        ins.then_inc(sems["tile"], 1)
                    elif last:
                        ins.then_inc(sems["res"], 1)
                    if last and c >= KO - EARLY:
                        square_sum(*last, c - (KO - EARLY))

            def attend(l, items):
                for s in range(len(items) + LAG_V):
                    it = items[s] if s < len(items) else None
                    if it and it["kind"] != "mix":
                        k = it["k"]
                        if k >= 3:
                            pe.wait_ge(sems["p"], nth("p", l, k - 2))
                        if items is CROSS and k == 64:
                            pe.wait_ge(sems["pt"], nth("pt", l, 72))
                        for j, (lo, hi, lhsT, rhs) in enumerate(it["sc"]):
                            ins = mm(PS[:, k % 3, lo:hi], lhsT, rhs, start=(j == 0), stop=(j == len(it["sc"]) - 1),
                                     skip_group_check=True)
                        ins.then_inc(sems["sc"], 1)
                    it = items[s - LAG_T] if 0 <= s - LAG_T < len(items) else None
                    if it:
                        t = it["t"]
                        if t >= 2:
                            pe.wait_ge(sems["pt"], nth("pt", l, t - 1))
                        if it["kind"] == "mix":
                            pe.wait_ge(sems["mixtok"], nth("mixtok", l, it["mixn"]))
                            for b in range(it["nb"]):
                                ins = nc.tensor.transpose(PS[:, 3 + t % 2, b * P:b * P + P],
                                                          it["src"][:, b * P:b * P + P], ident)
                        else:
                            pe.wait_ge(sems["p"], nth("p", l, it["k"] + 1))
                            for b in range(it["nb"]):
                                ins = nc.tensor.transpose(PS[:, 3 + t % 2, b * P:b * P + P],
                                                          Pr[it["k"] % 3][:, b * P:b * P + P], ident)
                        ins.then_inc(sems["tr"], 1)
                    it = items[s - LAG_V] if 0 <= s - LAG_V < len(items) else None
                    if it and it["kind"] != "mix":
                        pe.wait_ge(sems["pt"], nth("pt", l, it["t"] + 1))
                        if it.get("first", 0):
                            pe.wait_ge(sems["ofree"], nth("ofree", l, it["first"]))
                        for o, b, rhs, start, stop in it["pv"]:
                            ins = mm(o, PTs[it["t"] % 2][:, b * P:b * P + P], rhs, start=start, stop=stop)
                        ins.then_inc(sems["pv"], 1)

            pe.wait_ge(s_in, 16 * NIN)
            for c in range(EARLY):
                square_sum(0, 0, c)
            with pe.Fori(0, DEPTH) as l:
                pe.wait_ge(sems["params"], nth("params", l, 2))
                for kind, i in STEPS:
                    step(l, kind, i)
            pe.wait_ge(sems["b_in"], 48)
            for kind, i in STEPS2:
                step2(kind, i)

            ones_b, before_b = maskb[:, K_ONES:K_ONES + P], maskb[:, K_BEFORE:K_BEFORE + P]
            for c in range(KO):
                pe.wait_ge(sems["xn"], nth("xn", DEPTH, 24 + c + 1))
                ins = mm(PS[0:36, 0, :], par[:, M_WGE + 36 * c:M_WGE + 36 * c + 36], xn[:, c, :],
                         start=(c == 0), stop=(c == 7))
            ins.then_inc(MS["lgT"], 1)
            pe.wait_ge(MS["lgs"], 1)
            for qt in range(QT):
                ins = nc.tensor.transpose(PS[:, 1, 36 * qt:36 * qt + 36], lnb[0:36, qt * P:qt * P + P],
                                          ident[0:36, 0:36])
            ins.then_inc(MS["lg"], 1)
            for g in range(16):
                qt, half = g % 8 // 2, g % 2
                if g >= 4:
                    pe.wait_ge(MS["te"], g - 3)
                src = xn if g < 8 else xT
                for c in range(4):
                    ins = nc.tensor.transpose(PS[:, 4 + g % 4, c * P:c * P + P],
                                              src[:, 4 * half + c, qt * P:qt * P + P], ident)
                ins.then_inc(MS["tr"], 1)
            pe.wait_ge(MS["A"], 1)
            for qt in range(QT):
                for q in range(qt):
                    mm(PS[:, 1, 32 * qt:32 * qt + 32], ones_b, Ab[:, q, :], start=(q == 0), stop=False)
                mm(PS[:, 1, 32 * qt:32 * qt + 32], before_b, Ab[:, qt, :], start=(qt == 0), stop=True)
            for q in range(QT):
                ins = mm(PS[:, 1, 128:160], ones_b, Ab[:, q, :], start=(q == 0), stop=(q == 3))
            ins.then_inc(MS["rk"], 1)

            def index(i, u):
                pe.wait_ge(MS["od"], lin(i, u, 1, 1))
                pe.wait_ge(MS["ii"], lin(i, u, 1, 0))
                for qt in range(QT):
                    mm(PS[:, 7, 0:1], Ob[u % 2][:, qt, :], maskb[:, K_TID:K_TID + 1], start=(qt == 0), stop=False)
                    ins = mm(PS[:, 7, 0:1], Ob[u % 2][:, qt, :], maskb[:, K_TID + 1 + qt:K_TID + 2 + qt],
                             start=False, stop=(qt == 3))
                ins.then_inc(MS["ix"], 1)

            def turn_x(i, u):
                pe.wait_ge(MS["xg"][u % 2], dma_of(i, u))
                pe.wait_ge(MS["xev"], lin(i, u, 1, 0))
                for c in range(KO):
                    ins = nc.tensor.transpose(PS[:, c // 4, (c % 4) * P:(c % 4) * P + P],
                                              xg[u % 2][:, c * P:c * P + P], ident)
                ins.then_inc(MS["xt"], 1)

            def gate_up(w, bank, free, i, u):
                pe.wait_ge(MS["xev"], lin(i, u, 1, 1))
                pe.wait_ge(MS[free], lin(i, u, 1, 0))
                for k in range(4):
                    pe.wait_ge(MS[("glow" if k % 2 else "vlow") + w], lin(i, u, 2, k // 2 + 1))
                    for c in (2 * k, 2 * k + 1):
                        of = slice(T * (c % 2), T * (c % 2) + T)
                        ins = mm3(PS[:, bank, :], [x[:, c, :] for x in xgT[u % 2]],
                                  (high(w, k)[:, of], low(w, k)[:, of]),
                                  start=(c == 0), stop=(c == 7))
                    if k % 2:
                        ins.then_inc(MS["use" + w], 1)

            def turn_h(i, u):
                pe.wait_ge(MS["hm"], lin(i, u, 1, 1))
                pe.wait_ge(MS["hl"], lin(i, u, 1, 0))
                for c in range(4):
                    ins = nc.tensor.transpose(PS[:, 4, c * P:c * P + P], hsb[u % 2][:, c * P:c * P + P], ident)
                ins.then_inc(MS["ht"], 1)

            def down(i, u):
                pe.wait_ge(MS["hl"], lin(i, u, 1, 1))
                pe.wait_ge(MS["yea"], lin(i, u, 1, 0))
                pe.wait_ge(MS["yev"], lin(i, u, 1, 0))
                for k in range(4):
                    pe.wait_ge(MS["glowD" if k % 2 else "vlowD"], lin(i, u, 2, k // 2 + 1))
                    for j in range(2):
                        of = slice(T * j, T * j + T)
                        ins = mm3(PS[:, 5 + j, :], [x[:, k, :] for x in hT[u % 2]],
                                  (high("D", k)[:, of], low("D", k)[:, of]),
                                  start=(k == 0), stop=(k == 3))
                    if k % 2:
                        ins.then_inc(MS["useD"], 1)

            def moe_p(i, u, prev, next_):
                index(i, u + 2)
                turn_x(i, u + 1)
                if prev:
                    turn_h(i, u - 1)
                gate_up("G", 2, "sl", i, u)
                gate_up("U", 3, "hm", i, u)
                if prev:
                    down(i, u - 1)

            pe.wait_ge(MS["te"], 16)
            index(0, 0)
            index(0, 1)
            turn_x(0, 0)
            blocks(pe, moe_p, 0, NEXP)
            turn_h(NEXP // 2 - 1, 1)
            down(NEXP // 2 - 1, 1)
            with overflow(pe):
                blocks(pe, moe_p, NEXP, NEXP + OVB)
                turn_h((NEXP + OVB) // 2 - 1, 1)
                down((NEXP + OVB) // 2 - 1, 1)


def tile_of(t):
    return t if t < 12 else t + 4 if t < 18 else T_C + t - 18


STEPS = (
    [("norm", 0)]
    + [("feat", 0), ("feat", 1), ("gate_h", 0), ("feat", 2), ("gate_h", 1), ("scan", 0), ("feat", 3), ("scan", 1),
       ("gate_h", 2), ("feat", 4), ("gate_h", 3), ("decay", 0), ("feat", 5), ("feat", 6), ("feat", 7)]
    + [("feat", 8), ("feat", 9), ("feat", 10), ("feat", 11), ("vczero", 0), ("hi", 0), ("gram", 0), ("decay", 1),
       ("qk", 0), ("scan", 2)]
    + [("feat", 12), ("feat", 13), ("rs", 0), ("feat", 14), ("rs", 1), ("rr", 0), ("gram", 1), ("decay", 2), ("qk", 1),
       ("scan", 3), ("feat", 15), ("rs", 2), ("rr", 1), ("feat", 16), ("rs", 3), ("rr", 2), ("feat", 17), ("rs", 4),
       ("rr", 3), ("gram", 2), ("decay", 3), ("qk", 2), ("v", 0), ("rs", 5), ("rr", 4), ("gram", 3), ("qk", 3),
       ("feat", 18), ("rr", 5), ("dbuild", 0), ("feat", 19), ("dbuild", 1), ("gatem", 0), ("cmph", 0), ("cmpo", 0), ("gatet", 0),
       ("rs", 6), ("ket", 0), ("ket", 1), ("ket", 2), ("rr", 6)]
    + [("state", c) for c in range(4)] + [("hn", h) for h in range(4)]
    + [("attention", 0), ("wout", 0), ("norm", 1), ("ffn", 0)])


def tile2_of(f):
    return f if f < 8 else f + 4 if f < 16 else f + 8 if f < 18 else f + 10 if f < 34 else B_CQ + f - 34


NORMS2 = [(0, 0, 0), (1, None, None), (2, 1, 1), (3, 2, None)]
TOK2 = [(B_FV, 4, "fv", "fv"), (B_DV, 4, "dv", "dv"), (B_CV, 2, "cv", "cv")]
STEPS2 = (
    [("norm", 0), ("feat", 0), ("feat", 1), ("lam", 0), ("angles", 0)] + [("feat", i) for i in range(2, 7)]
    + [("trig", 0), ("feat", 7), ("flog", 0), ("tok", 0)]
    + [("feat", 8), ("feat", 9), ("rr", 0)]
    + [x for i in range(10, 16) for x in (("feat", i), ("rr", i - 9))] + [("tok", 1), ("rr", 7)]
    + [("norm", 1), ("feat", 16), ("feat", 17), ("tok", 2), ("feat", 18), ("sel", 0)]
    + [("feat", i) for i in range(19, 34)]
    + [("attention", 0), ("merge", 0), ("kouter", 0), ("norm", 2), ("feat", 34), ("feat", 35), ("cross", 0),
       ("kouter", 1), ("norm", 3)])
EARLY = 5
PARAMS2_AT = 204
DECAYED_AT = [8, 19, 22, 24]
A_CH = 2 + ROPES + 4
V_CH = 61 + 2 + 8


def lhs_tile(w):
    return w.reshape(KO, P, -1).transpose(1, 0, 2)


def ring_tiles(a):
    out = np.zeros((NTILES, P, 1024), np.float32)
    for l in range(DEPTH):
        w, base = a["w_in"][l], l * T_LAYER
        hq, hf, hi, hg, nq, kc, vc, ks, vs, kw, vw = (w[:, o:o + n] for o, n in (
            (0, 512), (512, 512), (1024, 512), (1536, 512), (2048, 512), (2560, 128), (2688, 128), (2816, 128),
            (2944, 128), (3072, 128), (3200, 128)))
        for i in range(4):
            for t, x in ((T_HF, hf), (T_HQ, hq), (T_HG, hg)):
                out[base + t + i] = lhs_tile(x[:, i * P:i * P + P]).reshape(P, -1)
            out[base + T_HI + i] = hi.reshape(4, 2, P, 512)[i].transpose(1, 0, 2).reshape(P, -1)
            pair = np.concatenate([nq[:, 64 * i:64 * i + 64], nq[:, 64 * (i + 4):64 * (i + 4) + 64]], 1)
            out[base + T_NQ + i] = lhs_tile(pair).reshape(P, -1)
        for t, x in ((T_NQ + 4, ks), (T_NQ + 5, kw), (T_C, kc), (T_C + 1, vc)):
            out[base + t] = lhs_tile(x).reshape(P, -1)
        vv = np.concatenate([vs, vw], 1).reshape(2, 4, P, 256)
        for i in range(2):
            out[base + T_V + i] = vv[i].transpose(1, 0, 2).reshape(P, -1)
        for j, x in enumerate((a["cmp_w1_k"][l], a["cmp_w1_v"][l])):
            x = x.reshape(4, 4, P, 256)
            for i in range(4):
                out[base + T_CMP + 4 * j + i] = x[i].transpose(1, 0, 2).reshape(P, -1)
        out[base + T_WO:base + T_WO + 8] = a["w_out"][l].reshape(8, P, 1024)
        g = a["w_ffn_in"][l].reshape(KO, P, 2, FFC, P).transpose(3, 2, 1, 0, 4)
        out[base + T_FFI:base + T_FFI + 2 * FFC] = g.reshape(2 * FFC, P, 1024)
        out[base + T_FFO:base + T_LAYER] = a["w_ffn_out"][l].reshape(FFC, P, 1024)
    block2_tiles(a, out)
    return out


def block2_tiles(a, out):
    w = a["w_in_2"][0]
    base = DEPTH * T_LAYER
    fq, fk, fv, _, dq, dk, dv, ga, gb = (w[:, o:o + n] for o, n in (
        (0, 512), (512, 512), (1024, 512), (1536, 8), (1544, 512), (2056, 512), (2568, 512), (3080, 1024),
        (4104, 1024)))
    for t, x in ((B_FQ, fq), (B_FK, fk), (B_DQ, dq), (B_DK, dk), (B_GA, ga), (B_GA + 8, gb),
                 (B_CK, a["w_ckv_2"][0][:, 0:256]), (B_CQ, a["w_cq_2"][0])):
        for i in range(x.shape[1] // P):
            out[base + t + i] = lhs_tile(x[:, i * P:i * P + P]).reshape(P, -1)
    for t, x in ((B_FV, fv), (B_DV, dv)):
        for i in range(4):
            out[base + t + i] = x.reshape(4, 2, P, 512)[i].transpose(1, 0, 2).reshape(P, -1)
    x = a["w_ckv_2"][0][:, 256:512].reshape(2, 4, P, 256)
    for i in range(2):
        out[base + B_CV + i] = x[i].transpose(1, 0, 2).reshape(P, -1)
    ab = np.stack([a["w_branch_a_2"][0], a["w_branch_b_2"][0]]).reshape(2, 4, P, 8, P)
    out[base + B_AB:base + B_AB + 8] = ab.transpose(3, 2, 0, 1, 4).reshape(8, P, 1024)
    out[base + B_WO:base + B_WO + 8] = a["w_out_2"][0].reshape(8, P, 1024)
    out[base + B_CO:base + B_CO + 2] = a["w_co_2"][0].reshape(2, P, 1024)


def block2_params(a):
    out = np.zeros((P, M_END), np.float32)
    for c, name in ((M_MIX, "g_mix_2"), (M_MEM, "g_mem_2"), (M_CROSS, "g_cross_2"), (M_FFN, "g_ffn_2")):
        out[:, c:c + 8] = a[name][0].reshape(8, P).T
    out[:, M_SUB] = a["g_diff_sub_2"][0]
    freq = np.float32(10000.0) ** (-np.arange(32, dtype=np.float32) * np.float32(2.0) / np.float32(64))
    out[:, M_FREQ] = freq[np.arange(P) % 32]
    out[0:8, M_BF] = a["b_fgate_2"][0]
    out[:, M_WF:M_WF + 64] = lhs_tile(a["w_in_2"][0][:, 1536:1544]).reshape(P, 64)
    for j, name in enumerate(("lambda_q1_2", "lambda_k1_2", "lambda_q2_2", "lambda_k2_2")):
        out[:, M_LAM + 64 * j:M_LAM + 64 * j + 64] = a[name][0]
    wge = np.concatenate([a["w_group_2"][0], a["w_expert_2"][0]], 1)
    out[:, M_WGE:M_WGE + 288] = lhs_tile(wge).reshape(P, 288)
    out[:, M_BGE:M_BGE + 36] = np.concatenate([a["b_group_2"][0], a["b_expert_2"][0]])
    out[:, M_IOTA:M_IOTA + P] = np.arange(P)
    out[:, M_E:M_E + NEXP] = np.arange(NEXP)
    return out


def layer_columns(a):
    out = np.zeros((P, DEPTH, NCOL), np.float32)
    for l in range(DEPTH):
        out[:, l, C_MIX:C_MIX + 8] = a["norm_mix"][l].reshape(8, P).T
        out[:, l, C_FFN:C_FFN + 8] = a["norm_ffn"][l].reshape(8, P).T
        out[:, l, C_GN] = a["hg_gnorm"][l]
        out[:, l, C_QG] = np.tile(a["q_gain"][l], 2)
        for j, br in enumerate((1, 2, 0)):
            out[:, l, C_KG + (j + 1) % 3] = np.tile(a["k_gain"][l][br], 2)
        for j, pe in enumerate((a["cmp_pe_k"][l], a["cmp_pe_v"][l])):
            x = pe.reshape(16, 2, 64).transpose(2, 1, 0).reshape(64, 32)
            out[:, l, C_PE + 32 * j:C_PE + 32 * j + 32] = np.concatenate([x, x], 0)
        out[:, l, C_LB:C_LB + 4] = a["hg_lb_logits"][l].reshape(4, P).T
    return out


def misc_weights(a):
    out = np.zeros((P, DEPTH, MISC), np.float32)
    for l in range(DEPTH):
        out[:, l, 0:192] = lhs_tile(a["w_in"][l][:, 3328:3352]).reshape(P, 192)
        out[:, l, 192:320] = a["cmp_w2_k"][l].reshape(2, P, 64).transpose(1, 0, 2).reshape(P, P)
        out[:, l, 320:448] = a["cmp_w2_v"][l].reshape(2, P, 64).transpose(1, 0, 2).reshape(P, P)
    return out


def constants():
    half = 32
    freqs = (np.float32(10000.0) ** (-np.arange(half, dtype=np.float32) / np.float32(half))).astype(np.float32)
    ang = np.arange(T, dtype=np.float32)[None, :] * freqs[np.arange(P) % half][:, None]
    p = np.arange(P)
    ones_64 = ((p[:, None] // 64) == (p[None, :] // 64)) / 64.0
    rot = np.zeros((P, P))
    for m in range(P):
        if m % 64 < 32:
            rot[m + 32, m] = -1.0
        else:
            rot[m - 32, m] = 1.0
    valid = np.zeros((P, P))
    valid[31:, 0] = 1.0
    mats = [np.full((P, P), 1.0 / D), np.full((P, P), 1.0 / P), ones_64, rot, np.eye(P), valid]
    s, t = p[:, None], p[None, :]
    gm = []
    for j in range(LEVELS):
        w = 64 >> j
        gm.append((s // (2 * w) == t // (2 * w)) & (s // w % 2 == 0) & (t // w % 2 == 1))
    gm.append(s == t)
    tabs = np.concatenate([np.cos(ang), np.sin(ang)] + mats, 1).astype(np.float32)
    tok = np.arange(T).reshape(QT, P)
    masks = [np.eye(P), np.where(t > s, NEG, 0.0)]
    for qt in range(QT):
        n = np.arange(P) % 32
        ok = (n[None, :] < CMP_N) & (n[None, :] * 16 + 31 <= tok[qt][:, None])
        masks.append(np.where(ok, 0.0, NEG))
    masks += [np.ones((P, P)), s < t]
    tid = np.zeros((P, 8))
    tid[:, 0] = p
    tid[:, 1:1 + QT] = np.arange(QT) * P
    masks += [tid] + gm
    masks = np.ascontiguousarray(np.concatenate(masks, 1).astype(np.float32))
    return tabs, (masks.view(np.uint32) >> 16).astype(np.uint16)


def kernel(**inputs):
    import concourse.bacc as _bacc
    from concourse.bass_utils import run_bass_kernel_spmd as _run

    a = {k: np.asarray(x) for k, x in inputs.items()}
    nc = _bacc.Bacc("TRN2", target_bir_lowering=False, num_devices=1)
    tabs, masks = constants()
    arrays = {
        "ring_w": ring_tiles(a),
        "xT_in": np.ascontiguousarray(a["x"][0].T).reshape(KO, P, T),
        "cols_in": layer_columns(a),
        "misc_in": misc_weights(a),
        "tabs_in": tabs,
        "masks_in": masks,
        "par_in": block2_params(a),
        "sel_in": np.ascontiguousarray(np.broadcast_to((np.arange(P)[:, None, None] == np.arange(8)[None, :, None]),
                                                       (P, 8, P))).astype(np.float32),
        "pos_in": np.ascontiguousarray(np.broadcast_to(a["positions_2"], (P, T))).astype(np.int32),
        "gfin_in": np.ascontiguousarray(np.broadcast_to(a["g_final_2"], (P, D))),
        "w_gate": a["w_exp_gate_2"][0], "w_up": a["w_exp_up_2"][0], "w_down": a["w_exp_down_2"][0],
        "memT_in": np.ascontiguousarray(a["mem_2"][0].T.reshape(KO, P, MEM).transpose(1, 0, 2)),
    }
    aps = {k: nc.dram_tensor(k, x.shape, mybir.dt.from_np(x.dtype), kind="ExternalInput").ap()
           for k, x in arrays.items()}
    hm_dram = nc.dram_tensor("hm_dram", (T, D), F32, kind="Internal").ap()
    y_dram = nc.dram_tensor("y_dram", (YROWS // P // 2, 2, P, D), F32, kind="Internal").ap()
    out = nc.dram_tensor("out", (QT, P, D), F32, kind="ExternalOutput").ap()
    build(nc, **aps, hm_dram=hm_dram, y_dram=y_dram, out=out)
    r = _run(nc, [arrays], core_ids=[0])
    return r.results[0]["out"].reshape(1, T, D)
```
